# Optimizing a Trainium2 kernel written in Bass

```python
import math
import jax, jax.numpy as jnp
from jax import lax
import numpy as np

D_MODEL = 1024
BATCH = 1
SEQ = 512
DEPTH = 2

HEAD_DIM = 64
Q_BLOCK = 128
ROPE_THETA = 10000.0
NORM_EPS = 1e-6
A_HEADS = 4
A_V_DIM = 2 * HEAD_DIM
B_HEADS = 8
B_PATTERNS = ((128, 1), (512, 4), (2048, 16))
C_HEADS = 4
C_NOPE_DIM = 64
C_ROPE_DIM = 32
C_V_DIM = 128
C_Q_RANK = 384
C_KV_RANK = 256
D_HEADS = 4
D_HEAD_DIM = 128
MIX_WIDTH = A_HEADS * A_V_DIM + B_HEADS * HEAD_DIM
EVEN_WIDTHS = (A_HEADS * 2 * HEAD_DIM, A_HEADS * 2 * HEAD_DIM, A_HEADS * A_V_DIM,
               B_HEADS * HEAD_DIM, B_HEADS * HEAD_DIM, B_HEADS * HEAD_DIM)
ODD_WIDTHS = (C_Q_RANK, C_KV_RANK, C_ROPE_DIM,
              D_HEADS * D_HEAD_DIM, D_HEADS * D_HEAD_DIM, D_HEADS * D_HEAD_DIM)
EVEN_IN = 3072
ODD_IN = 2208
D_FF = 2816
CONV_WIDTH = 3
N_EVEN = (DEPTH + 1) // 2
N_ODD = DEPTH // 2

kernel_name = "hybrid_diff_dilated_mla_stickbreak_trunk"

def rms_norm(x, g):
    xf = x.astype(jnp.float32)
    y = xf * lax.rsqrt(jnp.mean(xf * xf, axis=-1, keepdims=True) + NORM_EPS)
    return (y * g.astype(jnp.float32)).astype(x.dtype)

def rope_tables(seq, dim):
    inv_freq = ROPE_THETA ** (-jnp.arange(0, dim, 2, dtype=jnp.float32) / dim)
    ang = jnp.arange(seq, dtype=jnp.float32)[:, None] * inv_freq[None, :]
    return jnp.cos(ang), jnp.sin(ang)

def apply_rope(x, cos, sin):
    half = x.shape[-1] // 2
    shape = (1, x.shape[1]) + (1,) * (x.ndim - 3) + (half,)
    c = cos.reshape(shape).astype(x.dtype)
    s = sin.reshape(shape).astype(x.dtype)
    x1, x2 = x[..., :half], x[..., half:]
    return jnp.concatenate([x1 * c - x2 * s, x2 * c + x1 * s], axis=-1)

def split_cols(p, widths):
    out, start = [], 0
    for w in widths:
        out.append(p[..., start:start + w])
        start += w
    return out

def causal_query_blocks(fn, seq):
    return jnp.concatenate([fn(i * Q_BLOCK, (i + 1) * Q_BLOCK) for i in range(seq // Q_BLOCK)], axis=1)

def causal_mask(q0, kl, strict=False):
    qpos = q0 + jnp.arange(Q_BLOCK)[:, None]
    kpos = jnp.arange(kl)[None, :]
    return kpos < qpos if strict else kpos <= qpos

def masked_exp(s, mask):
    s = jnp.where(mask, s, -jnp.inf)
    e = jnp.exp(s - jnp.max(s, axis=-1, keepdims=True))
    return e, jnp.sum(e, axis=-1)

def reverse_exclusive_cumsum(x):
    lead, n = x.shape[:-1], x.shape[-1]
    nkb = n // Q_BLOCK
    xb = x.reshape(lead + (nkb, Q_BLOCK))
    tri = (jnp.arange(Q_BLOCK)[:, None] > jnp.arange(Q_BLOCK)[None, :]).astype(x.dtype)
    tri_b = (jnp.arange(nkb)[:, None] > jnp.arange(nkb)[None, :]).astype(x.dtype)
    within = jnp.einsum('...cm,mj->...cj', xb, tri)
    later = jnp.einsum('...m,mc->...c', jnp.sum(xb, axis=-1), tri_b)
    return (within + later[..., None]).reshape(x.shape)

def diff_attention(q, k, v, lam):
    scale = HEAD_DIM ** -0.5

    def block(q0, kl):
        s = jnp.einsum('bqhcd,bkhcd->bhcqk', q[:, q0:kl] * scale, k[:, :kl],
                       preferred_element_type=jnp.float32)
        e, den = masked_exp(s, causal_mask(q0, kl))
        o = jnp.einsum('bhcqk,bkhe->bqhce', e.astype(v.dtype), v[:, :kl])
        o = (o / jnp.transpose(den, (0, 3, 1, 2))[..., None]).astype(v.dtype)
        return o[:, :, :, 0] - lam * o[:, :, :, 1]

    return causal_query_blocks(block, q.shape[1])

def dilated_branch(q, k, v, window, dil):
    b, s, h, dh = q.shape
    qb = Q_BLOCK // dil
    nb = s // Q_BLOCK
    n_back = window // dil
    n_prev = -(-n_back // qb)
    band = (n_prev + 1) * qb
    scale = dh ** -0.5

    def to_blocks(t):
        return t.reshape(b, nb, qb, dil, h, dh)

    def to_band(t):
        tp = jnp.pad(to_blocks(t), ((0, 0), (n_prev, 0), (0, 0), (0, 0), (0, 0), (0, 0)))
        return jnp.concatenate([tp[:, c:c + nb] for c in range(n_prev + 1)], axis=2)

    kb, vb = to_band(k), to_band(v)
    qi = jnp.arange(qb)[:, None]
    kj = jnp.arange(band)[None, :]
    dist = qi + n_prev * qb - kj
    kpos = (jnp.arange(nb)[:, None, None] - n_prev) * qb + kj[None]
    valid = (dist >= 0) & (dist <= n_back) & (kpos >= 0)
    sc = jnp.einsum('bnqrhd,bnkrhd->bnrhqk', to_blocks(q) * scale, kb,
                    preferred_element_type=jnp.float32)
    sc = jnp.where(valid[None, :, None, None], sc, -jnp.inf)
    m = jnp.max(sc, axis=-1, keepdims=True)
    e = jnp.exp(sc - m)
    den = jnp.sum(e, axis=-1, keepdims=True)
    o = jnp.einsum('bnrhqk,bnkrhd->bnqrhd', (e / den).astype(v.dtype), vb).reshape(b, s, h, dh)
    lse = jnp.transpose((m + jnp.log(den))[..., 0], (0, 1, 4, 2, 3)).reshape(b, s, h)
    return o, lse

def dilated_attention(q, k, v):
    outs, lses = [], []
    for window, dil in B_PATTERNS:
        o, lse = dilated_branch(q, k, v, window, dil)
        outs.append(o)
        lses.append(lse)
    alpha = jax.nn.softmax(jnp.stack(lses, axis=0), axis=0)
    return jnp.einsum('gbsh,gbshd->bshd', alpha.astype(v.dtype), jnp.stack(outs, axis=0))

def mla_attention(q, k, v):
    scale = (C_NOPE_DIM + C_ROPE_DIM) ** -0.5

    def block(q0, kl):
        s = jnp.einsum('bqhd,bkhd->bhqk', q[:, q0:kl] * scale, k[:, :kl],
                       preferred_element_type=jnp.float32)
        e, den = masked_exp(s, causal_mask(q0, kl))
        o = jnp.einsum('bhqk,bkhd->bqhd', e.astype(v.dtype), v[:, :kl])
        return (o / jnp.transpose(den, (0, 2, 1))[..., None]).astype(v.dtype)

    return causal_query_blocks(block, q.shape[1])

def stick_breaking_attention(q, k, v):
    scale = D_HEAD_DIM ** -0.5

    def block(q0, kl):
        z = jnp.einsum('bqhd,bkhd->bhqk', q[:, q0:kl] * scale, k[:, :kl],
                       preferred_element_type=jnp.float32)
        mask = causal_mask(q0, kl, strict=True)
        log_keep = jnp.where(mask, jax.nn.log_sigmoid(-z), 0.0)
        a = jnp.where(mask, jnp.exp(z + log_keep + reverse_exclusive_cumsum(log_keep)), 0.0)
        return jnp.einsum('bhqk,bkhd->bqhd', a.astype(v.dtype), v[:, :kl])

    return causal_query_blocks(block, q.shape[1])

def even_mixer(h, w_in, lq1, lk1, lq2, lk2, subln_g, w_out, lam_init, cos, sin):
    b, s, _ = h.shape
    a_q, a_k, a_v, b_q, b_k, b_v = split_cols(h @ w_in, EVEN_WIDTHS)
    a_q = apply_rope(a_q.reshape(b, s, A_HEADS, 2, HEAD_DIM), cos, sin)
    a_k = apply_rope(a_k.reshape(b, s, A_HEADS, 2, HEAD_DIM), cos, sin)
    a_v = a_v.reshape(b, s, A_HEADS, A_V_DIM)
    f32 = jnp.float32
    lam = (jnp.exp(jnp.sum(lq1.astype(f32) * lk1.astype(f32)))
           - jnp.exp(jnp.sum(lq2.astype(f32) * lk2.astype(f32))) + lam_init)
    o_a = diff_attention(a_q, a_k, a_v, lam)
    o_a = rms_norm(o_a, subln_g) * (1.0 - lam_init)
    b_q = apply_rope(b_q.reshape(b, s, B_HEADS, HEAD_DIM), cos, sin)
    b_k = apply_rope(b_k.reshape(b, s, B_HEADS, HEAD_DIM), cos, sin)
    o_b = dilated_attention(b_q, b_k, b_v.reshape(b, s, B_HEADS, HEAD_DIM))
    o = jnp.concatenate([o_a.reshape(b, s, -1), o_b.reshape(b, s, -1)], axis=-1)
    return o @ w_out

def odd_mixer(h, w_in, q_norm_g, w_uq, kv_norm_g, w_ukv, w_out, cos_c, sin_c):
    b, s, _ = h.shape
    c_q, c_kv, c_kr, d_q, d_k, d_v = split_cols(h @ w_in, ODD_WIDTHS)
    q = (rms_norm(c_q, q_norm_g) @ w_uq).reshape(b, s, C_HEADS, C_NOPE_DIM + C_ROPE_DIM)
    q = jnp.concatenate([q[..., :C_NOPE_DIM], apply_rope(q[..., C_NOPE_DIM:], cos_c, sin_c)], axis=-1)
    kv = (rms_norm(c_kv, kv_norm_g) @ w_ukv).reshape(b, s, C_HEADS, C_NOPE_DIM + C_V_DIM)
    k_nope, v_c = kv[..., :C_NOPE_DIM], kv[..., C_NOPE_DIM:]
    k_rope = apply_rope(c_kr, cos_c, sin_c)
    k = jnp.concatenate([k_nope, jnp.broadcast_to(k_rope[:, :, None], (b, s, C_HEADS, C_ROPE_DIM))], axis=-1)
    o_c = mla_attention(q, k, v_c)
    o_d = stick_breaking_attention(d_q.reshape(b, s, D_HEADS, D_HEAD_DIM),
                                   d_k.reshape(b, s, D_HEADS, D_HEAD_DIM),
                                   d_v.reshape(b, s, D_HEADS, D_HEAD_DIM))
    o = jnp.concatenate([o_c.reshape(b, s, -1), o_d.reshape(b, s, -1)], axis=-1)
    return o @ w_out

def conv_ffn(h, w_up, conv_w, conv_b, w_down):
    gate, val = jnp.split(h @ w_up, 2, axis=-1)
    gate = lax.conv_general_dilated(
        gate, conv_w[:, None, :], window_strides=(1,), padding=((CONV_WIDTH - 1, 0),),
        dimension_numbers=('NWC', 'WIO', 'NWC'), feature_group_count=D_FF) + conv_b
    return (jax.nn.silu(gate) * val) @ w_down

def setup_inputs(seed: int = 0) -> dict:
    key = jax.random.key(seed)
    ks = iter(jax.random.split(key, 32))

    def dense(shape, fan_in):
        return jax.random.normal(next(ks), shape, jnp.float32) * (fan_in ** -0.5)

    def gain(shape):
        return 1.0 + 0.02 * jax.random.normal(next(ks), shape, jnp.float32)

    def small(shape, std):
        return std * jax.random.normal(next(ks), shape, jnp.float32)

    return {
        "x": jax.random.normal(next(ks), (BATCH, SEQ, D_MODEL), jnp.float32),
        "mix_norm_g": gain((DEPTH, D_MODEL)),
        "ffn_norm_g": gain((DEPTH, D_MODEL)),
        "final_norm_g": gain((D_MODEL,)),
        "ab_w_in": dense((N_EVEN, D_MODEL, EVEN_IN), D_MODEL),
        "a_lambda_q1": small((N_EVEN, HEAD_DIM), 0.1),
        "a_lambda_k1": small((N_EVEN, HEAD_DIM), 0.1),
        "a_lambda_q2": small((N_EVEN, HEAD_DIM), 0.1),
        "a_lambda_k2": small((N_EVEN, HEAD_DIM), 0.1),
        "a_subln_g": gain((N_EVEN, A_V_DIM)),
        "ab_w_out": dense((N_EVEN, MIX_WIDTH, D_MODEL), MIX_WIDTH),
        "cd_w_in": dense((N_ODD, D_MODEL, ODD_IN), D_MODEL),
        "c_q_norm_g": gain((N_ODD, C_Q_RANK)),
        "c_w_uq": dense((N_ODD, C_Q_RANK, C_HEADS * (C_NOPE_DIM + C_ROPE_DIM)), C_Q_RANK),
        "c_kv_norm_g": gain((N_ODD, C_KV_RANK)),
        "c_w_ukv": dense((N_ODD, C_KV_RANK, C_HEADS * (C_NOPE_DIM + C_V_DIM)), C_KV_RANK),
        "cd_w_out": dense((N_ODD, MIX_WIDTH, D_MODEL), MIX_WIDTH),
        "ffn_w_up": dense((DEPTH, D_MODEL, 2 * D_FF), D_MODEL),
        "ffn_conv_w": dense((DEPTH, CONV_WIDTH, D_FF), CONV_WIDTH),
        "ffn_conv_b": small((DEPTH, D_FF), 0.01),
        "ffn_w_down": dense((DEPTH, D_FF, D_MODEL), D_FF),
    }

def reference(x, mix_norm_g, ffn_norm_g, final_norm_g, ab_w_in, a_lambda_q1, a_lambda_k1,
              a_lambda_q2, a_lambda_k2, a_subln_g, ab_w_out, cd_w_in, c_q_norm_g, c_w_uq,
              c_kv_norm_g, c_w_ukv, cd_w_out, ffn_w_up, ffn_conv_w, ffn_conv_b, ffn_w_down):
    seq = x.shape[1]
    cos, sin = rope_tables(seq, HEAD_DIM)
    cos_c, sin_c = rope_tables(seq, C_ROPE_DIM)
    for layer in range(DEPTH):
        h = rms_norm(x, mix_norm_g[layer])
        j = layer // 2
        if layer % 2 == 0:
            lam_init = 0.8 - 0.6 * math.exp(-0.3 * layer)
            y = even_mixer(h, ab_w_in[j], a_lambda_q1[j], a_lambda_k1[j], a_lambda_q2[j],
                           a_lambda_k2[j], a_subln_g[j], ab_w_out[j], lam_init, cos, sin)
        else:
            y = odd_mixer(h, cd_w_in[j], c_q_norm_g[j], c_w_uq[j], c_kv_norm_g[j], c_w_ukv[j],
                          cd_w_out[j], cos_c, sin_c)
        x = x + y
        x = x + conv_ffn(rms_norm(x, ffn_norm_g[layer]), ffn_w_up[layer], ffn_conv_w[layer],
                         ffn_conv_b[layer], ffn_w_down[layer])
    return rms_norm(x, final_norm_g)


_drawn_inputs = setup_inputs


def setup_inputs(seed=0):
    import zlib

    import numpy as np

    out = dict(_drawn_inputs(seed))
    spreads = {}
    factors = {'ffn_norm_g': 2.963,
     'final_norm_g': 2.995,
     'a_lambda_q1': 8.0,
     'a_subln_g': 4.072,
     'c_q_norm_g': 8.0,
     'c_kv_norm_g': 8.0,
     'ffn_conv_b': 8.0}
    for name, (base, spread) in spreads.items():
        noise = np.random.default_rng([zlib.crc32(name.encode()), seed]).standard_normal(out[name].shape)
        drawn = base * np.exp(spread * noise) if base else spread * noise
        out[name] = __import__('jax').numpy.asarray(drawn.astype(out[name].dtype))
    for name, factor in factors.items():
        out[name] = (out[name] * factor).astype(out[name].dtype)
    return out
```

```python
import math
from contextlib import ExitStack

import concourse.bass as bass
from concourse import mybir

SEQ, DM, DFF = 512, 1024, 2816
NT = SEQ // 128
KT = DM // 128
FT = DFF // 128
UNIT = 2048
EPS = 1e-6
LAM_INIT = 0.8 - 0.6 * math.exp(-0.3 * 0)

W_IN0 = 0
W_OUT0 = W_IN0 + 12
W_UP0 = W_OUT0 + 4
W_DN0 = W_UP0 + FT
W_DQK = W_DN0 + FT // 2
W_C = W_DQK + 4
W_DV = W_C + 3
W_UQ = W_DV + 2
W_UKV = W_UQ + 1
W_OUT1 = W_UKV + 1
W_UP1 = W_OUT1 + 4
W_DN1 = W_UP1 + FT
W_ALL = W_DN1 + FT // 2

C_ID, C_CMUL, C_COS64, C_SIN64, C_COS32, C_SIN32, C_END = 0, 128, 640, 896, 1152, 1280, 1408
M_CAUSAL, M_STRICT, M_DIL, M_END = 0, 128, 256, 768
V_LAM, V_SUB, V_CONV, V_CG, V_END = 0, 256, 384, 384 + 2 * FT * 4, 384 + 2 * FT * 4 + 5


def trunk_program(nc, x_in, weights, consts, masks, vectors, gains, out):
    f32, f32r, bf16 = mybir.dt.float32, mybir.dt.float32r, mybir.dt.bfloat16
    ACT, ALU, AX = mybir.ActivationFunctionType, mybir.AluOpType, mybir.AxisListType
    ds = bass.ds
    n_tiles = W_ALL

    with ExitStack() as ctx:
        def sb(name, shape, dt=f32):
            return ctx.enter_context(nc.sbuf_tensor(name, shape, dt))

        def sem(name):
            return ctx.enter_context(nc.semaphore(name))

        x = sb("x", [128, NT, DM])
        hT_hi = sb("hT_hi", [128, KT, SEQ], f32r)
        hT_lo = sb("hT_lo", [128, KT, SEQ], f32r)
        w_raw = sb("w_raw", [128, 2, UNIT])
        w_hi = sb("w_hi", [128, 2, UNIT], f32r)
        w_lo = sb("w_lo", [128, 2, UNIT], f32r)
        region = sb("region", [128, 17024])
        y = region[:, 0:12288].rearrange("p (t n) -> p t n", t=NT)
        act = region[:, 0:FT * SEQ].rearrange("p (j n) -> p j n", j=FT)
        final = region[:, 0:4096].rearrange("p (t n) -> p t n", t=NT)
        dT = region[:, 0:4096].rearrange("p (c n) -> p c n", c=8)
        cT = region[:, 4096:6656].rearrange("p (c n) -> p c n", c=5)
        dv = region[:, 6656:8704].rearrange("p (t n) -> p t n", t=NT)
        q_tok = region[:, 8704:10240].rearrange("p (t n) -> p t n", t=NT)
        kv_tok = region[:, 10240:13312].rearrange("p (t n) -> p t n", t=NT)
        k_tok = region[:, 13312:14848].rearrange("p (t n) -> p t n", t=NT)
        kr = region[:, 14848:14976].rearrange("p (t n) -> p t n", t=NT)
        o_D = region[:, 14976:17024].rearrange("p (t n) -> p t n", t=NT)
        o_C = region[:, 4096:6144].rearrange("p (t n) -> p t n", t=NT)
        c_tmp = region[:, 4096:5120].rearrange("p (a n) -> p a n", a=2)

        xn = sb("xn", [128, 2, DM])
        probs = xn[:, 0, :].rearrange("p (a n) -> p a n", a=2)
        probsT = xn[:, 1, :].rearrange("p (a n) -> p a n", a=2)
        stage = sb("stage", [128, 2, SEQ])
        qk = sb("qk", [128, 4, SEQ])
        tmp = sb("tmp", [128, 2, SEQ])
        gain = sb("gain", [128, DM])
        cst = sb("cst", [128, C_END])
        vec = sb("vec", [128, V_END])
        mask_bf = sb("mask_bf", [128, M_END], bf16)
        ident_bf = sb("ident_bf", [128, 128], bf16)
        ones = sb("ones", [128, 1])
        sub_gain = sb("sub_gain", [128, 128])
        neg_lam = sb("neg_lam", [128, 1])
        lam_s = sb("lam_s", [128, 4])
        ss = sb("ss", [128, 16])
        var = sb("var", [128, 16])
        sd = sb("sd", [128, 16])
        rstd = sb("rstd", [128, 16])
        rs_a = sb("rs_a", [128, 16])
        neg_max = sb("neg_max", [128, 8])
        den = sb("den", [128, 8])
        rden = sb("rden", [128, 8])
        rden1 = sb("rden1", [128, 4])
        o_tmp = sb("o_tmp", [128, 128])

        ident = cst[:, C_ID:C_ID + 128]
        cmul = cst[:, C_CMUL:C_CMUL + 512]
        cos64 = cst[:, C_COS64:C_COS64 + 256].rearrange("p (t d) -> p t d", t=NT)
        sin64 = cst[:, C_SIN64:C_SIN64 + 256].rearrange("p (t d) -> p t d", t=NT)
        cos32 = cst[:, C_COS32:C_COS32 + 128].rearrange("p (t d) -> p t d", t=NT)
        sin32 = cst[:, C_SIN32:C_SIN32 + 128].rearrange("p (t d) -> p t d", t=NT)
        masks_f32 = region[:, 0:M_END]

        ps = ctx.enter_context(nc.psum_tensor("ps", [128, 8, 512], f32))

        x_loaded = [sem(f"x_loaded{t}") for t in range(NT)]
        cst_loaded, vec_loaded, mask_loaded = sem("cst_loaded"), sem("vec_loaded"), sem("mask_loaded")
        gain_loaded, out_stored = sem("gain_loaded"), sem("out_stored")
        w_loaded = [sem("w_loaded0"), sem("w_loaded1")]
        w_hi_ready, w_lo_ready, mm_done = sem("w_hi_ready"), sem("w_lo_ready"), sem("mm_done")
        masks_ready, ones_ready = sem("masks_ready"), sem("ones_ready")
        lam_dots, lam_exps = sem("lam_dots"), sem("lam_exps")
        x_done = sem("x_done")
        ss_ready, var_ready, sd_ready = sem("ss_ready"), sem("var_ready"), sem("sd_ready")
        src_ready = sem("src_ready")
        turned, turn_hi, turn_lo = sem("turned"), sem("turn_hi"), sem("turn_lo")
        in_bank_free = sem("in_bank_free")
        rope_ready, qk_turned, qT_ready, kT_ready = sem("rope_ready"), sem("qk_turned"), sem("qT_ready"), sem("kT_ready")
        scores_ready, max_ready, exp_ready, mult_ready = sem("scores_ready"), sem("max_ready"), sem("exp_ready"), sem("mult_ready")
        pT_ready, pT_copied, pv_ready, o_ready = sem("pT_ready"), sem("pT_copied"), sem("pv_ready"), sem("o_ready")
        conv_started, conv_done, silu_ready = [[sem(f"{n}{l}") for l in range(2)] for n in
                                               ("conv_started", "conv_done", "silu_ready")]
        val_bank_free = [sem(f"val_bank_free{l}") for l in range(2)]
        act_hi, act_lo = [[sem(f"{n}{l}") for l in range(2)] for n in ("act_hi", "act_lo")]
        dT_copied, c_copied, sq_ready, kr_copied = sem("dT_copied"), sem("c_copied"), sem("sq_ready"), sem("kr_copied")
        c_stats, dv_copied, c_hi, c_lo, q_scaled, kv_scaled, c_roped = (
            sem(n) for n in ("c_stats", "dv_copied", "c_hi", "c_lo", "q_scaled", "kv_scaled", "c_roped"))
        d_q, d_scores, d_soft, d_sp, d_arg, d_exp, d_turned, d_copied, d_pv, d_out = (
            sem(n) for n in ("d_q", "d_scores", "d_soft", "d_sp", "d_arg", "d_exp", "d_turned", "d_copied", "d_pv", "d_out"))
        act_own, dve_own, pool_own = sem("act_own"), sem("dve_own"), sem("pool_own")

        block = ctx.enter_context(nc.Block())

        class Own:

            def __init__(self, eng, steps):
                self.eng, self.steps, self.n, self.shift = eng, steps, 0, 0

            def mark(self, ins):
                ins.then_inc(self.steps, 1)
                self.n += 1
                return self.n

            def wait(self, value):
                self.eng.wait_ge(self.steps, self.shift + value)

            def link(self, ins):
                self.wait(self.mark(ins))

            def loop(self, i, turns, marks):
                start, self.shift = self.n, i * marks

                def end():
                    assert self.n - start == marks, self.n - start
                    self.n, self.shift = start + turns * marks, 0
                return end

        def norm_base(k):
            return 4 * (k - 1)

        def unit(k):
            return k // 2, k % 2, 128 * (k // 2 + 1)

        @block.sync
        def _(sp):
            def load(m, slot):
                sp.dma_start(w_raw[:, slot, :], weights[m, :, :]).then_inc(w_loaded[slot], 16)

            load(0, 0)
            load(1, 1)
            with sp.Fori(1, n_tiles // 2) as j:
                for slot in range(2):
                    sp.wait_ge(w_lo_ready, 2 * j + slot - 1)
                    sp.dma_start(w_raw[:, slot, :].unsqueeze(1),
                                 weights[ds(2 * j + slot, 1), :, :].rearrange("m p n -> p m n"))\
                      .then_inc(w_loaded[slot], 16)
            if n_tiles % 2:
                sp.wait_ge(w_lo_ready, n_tiles - 2)
                load(n_tiles - 1, (n_tiles - 1) % 2)
            for t in range(NT):
                sp.wait_ge(src_ready, 5 * NT + t + 1)
                sp.dma_start(out[0, t * 128:(t + 1) * 128, :], final[:, t, :]).then_inc(out_stored, 16)
            sp.wait_ge(out_stored, 16 * NT)

        @block.gpsimd
        def _(pool):
            own = Own(pool, pool_own)

            def split_lo(m, slot):
                pool.wait_ge(w_hi_ready, m + 1)
                pool.tensor_tensor(w_lo[:, slot, :], w_raw[:, slot, :], w_hi[:, slot, :].bitcast(f32),
                                   ALU.subtract).then_inc(w_lo_ready, 1)

            def split_range(a, b):
                b = min(b, n_tiles)
                if a >= b:
                    return
                if a % 2:
                    split_lo(a, 1)
                    a += 1
                if b - a >= 2:
                    with pool.Fori(0, (b - a) // 2) as j:
                        for slot in range(2):
                            split_lo(2 * j + (a + slot), slot)
                if (b - a) % 2:
                    split_lo(b - 1, 0)

            def rotate(dst, src, cos, sin, shape, half, done):
                t1 = tmp[:, 0, :].rearrange(shape[0], **shape[1])
                t2 = tmp[:, 1, :].rearrange(shape[0], **shape[1])
                own.mark(pool.tensor_tensor(t1, src, cos, ALU.mult))
                own.mark(pool.tensor_tensor(t2[:, :, :, 0:half], src[:, :, :, half:], sin[:, :, :, 0:half], ALU.mult))
                own.link(pool.tensor_tensor(t2[:, :, :, half:], src[:, :, :, 0:half], sin[:, :, :, half:], ALU.mult))
                pool.tensor_tensor(dst, t1, t2, ALU.add).then_inc(done, 1)

            heads64 = ("p (t m d) -> p t m d", dict(t=NT, m=2))

            def table(tab, shape):
                return tab.unsqueeze(2).broadcast_to(shape)

            def rope_head(q_base, h, g):
                for s in range(2):
                    src = y[:, :, ds(h * 128 + (q_base + 512 * s), 128)].rearrange("p t (m d) -> p t m d", m=2)
                    dst = stage[:, s, :].rearrange(heads64[0], **heads64[1])
                    rotate(dst, src, table(cos64, [128, NT, 2, 64]), table(sin64, [128, NT, 2, 64]),
                           heads64, 32, rope_ready)
                    pool.wait_ge(rope_ready, 2 * g + s + 1)

            split_range(0, W_OUT0 + 2)
            pool.wait_ge(in_bank_free, 8 + 24)
            rope_head(0, 0, 0)
            with pool.Fori(1, 4) as h:
                pool.wait_ge(qk_turned, 2 * h)
                end = own.loop(h - 1, 3, 6)
                rope_head(0, h, h)
                end()
            with pool.Fori(0, 4) as h:
                pool.wait_ge(qk_turned, 2 * h + 8)
                end = own.loop(h, 4, 6)
                rope_head(1536, h, h + 4)
                end()
            split_range(W_OUT0 + 2, W_OUT1 + 2)
            pool.wait_ge(kr_copied, 1)
            pool.wait_ge(c_lo, 5)
            kr4 = kr[:, :, :].unsqueeze(2)
            t1 = c_tmp[:, 0, 0:128].rearrange("p (t d) -> p t d", t=NT).unsqueeze(2)
            t2 = c_tmp[:, 1, 0:128].rearrange("p (t d) -> p t d", t=NT).unsqueeze(2)
            c4, s4 = cos32.unsqueeze(2), sin32.unsqueeze(2)
            own.mark(pool.tensor_tensor(t1, kr4, c4, ALU.mult))
            own.mark(pool.tensor_tensor(t2[:, :, :, 0:16], kr4[:, :, :, 16:], s4[:, :, :, 0:16], ALU.mult))
            own.link(pool.tensor_tensor(t2[:, :, :, 16:], kr4[:, :, :, 0:16], s4[:, :, :, 16:], ALU.mult))
            own.link(pool.tensor_tensor(kr4, t1, t2, ALU.add))
            pool.wait_ge(q_scaled, NT)
            q4 = q_tok.rearrange("p t (h d) -> p t h d", h=4)[:, :, :, 64:96]
            t1 = c_tmp[:, 0, :].rearrange("p (t h d) -> p t h d", t=NT, h=4)
            t2 = c_tmp[:, 1, :].rearrange("p (t h d) -> p t h d", t=NT, h=4)
            c4, s4 = table(cos32, [128, NT, 4, 32]), table(sin32, [128, NT, 4, 32])
            own.mark(pool.tensor_tensor(t1, q4, c4, ALU.mult))
            own.mark(pool.tensor_tensor(t2[:, :, :, 0:16], q4[:, :, :, 16:], s4[:, :, :, 0:16], ALU.mult))
            own.link(pool.tensor_tensor(t2[:, :, :, 16:], q4[:, :, :, 0:16], s4[:, :, :, 16:], ALU.mult))
            pool.tensor_tensor(q4, t1, t2, ALU.add).then_inc(c_roped, 1)
            pool.wait_ge(kv_scaled, NT)
            k4 = k_tok.rearrange("p t (h d) -> p t h d", h=4)
            pool.tensor_copy(k4[:, :, :, 0:64],
                             kv_tok.rearrange("p t (h d) -> p t h d", h=4)[:, :, :, 0:64]).then_inc(c_roped, 1)
            pool.tensor_copy(k4[:, :, :, 64:96],
                             kr.unsqueeze(2).broadcast_to([128, NT, 4, 32])).then_inc(c_roped, 1)
            split_range(W_OUT1 + 2, n_tiles)

        @block.scalar
        def _(sc):
            own = Own(sc, act_own)

            def split_hi(slot, fill):
                sc.wait_ge(w_loaded[slot], 16 * fill)
                sc.activation(w_hi[:, slot, :], w_raw[:, slot, :], ACT.Copy).then_inc(w_hi_ready, 1)

            def split_after(n):
                if n + 2 < n_tiles:
                    sc.wait_ge(mm_done, 4 * (n + 1))
                    split_hi(n % 2, n // 2 + 2)

            def split_after_in_loop(i, n0):
                sc.wait_ge(mm_done, 8 * i + 4 * (n0 + 1))
                split_hi(n0 % 2, i + (n0 // 2 + 2))

            gains_asked = [0]

            def load_gain():
                g = gains_asked[0]
                sc.dma_start(gain[:, :], gains[:, g, :]).then_inc(gain_loaded, 16)
                gains_asked[0] += 1

            roots = [0]

            def root(width):
                sc.wait_ge(var_ready, roots[0] + 1)
                roots[0] += 1
                sc.activation(sd[:, 0:width], var[:, 0:width], ACT.Sqrt).then_inc(sd_ready, 1)

            def squares(k):
                for t in range(NT):
                    if k == 0:
                        sc.wait_ge(x_loaded[t], 16)
                    else:
                        sc.wait_ge(x_done, norm_base(k) + t + 1)
                    if t >= 1:
                        sc.wait_ge(ss_ready, 4 * k + t)
                    sc.activation(tmp[:, :, :].rearrange("p a n -> p (a n)"), x[:, t, :], ACT.Square,
                                  accum_out=ss[:, t:t + 1]).then_inc(ss_ready, 1)
                root(NT)

            turns = [0]

            def turn():
                for b in range(8):
                    t, g = b // 2, b % 2
                    sc.wait_ge(turned, 8 * turns[0] + b + 1)
                    sc.activation(hT_hi[:, 4 * g:4 * g + 4, t * 128:(t + 1) * 128],
                                  ps[:, b, :].rearrange("p (j n) -> p j n", j=4), ACT.Copy).then_inc(turn_hi, 1)
                turns[0] += 1

            def attention(kind, h, g):
                n_q = 2 if kind == "C" else 1
                for s in range(n_q):
                    if kind == "C":
                        sc.wait_ge(qk_turned, 16 + 4 * (g - 8) + 2 * s + 1)
                        sc.activation(qk[0:96, s, :], ps[0:96, 4 + 2 * s, :], ACT.Copy, scale=96 ** -0.5)\
                          .then_inc(qT_ready, 1)
                    else:
                        sc.wait_ge(qk_turned, 2 * g + 1)
                        sc.activation(qk[:, 0, :], ps[:, 4, :], ACT.Copy, scale=0.125).then_inc(qT_ready, 1)
                for k in range(9):
                    if k < 8:
                        i, m, w = unit(k)
                        sc.wait_ge(max_ready, 8 * g + k + 1)
                        if k >= 2:
                            sc.wait_ge(pT_ready, 8 * g + k - 1)
                        if kind == "B":
                            sc.activation(probs[:, m, 0:w], ps[:, m, 0:w], ACT.Exp, bias=neg_max[:, k:k + 1])\
                              .then_inc(exp_ready, 1)
                        else:
                            sc.activation(probs[:, m, 0:w], ps[:, m, 0:w], ACT.Exp, bias=neg_max[:, k:k + 1],
                                          accum_out=den[:, k:k + 1]).then_inc(exp_ready, 1)
                    if k >= 1:
                        i, m, w = unit(k - 1)
                        sc.wait_ge(pT_ready, 8 * g + k)
                        if k >= 3:
                            sc.wait_ge(pv_ready, 8 * g + k - 2)
                        sc.activation(probsT[:, m, 0:w], ps[:, 2 + m, 0:w], ACT.Copy).then_inc(pT_copied, 1)

            def mlp(l, n0):
                with sc.Fori(0, FT // 2) as i:
                    for s in range(2):
                        sc.wait_ge(mm_done, 8 * i + 4 * n0 + 2 * s + 2)
                        col = V_CONV + l * FT * 4 + 4 * s
                        sc.activation(qk[:, s, :], ps[:, s, :], ACT.Identity,
                                      scale=vec[:, ds(8 * i + (col + 2), 1)],
                                      bias=vec[:, ds(8 * i + (col + 3), 1)]).then_inc(conv_started[l], 1)
                    split_after_in_loop(i, n0)
                    for s in range(2):
                        sc.wait_ge(conv_done[l], 2 * i + s + 1)
                        sc.activation(qk[:, 2 + s, :], qk[:, s, :], ACT.Silu).then_inc(silu_ready[l], 1)
                    split_after_in_loop(i, n0 + 1)
                    sc.wait_ge(silu_ready[l], 2 * i + 2)
                n1 = n0 + FT

                def halves(u0, kt, slot, count=4):
                    sc.activation(hT_hi[:, 4 * slot + u0:4 * slot + u0 + count, :], act[:, ds(kt, count), :], ACT.Copy)\
                      .then_inc(act_hi[l], count)

                sc.wait_ge(val_bank_free[l], 2 + FT)
                halves(0, 0, 0, 2)
                halves(2, 2, 0, 2)
                halves(0, 4, 1)
                for j in range(4):
                    sc.wait_ge(mm_done, 4 * (n1 + j + 1))
                    split_hi(j % 2, (n1 + j) // 2 + 2)
                    if j == 3:
                        halves(0, 20, 1, 2)
                        halves(2, 0, 1, 2)
                    else:
                        halves(0, 8 + 4 * j, j % 2)
                with sc.Fori(0, 2) as i:
                    for b in range(2):
                        sc.wait_ge(mm_done, 8 * i + 4 * (n1 + b + 5))
                        split_hi(b, i + ((n1 + 4) // 2 + 2))
                        halves(0, 8 * i + (2 + 4 * b), b)
                sc.wait_ge(mm_done, 4 * (n1 + 9))
                split_hi(0, (n1 + 8) // 2 + 2)
                halves(0, 18, 0)
                for j in (9, 10):
                    split_after(n1 + j)

            for t in range(NT):
                sc.dma_start(x[:, t, :], x_in[0, t * 128:(t + 1) * 128, :]).then_inc(x_loaded[t], 16)
            sc.dma_start(cst[:, :], consts).then_inc(cst_loaded, 16)
            load_gain()
            sc.dma_start(vec[:, :], vectors).then_inc(vec_loaded, 16)
            sc.dma_start(masks_f32, masks).then_inc(mask_loaded, 16)
            squares(0)
            split_hi(0, 1)
            split_hi(1, 1)
            turn()
            load_gain()
            sc.wait_ge(lam_dots, 1)
            sc.activation(lam_s[:, 2:4], lam_s[:, 0:2], ACT.Exp).then_inc(lam_exps, 1)
            with sc.Fori(0, 3) as i:
                for j in range(4):
                    sc.wait_ge(mm_done, 16 * i + 4 * (j + 1))
                    split_hi(j % 2, 2 * i + (j // 2 + 2))
            with sc.Fori(0, 4) as h:
                attention("A", h, h)
            with sc.Fori(0, 4) as h:
                attention("B", h, h + 4)
            root(16)
            turn()
            for n in range(W_OUT0, W_UP0):
                split_after(n)
            squares(1)
            turn()
            load_gain()
            mlp(0, W_UP0)
            squares(2)
            turn()
            load_gain()
            for n in range(W_DQK, W_C):
                split_after(n)
            for c in range(5):
                n = W_C + c // 2
                sc.wait_ge(mm_done, 4 * n + 2 * (c % 2) + 2)
                sc.activation(cT[:, c, :], ps[:, c, :], ACT.Copy, scale=vec[:, V_CG + c:V_CG + c + 1])\
                  .then_inc(c_copied, 1)
                sq = qk[:, c, :] if c < 4 else tmp[:, 0, :]
                sc.activation(sq, ps[:, c, :], ACT.Square).then_inc(sq_ready, 1)
                if c % 2:
                    split_after(n)
            split_after(W_C + 2)
            root(8)
            split_after(W_DV)
            split_after(W_DV + 1)
            sc.wait_ge(c_copied, 5)
            for c in range(5):
                sc.activation(hT_hi[:, c, :], cT[:, c, :], ACT.Copy).then_inc(c_hi, 1)
            split_after(W_UQ)
            split_after(W_UKV)
            with sc.Fori(0, 2) as p:
                for m in range(2):
                    sc.activation(qk[:, m, :].unsqueeze(1), dT[:, ds(2 * p + m, 1), :], ACT.Copy, scale=128 ** -0.5)\
                      .then_inc(d_q, 1)
                end = own.loop(p, 2, 16)
                for k in range(9):
                    if k < 8:
                        i, m, w = unit(k)
                        bank = (0, 1, 4, 5)[k % 4]
                        sc.wait_ge(d_scores, 8 * p + k + 1)
                        if k >= 2:
                            sc.wait_ge(d_sp, 8 * p + k - 1)
                        own.link(sc.activation(tmp[:, m, 0:w], ps[:, bank, 0:w], ACT.Abs))
                        own.link(sc.activation(tmp[:, m, 0:w], tmp[:, m, 0:w], ACT.Exp, scale=-1.0))
                        sc.activation(tmp[:, m, 0:w], tmp[:, m, 0:w], ACT.Ln, bias=ones[:, 0:1]).then_inc(d_soft, 1)
                    if k >= 1:
                        i, m, w = unit(k - 1)
                        sc.wait_ge(d_arg, 8 * p + k)
                        sc.activation(probs[:, m, 0:w], probs[:, m, 0:w], ACT.Exp).then_inc(d_exp, 1)
                end()
            for g in (8, 9):
                attention("C", g - 8, g)
            turn()
            for n in range(W_OUT1, W_UP1):
                split_after(n)
            squares(3)
            turn()
            load_gain()
            mlp(1, W_UP1)
            squares(4)

        @block.vector
        def _(ve):
            own = Own(ve, dve_own)
            roots = [0]
            norms = [0]
            turns = [0]

            def rsqrt(width, scales):
                for (a, b), s in scales:
                    ins = ve.tensor_scalar(var[:, a:b], ss[:, a:b], s, EPS, ALU.mult, ALU.add)
                    if b < width:
                        own.link(ins)
                ins.then_inc(var_ready, 1)
                roots[0] += 1
                ve.wait_ge(sd_ready, roots[0])
                own.link(ve.reciprocal(rstd[:, 0:width], sd[:, 0:width]))
                own.link(ve.tensor_tensor(rs_a[:, 0:width], rstd[:, 0:width], rstd[:, 0:width], ALU.mult))
                own.link(ve.tensor_tensor(rs_a[:, 0:width], rs_a[:, 0:width], var[:, 0:width], ALU.mult))
                own.link(ve.tensor_scalar(rs_a[:, 0:width], rs_a[:, 0:width], -0.5, 1.5, ALU.mult, ALU.add))
                own.link(ve.tensor_tensor(rstd[:, 0:width], rstd[:, 0:width], rs_a[:, 0:width], ALU.mult))

            def lows(b):
                t, g = b // 2, b % 2
                ve.wait_ge(turn_hi, 8 * turns[0] + b + 1)
                hi = hT_hi[:, 4 * g:4 * g + 4, t * 128:(t + 1) * 128]
                ve.tensor_tensor(hT_lo[:, 4 * g:4 * g + 4, t * 128:(t + 1) * 128],
                                 ps[:, b, :].rearrange("p (j n) -> p j n", j=4), hi.bitcast(f32),
                                 ALU.subtract).then_inc(turn_lo, 1)

            def norm(k, last=False):
                ve.wait_ge(ss_ready, 4 * (k + 1))
                rsqrt(NT, [((0, NT), 1.0 / DM)])
                ve.wait_ge(gain_loaded, 16 * (k + 1))
                for t in range(NT):
                    if t >= 2 and not last:
                        ve.wait_ge(turned, 8 * turns[0] + 2 * (t - 1))
                    dst = final[:, t, :] if last else xn[:, t % 2, :]
                    ve.scalar_tensor_tensor(dst, x[:, t, :], rstd[:, t:t + 1], gain[:, :], ALU.mult, ALU.mult)\
                      .then_inc(src_ready, 1)
                    if t >= 1 and not last:
                        lows(2 * t - 2)
                        lows(2 * t - 1)
                if not last:
                    lows(6)
                    lows(7)
                    turns[0] += 1

            def attention(kind, h, g):
                for s in range(2 if kind == "C" else 1):
                    if kind == "C":
                        ve.wait_ge(qk_turned, 16 + 4 * (g - 8) + 2 * s + 2)
                        ve.tensor_copy(qk[0:96, 2 + s, :], ps[0:96, 5 + 2 * s, :]).then_inc(kT_ready, 1)
                    else:
                        ve.wait_ge(qk_turned, 2 * g + 2)
                        ve.tensor_copy(qk[:, 2, :], ps[:, 5, :]).then_inc(kT_ready, 1)
                for k in range(11):
                    if k < 8:
                        i, m, w = unit(k)
                        ve.wait_ge(scores_ready, 8 * g + k + 1)
                        ve.tensor_reduce(neg_max[:, k:k + 1], ps[:, m, 0:w], AX.X, ALU.max, negate=True)\
                          .then_inc(max_ready, 1)
                    if kind == "B" and 1 <= k <= 8:
                        i, m, w = unit(k - 1)
                        ve.wait_ge(exp_ready, 8 * g + k)
                        ve.scalar_tensor_tensor(probs[:, m, 0:w], probs[:, m, 0:w], 1.0, cmul[:, 512 - w:512],
                                                ALU.mult, ALU.mult, accum_out=den[:, k - 1:k])\
                          .then_inc(mult_ready, 1)
                    if k >= 4 and k % 2 == 0:
                        i = (k - 4) // 2
                        bank = ps[:, 6 + i % 2, :]
                        ve.wait_ge(pv_ready, 8 * g + 2 * i + 2)
                        own.link(ve.reciprocal(rden[:, 2 * i:2 * i + 2], den[:, 2 * i:2 * i + 2]))
                        if kind == "A":
                            own.link(ve.tensor_tensor(rden1[:, i:i + 1], rden[:, 2 * i + 1:2 * i + 2], neg_lam[:, :], ALU.mult))
                            own.link(ve.tensor_scalar(o_tmp[:, :], bank[:, 128:256], rden1[:, i:i + 1], None, ALU.mult))
                            ve.scalar_tensor_tensor(y[:, i, ds(h * 128, 128)], bank[:, 0:128], rden[:, 2 * i:2 * i + 1],
                                                    o_tmp[:, :], ALU.mult, ALU.add).then_inc(o_ready, 1)
                        elif kind == "B":
                            ve.tensor_tensor(y[:, i, ds(h * 128 + 1536, 128)].rearrange("p (m d) -> p m d", m=2),
                                             bank[:, 0:128].rearrange("p (m d) -> p m d", m=2),
                                             rden[:, 2 * i:2 * i + 2].unsqueeze(2).broadcast_to([128, 2, 64]),
                                             ALU.mult).then_inc(o_ready, 1)
                        else:
                            ve.tensor_tensor(o_C[:, i, h * 256:(h + 1) * 256].rearrange("p (m d) -> p m d", m=2),
                                             bank[:, 0:256].rearrange("p (m d) -> p m d", m=2),
                                             rden[:, 2 * i:2 * i + 2].unsqueeze(2).broadcast_to([128, 2, 128]),
                                             ALU.mult).then_inc(o_ready, 1)

            def residual(n0):
                for c in range(2):
                    for t in range(NT):
                        ve.wait_ge(mm_done, 4 * (n0 + 2 * c + 1) + t + 1)
                        part = x[:, t, c * 512:(c + 1) * 512]
                        ins = ve.tensor_tensor(part, part, ps[:, 4 * c + t, :], ALU.add)
                        if c:
                            ins.then_inc(x_done, 1)

            def mlp(l, n0):
                ve.sem_inc(val_bank_free[l], 2)
                with ve.Fori(0, FT // 2) as i:
                    end = own.loop(i, FT // 2, 2)
                    for s in range(2):
                        col = V_CONV + l * FT * 4 + 4 * s
                        ve.wait_ge(conv_started[l], 2 * i + s + 1)
                        own.link(ve.scalar_tensor_tensor(qk[:, s, 1:SEQ], ps[:, s, 0:SEQ - 1],
                                                         vec[:, ds(8 * i + (col + 1), 1)], qk[:, s, 1:SEQ],
                                                         ALU.mult, ALU.add))
                        ve.scalar_tensor_tensor(qk[:, s, 2:SEQ], ps[:, s, 0:SEQ - 2], vec[:, ds(8 * i + col, 1)],
                                                qk[:, s, 2:SEQ], ALU.mult, ALU.add).then_inc(conv_done[l], 1)
                    for s in range(2):
                        ve.wait_ge(silu_ready[l], 2 * i + s + 1)
                        ve.wait_ge(mm_done, 8 * i + 4 * (n0 + 1) + 2 * s + 2)
                        ve.tensor_tensor(act[:, ds(2 * i + s, 1), :], ps[:, 2 + s:3 + s, :], qk[:, 2 + s:3 + s, :],
                                         ALU.mult).then_inc(val_bank_free[l], 1)
                    end()
                n1 = n0 + FT

                def lows_of(done, u0, kt, slot, count=4):
                    ve.wait_ge(act_hi[l], done)
                    places = slice(4 * slot + u0, 4 * slot + u0 + count)
                    ve.tensor_tensor(hT_lo[:, places, :], act[:, ds(kt, count), :], hT_hi[:, places, :].bitcast(f32),
                                     ALU.subtract).then_inc(act_lo[l], count)

                def column_half(c, ready):
                    for t in range(NT):
                        ve.wait_ge(mm_done, ready(t))
                        part = x[:, t, c * 512:(c + 1) * 512]
                        ins = ve.tensor_tensor(part, part, ps[:, 4 * c + t, :], ALU.add)
                        if c:
                            ins.then_inc(x_done, 1)

                lows_of(2, 0, 0, 0, 2)
                lows_of(4, 2, 2, 0, 2)
                lows_of(8, 0, 4, 1)
                for j in range(2, 5):
                    lows_of(4 * j + 4, 0, 4 * j, j % 2)
                lows_of(22, 0, 20, 1, 2)
                lows_of(24, 2, 0, 1, 2)
                lows_of(28, 0, 2, 0)
                column_half(0, lambda t: 4 * (n1 + 5) + 2)
                lows_of(32, 0, 6, 1)
                for j in range(8, 11):
                    lows_of(4 * j + 4, 0, 4 * j - FT, j % 2)
                column_half(1, lambda t: 4 * (n1 + 10) + t + 1)

            ve.memset(ones[:, :], 1.0).then_inc(ones_ready, 1)
            norm(0)
            ve.wait_ge(cst_loaded, 16)
            own.mark(ve.tensor_copy(ident_bf[:, :], ident))
            ve.wait_ge(mask_loaded, 16)
            ve.tensor_copy(mask_bf[:, :], masks_f32).then_inc(masks_ready, 1)
            ve.wait_ge(vec_loaded, 16)
            for j in range(2):
                a = V_LAM + 128 * j
                own.link(ve.tensor_tensor(o_tmp[:, 64 * j:64 * j + 64], vec[:, a:a + 64], vec[:, a + 64:a + 128], ALU.mult))
            ve.tensor_reduce(lam_s[:, 0:2], o_tmp[:, :].rearrange("p (a n) -> p a n", a=2), AX.X, ALU.add)\
              .then_inc(lam_dots, 1)
            own.mark(ve.tensor_scalar(sub_gain[:, :], vec[:, V_SUB:V_SUB + 128], 1.0 - LAM_INIT, None, ALU.mult))
            ve.wait_ge(lam_exps, 1)
            own.link(ve.tensor_tensor(neg_lam[:, :], lam_s[:, 3:4], lam_s[:, 2:3], ALU.subtract))
            own.link(ve.tensor_scalar(neg_lam[:, :], neg_lam[:, :], -LAM_INIT, None, ALU.add))
            ve.wait_ge(masks_ready, 1)
            ve.sem_inc(in_bank_free, 8)
            with ve.Fori(0, 3) as i:
                for s in range(2):
                    for t in range(NT):
                        ve.wait_ge(mm_done, 16 * i + 4 * (2 * s + 1) + t + 1)
                        ve.tensor_copy(y[:, t, ds(1024 * i + 512 * s, 512)], ps[:, 4 * s + t, :])\
                          .then_inc(in_bank_free, 1)
            with ve.Fori(0, 4) as h:
                end = own.loop(h, 4, 12)
                attention("A", h, h)
                end()
            with ve.Fori(0, 4) as h:
                end = own.loop(h, 4, 4)
                attention("B", h, h + 4)
                end()
            ve.wait_ge(o_ready, 32)
            for t in range(NT):
                own.link(ve.tensor_tensor(tmp[:, 0, :], y[:, t, 0:512], y[:, t, 0:512], ALU.mult))
                own.link(ve.tensor_reduce(ss[:, 4 * t:4 * t + 4], tmp[:, 0, :].rearrange("p (h d) -> p h d", h=4),
                                          AX.X, ALU.add))
            rsqrt(16, [((0, 16), 1.0 / 128)])
            for t in range(NT):
                if t >= 2:
                    ve.wait_ge(turned, 8 * turns[0] + 2 * (t - 1) - 1)
                for h in range(4):
                    ins = ve.scalar_tensor_tensor(xn[:, t % 2, h * 128:(h + 1) * 128], y[:, t, h * 128:(h + 1) * 128],
                                                  rstd[:, 4 * t + h:4 * t + h + 1], sub_gain[:, :], ALU.mult, ALU.mult)
                ins.then_inc(src_ready, 1)
                if t >= 1:
                    lows(2 * t - 2)
                    lows(2 * t - 1)
            lows(6)
            lows(7)
            turns[0] += 1
            residual(W_OUT0)
            norm(1)
            mlp(0, W_UP0)
            norm(2)
            with ve.Fori(0, 2) as i:
                for c in range(4):
                    ve.wait_ge(mm_done, 8 * i + 4 * (W_DQK + c // 2) + 2 * (c % 2) + 2)
                    ve.tensor_copy(dT[:, ds(4 * i + c, 1), :], ps[:, ds(4 * i + c, 1), :]).then_inc(dT_copied, 1)
            ve.wait_ge(mm_done, 4 * (W_C + 3))
            ve.tensor_copy(kr, ps[:, 5, 0:128].rearrange("p (t d) -> p t d", t=NT)).then_inc(kr_copied, 1)
            ve.wait_ge(c_stats, 1)
            own.link(ve.tensor_copy(ss[:, 0:8], ps[:, 6, 0:8]))
            rsqrt(8, [((0, 4), 1.0 / 384), ((4, 8), 1.0 / 256)])
            for t in range(NT):
                ve.wait_ge(mm_done, 4 * (W_DV + 1) + t + 1)
                ve.tensor_copy(dv[:, t, :], ps[:, t, :]).then_inc(dv_copied, 1)
            for c in range(5):
                ve.wait_ge(c_hi, c + 1)
                ve.tensor_tensor(hT_lo[:, c, :], cT[:, c, :], hT_hi[:, c, :].bitcast(f32), ALU.subtract)\
                  .then_inc(c_lo, 1)
            for t in range(NT):
                ve.wait_ge(mm_done, 4 * W_UQ + t + 1)
                ve.tensor_scalar(q_tok[:, t, :], ps[:, 4 + t, 0:384], rstd[:, t:t + 1], None, ALU.mult)\
                  .then_inc(q_scaled, 1)
            for t in range(NT):
                ve.wait_ge(mm_done, 4 * W_UKV + t + 1)
                for c in range(2):
                    ins = ve.tensor_scalar(kv_tok[:, t, 384 * c:384 * c + 384], ps[:, 4 * c + t, 0:384],
                                           rstd[:, 4 + t:5 + t], None, ALU.mult)
                ins.then_inc(kv_scaled, 1)
            with ve.Fori(0, 2) as p:
                end = own.loop(p, 2, 8)
                for k in range(12):
                    if k < 8:
                        i, m, w = unit(k)
                        bank = (0, 1, 4, 5)[k % 4]
                        ve.wait_ge(d_soft, 8 * p + k + 1)
                        sp_ = stage[:, m, 0:w]
                        ve.scalar_tensor_tensor(sp_, ps[:, bank, 0:w], 0.0, tmp[:, m, 0:w], ALU.max, ALU.add)\
                          .then_inc(d_sp, 1)
                        ve.wait_ge(d_sp, 8 * p + k + 1)
                        own.link(ve.tensor_tensor_scan(sp_[:, ::-1], sp_[:, ::-1], sp_[:, ::-1], 0.0, ALU.add, ALU.max))
                        if k >= 2:
                            ve.wait_ge(d_turned, 8 * p + k - 1)
                        ve.tensor_tensor(probs[:, m, 0:w], ps[:, bank, 0:w], sp_, ALU.subtract).then_inc(d_arg, 1)
                    if 2 <= k < 10:
                        i, m, w = unit(k - 2)
                        ve.wait_ge(d_turned, 8 * p + k - 1)
                        if k >= 4:
                            ve.wait_ge(d_pv, 8 * p + k - 3)
                        ve.tensor_copy(probsT[:, m, 0:w], ps[:, 2 + m, 0:w]).then_inc(d_copied, 1)
                    if k >= 5 and k % 2:
                        i = (k - 5) // 2
                        ve.wait_ge(d_pv, 8 * p + 2 * i + 2)
                        ve.tensor_copy(o_D[:, i, ds(256 * p, 256)], ps[:, 6 + i % 2, 0:256]).then_inc(d_out, 1)
                end()
            for g in (8, 9):
                attention("C", g - 8, g)
            for b in range(8):
                lows(b)
            turns[0] += 1
            residual(W_OUT1)
            norm(3)
            mlp(1, W_UP1)
            norm(4, last=True)

        @block.tensor
        def _(pe):
            PASSES = ((hT_hi, w_hi), (hT_hi, w_lo), (hT_lo, w_hi))
            turns = [0]

            def turn(source, ready):
                for t in range(NT):
                    for j in range(KT):
                        if j % 4 == 0:
                            ready(t, j // 4)
                        ins = pe.transpose(ps[:, 2 * t + j // 4, 128 * (j % 4):128 * (j % 4) + 128], source(t, j), ident)
                        if j % 4 == 3:
                            ins.then_inc(turned, 1)
                turns[0] += 1

            def tokens_tile(slot, first, last, k0, nk, width, banks, before=None, offset=0, inc=1):
                for t in range(NT):
                    if before:
                        before(t)
                    for k in range(nk):
                        for n, (h, w) in enumerate(PASSES):
                            ins = pe.matmul(ps[:, banks[t], 0:width], h[:, k0 + k, t * 128:(t + 1) * 128],
                                            w[:, slot, k * width:(k + 1) * width],
                                            start=first and k == 0 and n == 0,
                                            stop=last and k == nk - 1 and n == 2)
                    ins.then_inc(mm_done, inc)

            def channels(slot, s, bank, pitch=256):
                for k in range(KT):
                    for n, (h, w) in enumerate(PASSES):
                        ins = pe.matmul(bank, w[:, slot, k * pitch + 128 * s:k * pitch + 128 * s + 128], h[:, k:k + 1, :],
                                        start=k == 0 and n == 0, stop=k == KT - 1 and n == 2)
                ins.then_inc(mm_done, 2)

            def tok_ready(t):
                pe.wait_ge(turn_lo, 8 * (turns[0] - 1) + 2 * t + 2)

            def project_out(n0):
                for c in range(2):
                    for half in range(2):
                        n = n0 + 2 * c + half
                        pe.wait_ge(w_lo_ready, n + 1)
                        tokens_tile(n % 2, half == 0, half == 1, 4 * half, 4, 512, [4 * c + t for t in range(NT)],
                                    tok_ready if c == 0 and half == 0 else None)

            def attention(kind, h, g):
                if kind == "C":
                    for s in range(2):
                        if s == 1 and g > 8:
                            pe.wait_ge(o_ready, 4 * g)
                        for src, bank in ((q_tok, 4 + 2 * s), (k_tok, 5 + 2 * s)):
                            for t in range(NT):
                                ins = pe.transpose(ps[0:96, bank, t * 128:(t + 1) * 128],
                                                   src[:, t, (2 * h + s) * 96:(2 * h + s + 1) * 96], ident)
                            ins.then_inc(qk_turned, 1)
                else:
                    for s in range(2):
                        pe.wait_ge(rope_ready, 2 * g + s + 1)
                        for t in range(NT):
                            ins = pe.transpose(ps[:, 4 + s, t * 128:(t + 1) * 128], stage[:, s, t * 128:(t + 1) * 128], ident)
                        ins.then_inc(qk_turned, 1)
                for k in range(10):
                    if k < 8:
                        i, m, w = unit(k)
                        if kind == "C":
                            pe.wait_ge(qT_ready, 8 + 2 * (g - 8) + m + 1)
                            pe.wait_ge(kT_ready, 8 + 2 * (g - 8) + m + 1)
                            q, kk = qk[0:96, m, i * 128:(i + 1) * 128], qk[0:96, 2 + m, 0:w]
                        else:
                            if k == 0:
                                pe.wait_ge(qT_ready, g + 1)
                                pe.wait_ge(kT_ready, g + 1)
                            q, kk = qk[64 * m:64 * m + 64, 0, i * 128:(i + 1) * 128], qk[64 * m:64 * m + 64, 2, 0:w]
                        if k >= 2:
                            pe.wait_ge(exp_ready, 8 * g + k - 1)
                        pe.matmul(ps[:, m, 0:w], q, kk, start=True, stop=False)
                        if kind == "B":
                            ins = pe.matmul(ps[:, m, 0:w], ident_bf[:, :], mask_bf[:, M_END - w:M_END], start=False, stop=True)
                        else:
                            ins = pe.matmul(ps[:, m, w - 128:w], ident_bf[:, :], mask_bf[:, M_CAUSAL:M_CAUSAL + 128],
                                            start=False, stop=True)
                        ins.then_inc(scores_ready, 1)
                    if 1 <= k <= 8:
                        i, m, w = unit(k - 1)
                        if kind == "B":
                            pe.wait_ge(mult_ready, 8 * (g - 4) + k)
                        else:
                            pe.wait_ge(exp_ready, 8 * g + k)
                        if k >= 3:
                            pe.wait_ge(pT_copied, 8 * g + k - 2)
                        for b in range(i + 1):
                            ins = pe.transpose(ps[:, 2 + m, b * 128:(b + 1) * 128], probs[:, m, b * 128:(b + 1) * 128], ident)
                        ins.then_inc(pT_ready, 1)
                    if k >= 2:
                        i, m, w = unit(k - 2)
                        pe.wait_ge(pT_copied, 8 * g + k - 1)
                        if i >= 2 and m == 0:
                            pe.wait_ge(o_ready, 4 * g + i - 1)
                        for b in range(i + 1):
                            if kind == "A":
                                v, o = y[:, b, ds(h * 128 + 1024, 128)], ps[:, 6 + i % 2, 128 * m:128 * m + 128]
                            elif kind == "B":
                                v, o = y[:, b, ds(h * 128 + (2560 + 64 * m), 64)], ps[:, 6 + i % 2, 64 * m:64 * m + 64]
                            else:
                                c0 = 192 * (2 * h + m) + 64
                                v, o = kv_tok[:, b, c0:c0 + 128], ps[:, 6 + i % 2, 128 * m:128 * m + 128]
                            ins = pe.matmul(o, probsT[:, m, b * 128:(b + 1) * 128], v, start=b == 0, stop=b == i)
                        ins.then_inc(pv_ready, 1)

            def mlp(l, n0):
                pe.wait_ge(turn_lo, 8 * turns[0])
                with pe.Fori(0, FT // 2) as i:
                    for half in range(2):
                        pe.wait_ge(w_lo_ready, 2 * i + (n0 + half + 1))
                        for s in range(2):
                            if half:
                                pe.wait_ge(val_bank_free[l], 2 * i + s + 1)
                            channels(half, s, ps[:, 2 * half + s:2 * half + s + 1, :])
                    pe.wait_ge(conv_done[l], 2 * i + 2)
                n1 = n0 + FT

                def down_tile(slot, parts, last, wait_w, wait_lo):
                    pe.wait_ge(w_lo_ready, wait_w)
                    pe.wait_ge(act_lo[l], wait_lo)
                    for c, units, first, stop, incs in parts:
                        for t in range(NT):
                            for u in units:
                                for n, (h, w) in enumerate(PASSES):
                                    ins = pe.matmul(ps[:, 4 * c + t, :], h[:, 4 * slot + u, t * 128:(t + 1) * 128],
                                                    w[:, slot, u * 512:(u + 1) * 512],
                                                    start=first and u == units[0] and n == 0,
                                                    stop=stop and u == units[-1] and n == 2)
                            if incs[t]:
                                ins.then_inc(mm_done, incs[t])

                every, four = (1, 1, 1, 1), (0, 1, 2, 3)
                down_tile(0, [(0, four, True, False, every)], False, n1 + 1, 4)
                with pe.Fori(0, 2) as i:
                    for b in range(2):
                        down_tile(1 - b, [(0, four, False, False, every)], False,
                                  2 * i + (n1 + b + 2), 8 * i + 4 * (b + 2))
                down_tile(1, [(0, (0, 1), False, True, (0, 0, 0, 2)), (1, (2, 3), True, False, (0, 0, 0, 2))],
                          False, n1 + 6, 24)
                with pe.Fori(0, 2) as i:
                    for b in range(2):
                        down_tile(b, [(1, four, False, False, every)], False,
                                  2 * i + (n1 + b + 7), 8 * i + 4 * (b + 7))
                down_tile(0, [(1, four, False, True, every)], True, n1 + 11, 44)

            pe.wait_ge(cst_loaded, 16)
            turn(lambda t, j: xn[:, t % 2, j * 128:(j + 1) * 128],
                 lambda t, g: pe.wait_ge(src_ready, t + 1))
            pe.wait_ge(turn_lo, 8)
            with pe.Fori(0, 3) as i:
                for s in range(2):
                    for half in range(2):
                        pe.wait_ge(w_lo_ready, 4 * i + (2 * s + half + 1))
                        tokens_tile(half, half == 0, half == 1, 4 * half, 4, 512, [4 * s + t for t in range(NT)],
                                    (lambda t: pe.wait_ge(in_bank_free, 8 * i + (4 * s + t + 1))) if half == 0 else None)
            pe.wait_ge(masks_ready, 1)
            pe.wait_ge(in_bank_free, 8 + 24)
            with pe.Fori(0, 4) as h:
                attention("A", h, h)
            with pe.Fori(0, 4) as h:
                attention("B", h, h + 4)

            def mixed_ready(t, g):
                if g == 0:
                    pe.wait_ge(src_ready, 4 + t + 1)
            turn(lambda t, j: xn[:, t % 2, j * 128:(j + 1) * 128] if j < 4 else y[:, t, 1024 + j * 128:1152 + j * 128],
                 mixed_ready)
            project_out(W_OUT0)
            turn(lambda t, j: xn[:, t % 2, j * 128:(j + 1) * 128],
                 lambda t, g: pe.wait_ge(src_ready, 8 + t + 1))
            mlp(0, W_UP0)
            turn(lambda t, j: xn[:, t % 2, j * 128:(j + 1) * 128],
                 lambda t, g: pe.wait_ge(src_ready, 12 + t + 1))
            pe.wait_ge(turn_lo, 8 * turns[0])
            with pe.Fori(0, 2) as i:
                for half in range(2):
                    pe.wait_ge(w_lo_ready, 2 * i + (W_DQK + half + 1))
                    for s in range(2):
                        channels((W_DQK + half) % 2, s, ps[:, ds(4 * i + (2 * half + s), 1), :])
            for c in range(5):
                n = W_C + c // 2
                pe.wait_ge(w_lo_ready, n + 1)
                pe.wait_ge(dT_copied, c + 1)
                channels(n % 2, c % 2, ps[:, c:c + 1, :], 160 if c == 4 else 256)
            pe.wait_ge(dT_copied, 6)
            n = W_C + 2
            for t in range(NT):
                for k in range(KT):
                    for m, (h, w) in enumerate(PASSES):
                        ins = pe.matmul(ps[:, 5, 32 * t:32 * t + 32], h[:, k, t * 128:(t + 1) * 128],
                                        w[:, n % 2, k * 160 + 128:k * 160 + 160],
                                        start=k == 0 and m == 0, stop=k == KT - 1 and m == 2)
            ins.then_inc(mm_done, 2)
            pe.wait_ge(sq_ready, 5)
            pe.wait_ge(dT_copied, 7)
            pe.wait_ge(ones_ready, 1)
            for which, cs in ((0, (0, 1, 2)), (1, (3, 4))):
                for t in range(NT):
                    for c in cs:
                        sq = qk[:, c, t * 128:(t + 1) * 128] if c < 4 else tmp[:, 0, t * 128:(t + 1) * 128]
                        ins = pe.matmul(ps[:, 6, 4 * which + t:4 * which + t + 1], sq, ones[:, :],
                                        start=c == cs[0], stop=c == cs[-1])
            ins.then_inc(c_stats, 1)
            for half in range(2):
                n = W_DV + half
                pe.wait_ge(w_lo_ready, n + 1)
                if half == 0:
                    pe.wait_ge(c_copied, 5)
                tokens_tile(n % 2, half == 0, half == 1, 4 * half, 4, 512, range(NT))
            pe.wait_ge(w_lo_ready, W_UQ + 1)
            pe.wait_ge(c_lo, 5)
            tokens_tile(W_UQ % 2, True, True, 0, 3, 384, [4, 5, 6, 7])
            pe.wait_ge(w_lo_ready, W_UKV + 1)
            for t in range(NT):
                pe.wait_ge(q_scaled, t + 1)
                for c in range(2):
                    for k in range(2):
                        for m, (h, w) in enumerate(PASSES):
                            ins = pe.matmul(ps[:, 4 * c + t, 0:384], h[:, 3 + k, t * 128:(t + 1) * 128],
                                            w[:, W_UKV % 2, k * 768 + 384 * c:k * 768 + 384 * c + 384],
                                            start=k == 0 and m == 0, stop=k == 1 and m == 2)
                ins.then_inc(mm_done, 1)
            pe.wait_ge(kv_scaled, NT)
            with pe.Fori(0, 2) as p:
                for k in range(11):
                    if k < 8:
                        i, m, w = unit(k)
                        bank = (0, 1, 4, 5)[k % 4]
                        if k < 2:
                            pe.wait_ge(d_q, 2 * p + m + 1)
                        if k >= 4:
                            pe.wait_ge(d_arg, 8 * p + k - 3)
                        pe.matmul(ps[:, bank:bank + 1, 0:w], qk[:, m, i * 128:(i + 1) * 128],
                                  dT[:, ds(2 * p + (4 + m), 1), 0:w], start=True, stop=False)
                        pe.matmul(ps[:, bank, w - 128:w], ident_bf[:, :], mask_bf[:, M_STRICT:M_STRICT + 128],
                                  start=False, stop=True).then_inc(d_scores, 1)
                    if 2 <= k < 10:
                        i, m, w = unit(k - 2)
                        pe.wait_ge(d_exp, 8 * p + k - 1)
                        if k >= 4:
                            pe.wait_ge(d_copied, 8 * p + k - 3)
                        for b in range(i + 1):
                            ins = pe.transpose(ps[:, 2 + m, b * 128:(b + 1) * 128], probs[:, m, b * 128:(b + 1) * 128], ident)
                        ins.then_inc(d_turned, 1)
                    if k >= 3:
                        i, m, w = unit(k - 3)
                        pe.wait_ge(d_copied, 8 * p + k - 2)
                        if i >= 2 and m == 0:
                            pe.wait_ge(d_out, 4 * p + i - 1)
                        for b in range(i + 1):
                            ins = pe.matmul(ps[:, 6 + i % 2, 128 * m:128 * m + 128], probsT[:, m, b * 128:(b + 1) * 128],
                                            dv[:, b, ds(256 * p + 128 * m, 128)], start=b == 0, stop=b == i)
                        ins.then_inc(d_pv, 1)
            pe.wait_ge(c_roped, 3)
            pe.wait_ge(d_out, 8)
            for g in (8, 9):
                attention("C", g - 8, g)
            pe.wait_ge(o_ready, 40)
            turn(lambda t, j: o_C[:, t, j * 128:(j + 1) * 128] if j < 4 else o_D[:, t, (j - 4) * 128:(j - 3) * 128],
                 lambda t, g: None)
            project_out(W_OUT1)
            turn(lambda t, j: xn[:, t % 2, j * 128:(j + 1) * 128],
                 lambda t, g: pe.wait_ge(src_ready, 16 + t + 1))
            mlp(1, W_UP1)


def _constants():
    import numpy as np
    p = np.arange(128)
    consts = np.zeros((128, C_END), np.float32)
    consts[:, C_ID:C_ID + 128] = np.eye(128)
    masks = np.zeros((128, M_END), np.float32)
    q, k = p[:, None], p[None, :]
    masks[:, M_CAUSAL:M_CAUSAL + 128] = np.where(k <= q, 0.0, -1e30)
    masks[:, M_STRICT:M_STRICT + 128] = np.where(k < q, 0.0, -1e30)
    for s in range(4):
        d = q - k + 128 * (3 - s)
        seen = ((d >= 0) & (d <= 128)).astype(np.float32) + ((d >= 0) & (d % 4 == 0)) + ((d >= 0) & (d % 16 == 0))
        consts[:, C_CMUL + 128 * s:C_CMUL + 128 * s + 128] = seen
        masks[:, M_DIL + 128 * s:M_DIL + 128 * s + 128] = np.where(seen > 0, 0.0, -1e30)
    for dim, c0, s0 in ((64, C_COS64, C_SIN64), (32, C_COS32, C_SIN32)):
        inv = (np.float32(10000.0) ** (-np.arange(0, dim, 2, dtype=np.float32) / np.float32(dim))).astype(np.float32)
        ang = np.arange(SEQ, dtype=np.float32)[:, None] * inv[None, :]
        cos, sin = np.cos(ang).astype(np.float32), np.sin(ang).astype(np.float32)
        for base, tab in ((c0, np.concatenate([cos, cos], 1)), (s0, np.concatenate([-sin, sin], 1))):
            consts[:, base:base + NT * dim] = tab.reshape(NT, 128, dim).transpose(1, 0, 2).reshape(128, -1)
    return consts, masks


def _weight_tiles(ab_w_in, ab_w_out, cd_w_in, c_w_uq, c_w_ukv, cd_w_out, ffn_w_up, ffn_w_down):
    import numpy as np

    def tiles(a):
        a = a.transpose(1, 0, 2).reshape(128, -1)
        out = np.zeros((1, 128, UNIT), np.float32)
        out[0, :, :a.shape[1]] = a
        return out

    def tokens(w):
        w = w.reshape(KT, 128, -1)
        return [tiles(w[4 * h:4 * h + 4, :, c:c + 512]) for c in range(0, w.shape[2], 512) for h in range(2)]

    def channels(w, width=256):
        w = w.reshape(KT, 128, -1)
        return [tiles(w[:, :, c:c + width]) for c in range(0, w.shape[2], width)]

    def mlp(l):
        gate, val = channels(ffn_w_up[l][:, :DFF]), channels(ffn_w_up[l][:, DFF:])
        up = [t for pair in zip(gate, val) for t in pair]
        units = [ffn_w_down[l].reshape(FT, 128, DM)[k, :, 512 * c:512 * c + 512] for c in range(2) for k in range(FT)]
        return up + [tiles(np.stack(units[u:u + 4])) for u in range(0, 2 * FT, 4)]

    cd = cd_w_in[0]
    all_tiles = tokens(ab_w_in[0]) + tokens(ab_w_out[0]) + mlp(0)
    all_tiles += channels(cd[:, 672:1696]) + channels(cd[:, 0:512]) + channels(cd[:, 512:672], 160)
    all_tiles += tokens(cd[:, 1696:2208])
    all_tiles += [tiles(c_w_uq[0].reshape(3, 128, 384)), tiles(c_w_ukv[0].reshape(2, 128, 768))]
    all_tiles += tokens(cd_w_out[0]) + mlp(1)
    out = np.concatenate(all_tiles)
    assert out.shape == (W_ALL, 128, UNIT)
    return out


def kernel(x, mix_norm_g, ffn_norm_g, final_norm_g, ab_w_in, a_lambda_q1, a_lambda_k1, a_lambda_q2, a_lambda_k2,
           a_subln_g, ab_w_out, cd_w_in, c_q_norm_g, c_w_uq, c_kv_norm_g, c_w_ukv, cd_w_out, ffn_w_up, ffn_conv_w,
           ffn_conv_b, ffn_w_down):
    import numpy as np
    import concourse.bacc as bacc
    from concourse.bass_utils import run_bass_kernel_spmd

    consts, masks = _constants()
    a = np.asarray
    conv = np.concatenate([a(ffn_conv_w), a(ffn_conv_b)[:, None, :]], 1)
    conv = conv.reshape(2, 4, FT, 128).transpose(3, 0, 2, 1).reshape(128, -1)
    rows = np.concatenate([a(a_lambda_q1)[0], a(a_lambda_k1)[0], a(a_lambda_q2)[0], a(a_lambda_k2)[0], a(a_subln_g)[0]])
    latent = np.concatenate([a(c_q_norm_g)[0], a(c_kv_norm_g)[0]]).reshape(5, 128).T
    vectors = np.concatenate([np.broadcast_to(rows, (128, 384)), conv, latent], 1)
    gains = np.stack([a(mix_norm_g)[0], a(ffn_norm_g)[0], a(mix_norm_g)[1], a(ffn_norm_g)[1], a(final_norm_g)])
    arrays = {
        "x_in": a(x),
        "weights": _weight_tiles(*(a(w) for w in (ab_w_in, ab_w_out, cd_w_in, c_w_uq, c_w_ukv, cd_w_out,
                                                   ffn_w_up, ffn_w_down))),
        "consts": consts, "masks": masks, "vectors": vectors,
        "gains": np.broadcast_to(gains, (128, 5, DM)),
    }
    arrays = {name: np.ascontiguousarray(v) for name, v in arrays.items()}
    nc = bacc.Bacc("TRN2", target_bir_lowering=False, num_devices=1)
    args = [nc.dram_tensor(name, v.shape, mybir.dt.from_np(v.dtype), kind="ExternalInput").ap()
            for name, v in arrays.items()]
    out = nc.dram_tensor("out", (1, SEQ, DM), mybir.dt.float32, kind="ExternalOutput").ap()
    trunk_program(nc, *args, out)
    r = run_bass_kernel_spmd(nc, [arrays], core_ids=[0])
    return r.results[0]["out"]
```

```python
import math
from contextlib import ExitStack

import concourse.bass as bass
from concourse import mybir

SEQ, DM, DFF = 512, 1024, 2816
NT = SEQ // 128
KT = DM // 128
FT = DFF // 128
UNIT = 2048
EPS = 1e-6
LAM_INIT = 0.8 - 0.6 * math.exp(-0.3 * 0)

W_IN0 = 0
W_OUT0 = W_IN0 + 16
W_UP0 = W_OUT0 + 4
W_DN0 = W_UP0 + FT
W_DQK = W_DN0 + FT // 2
W_C = W_DQK + 4
W_DV = W_C + 3
W_UQ = W_DV + 2
W_UKV = W_UQ + 1
W_OUT1 = W_UKV + 1
W_UP1 = W_OUT1 + 4
W_DN1 = W_UP1 + FT
W_ALL = W_DN1 + FT // 2

C_ID, C_CMUL, C_COS64, C_SIN64, C_COS32, C_SIN32, C_END = 0, 128, 640, 896, 1152, 1280, 1408
M_CAUSAL, M_STRICT, M_DIL, M_END = 0, 128, 256, 768
V_LAM, V_SUB, V_CONV, V_CG, V_END = 0, 256, 384, 384 + 2 * FT * 4, 384 + 2 * FT * 4 + 5


def trunk_program(nc, x_in, weights, consts, masks, vectors, gains, out):
    f32, f32r, bf16 = mybir.dt.float32, mybir.dt.float32r, mybir.dt.bfloat16
    ACT, ALU, AX = mybir.ActivationFunctionType, mybir.AluOpType, mybir.AxisListType
    ds = bass.ds
    n_tiles = W_ALL

    with ExitStack() as ctx:
        def sb(name, shape, dt=f32):
            return ctx.enter_context(nc.sbuf_tensor(name, shape, dt))

        def sem(name):
            return ctx.enter_context(nc.semaphore(name))

        x = sb("x", [128, NT, DM])
        hT_hi = sb("hT_hi", [128, KT, SEQ], f32r)
        hT_lo = sb("hT_lo", [128, KT, SEQ], f32r)
        w_raw = sb("w_raw", [128, 2, UNIT])
        w_hi = sb("w_hi", [128, 2, UNIT], f32r)
        w_lo = sb("w_lo", [128, 2, UNIT], f32r)
        region_at = nc.sbuf_base
        region = sb("region", [128, 17024])
        y = region[:, 0:12288].rearrange("p (t n) -> p t n", t=NT)
        act = region[:, 0:FT * SEQ].rearrange("p (j n) -> p j n", j=FT)
        final = region[:, 0:4096].rearrange("p (t n) -> p t n", t=NT)
        dT = region[:, 0:4096].rearrange("p (c n) -> p c n", c=8)
        cT = region[:, 4096:6656].rearrange("p (c n) -> p c n", c=5)
        dv = region[:, 6656:8704].rearrange("p (t n) -> p t n", t=NT)
        q_tok = region[:, 8704:10240].rearrange("p (t n) -> p t n", t=NT)
        kv_tok = region[:, 10240:13312].rearrange("p (t n) -> p t n", t=NT)
        k_tok = region[:, 13312:14848].rearrange("p (t n) -> p t n", t=NT)
        kr = region[:, 14848:14976].rearrange("p (t n) -> p t n", t=NT)
        o_D = region[:, 14976:17024].rearrange("p (t n) -> p t n", t=NT)
        o_C = region[:, 4096:6144].rearrange("p (t n) -> p t n", t=NT)
        c_tmp = region[:, 4096:5120].rearrange("p (a n) -> p a n", a=2)

        xn = sb("xn", [128, 2, DM])
        probs = xn[:, 0, :].rearrange("p (a n) -> p a n", a=2)
        probsT = xn[:, 1, :].rearrange("p (a n) -> p a n", a=2)
        stage_mem = sb("stage", [128, 1024])
        stage = stage_mem[:, :].rearrange("p (t n) -> p t n", t=NT)
        d_sums = stage_mem[:, :].rearrange("p (a n) -> p a n", a=2)
        qk = sb("qk", [128, 4, SEQ])
        tmp = sb("tmp", [128, 2, SEQ])
        gain = sb("gain", [128, DM])
        cst = sb("cst", [128, C_END])
        vec = sb("vec", [128, V_END])
        mask_bf = sb("mask_bf", [128, M_END], bf16)
        ident_bf = sb("ident_bf", [128, 128], bf16)
        ones = sb("ones", [128, 1])
        sub_gain = sb("sub_gain", [128, 128])
        neg_lam = sb("neg_lam", [128, 1])
        lam_s = sb("lam_s", [128, 4])
        ss = sb("ss", [128, 16])
        var = sb("var", [128, 16])
        sd = sb("sd", [128, 16])
        rstd = sb("rstd", [128, 16])
        rs_a = sb("rs_a", [128, 16])
        neg_max = sb("neg_max", [128, 8])
        den = sb("den", [128, 8])
        rden = sb("rden", [128, 8])
        rden1 = sb("rden1", [128, 4])
        o_tmp = sb("o_tmp", [128, 128])

        ident = cst[:, C_ID:C_ID + 128]
        cmul = cst[:, C_CMUL:C_CMUL + 512]
        cos64 = cst[:, C_COS64:C_COS64 + 256].rearrange("p (t d) -> p t d", t=NT)
        sin64 = cst[:, C_SIN64:C_SIN64 + 256].rearrange("p (t d) -> p t d", t=NT)
        cos32 = cst[:, C_COS32:C_COS32 + 128].rearrange("p (t d) -> p t d", t=NT)
        sin32 = cst[:, C_SIN32:C_SIN32 + 128].rearrange("p (t d) -> p t d", t=NT)
        first_hi = nc.alloc_sbuf_tensor_at("first_hi", [128, 4, SEQ], f32r, offset=region_at + 4 * 12288)
        first_lo = nc.alloc_sbuf_tensor_at("first_lo", [128, 4, SEQ], f32r, offset=region_at + 4 * (12288 + 4 * SEQ))
        masks_f32 = region[:, 12288:12288 + M_END]

        ps = ctx.enter_context(nc.psum_tensor("ps", [128, 8, 512], f32))

        x_loaded = [sem(f"x_loaded{t}") for t in range(NT)]
        ident_loaded, cst_loaded, vec_loaded, mask_loaded = sem("ident_loaded"), sem("cst_loaded"), sem("vec_loaded"), sem("mask_loaded")
        gain_loaded, out_stored = sem("gain_loaded"), sem("out_stored")
        w_loaded = [sem("w_loaded0"), sem("w_loaded1")]
        w_hi_ready, w_lo_ready, mm_done = sem("w_hi_ready"), sem("w_lo_ready"), sem("mm_done")
        masks_ready, ones_ready = sem("masks_ready"), sem("ones_ready")
        lam_dots, lam_exps = sem("lam_dots"), sem("lam_exps")
        x_done = sem("x_done")
        ss_ready, var_ready, sd_ready = sem("ss_ready"), sem("var_ready"), sem("sd_ready")
        src_ready = sem("src_ready")
        turned, turn_hi, turn_lo = sem("turned"), sem("turn_hi"), sem("turn_lo")
        part_copied = sem("part_copied")
        rope_ready, qk_turned, qT_ready, kT_ready = sem("rope_ready"), sem("qk_turned"), sem("qT_ready"), sem("kT_ready")
        scores_ready, max_ready, exp_ready, mult_ready = sem("scores_ready"), sem("max_ready"), sem("exp_ready"), sem("mult_ready")
        pT_ready, pT_copied, pv_ready, o_ready = sem("pT_ready"), sem("pT_copied"), sem("pv_ready"), sem("o_ready")
        conv_started, conv_done, silu_ready = [[sem(f"{n}{l}") for l in range(2)] for n in
                                               ("conv_started", "conv_done", "silu_ready")]
        val_bank_free = [sem(f"val_bank_free{l}") for l in range(2)]
        act_hi, act_lo = [[sem(f"{n}{l}") for l in range(2)] for n in ("act_hi", "act_lo")]
        dT_copied, c_copied, sq_ready, kr_copied = sem("dT_copied"), sem("c_copied"), sem("sq_ready"), sem("kr_copied")
        c_stats, dv_copied, c_hi, c_lo, q_scaled, kv_scaled, c_roped = (
            sem(n) for n in ("c_stats", "dv_copied", "c_hi", "c_lo", "q_scaled", "kv_scaled", "c_roped"))
        d_q, d_scores, d_soft, d_sp, d_arg, d_exp, d_turned, d_copied, d_pv, d_out = (
            sem(n) for n in ("d_q", "d_scores", "d_soft", "d_sp", "d_arg", "d_exp", "d_turned", "d_copied", "d_pv", "d_out"))
        act_own, dve_own, pool_own = sem("act_own"), sem("dve_own"), sem("pool_own")

        block = ctx.enter_context(nc.Block())

        class Own:

            def __init__(self, eng, steps):
                self.eng, self.steps, self.n, self.shift = eng, steps, 0, 0

            def mark(self, ins):
                ins.then_inc(self.steps, 1)
                self.n += 1
                return self.n

            def wait(self, value):
                self.eng.wait_ge(self.steps, self.shift + value)

            def link(self, ins):
                self.wait(self.mark(ins))

            def loop(self, i, turns, marks):
                start, self.shift = self.n, i * marks

                def end():
                    assert self.n - start == marks, self.n - start
                    self.n, self.shift = start + turns * marks, 0
                return end

        def load_x(eng, t):
            eng.dma_start(x[:, t, :], x_in[0, t * 128:(t + 1) * 128, :]).then_inc(x_loaded[t], 16)

        def norm_base(k):
            return 4 * (k - 1)

        def unit(k):
            return k // 2, k % 2, 128 * (k // 2 + 1)

        X_STEPS, A_FREE, B_FREE = (4, 6, 7, 8), 5, 8

        FILL = {0: (0, 1), 1: (2, 3), 2: (4,), 3: (5,), 4: (6,), 5: (7,)}

        @block.sync
        def _(sp):
            def load(m, slot):
                sp.dma_start(w_raw[:, slot, :], weights[m, :, :]).then_inc(w_loaded[slot], 16)

            load(0, 0)
            sp.dma_start(cst[:, 0:C_CMUL], consts[:, 0:C_CMUL]).then_inc(ident_loaded, 16)
            load(1, 1)
            for t in range(1, NT):
                load_x(sp, t)
            sp.dma_start(cst[:, C_CMUL:], consts[:, C_CMUL:]).then_inc(cst_loaded, 16)
            sp.dma_start(vec[:, :], vectors).then_inc(vec_loaded, 16)
            sp.dma_start(masks_f32, masks).then_inc(mask_loaded, 16)
            with sp.Fori(1, n_tiles // 2) as j:
                for slot in range(2):
                    sp.wait_ge(w_lo_ready, 2 * j + slot - 1)
                    sp.dma_start(w_raw[:, slot, :].unsqueeze(1),
                                 weights[ds(2 * j + slot, 1), :, :].rearrange("m p n -> p m n"))\
                      .then_inc(w_loaded[slot], 16)
            if n_tiles % 2:
                sp.wait_ge(w_lo_ready, n_tiles - 2)
                load(n_tiles - 1, (n_tiles - 1) % 2)
            for t in range(NT):
                sp.wait_ge(src_ready, 5 * NT + t + 1)
                sp.dma_start(out[0, t * 128:(t + 1) * 128, :], final[:, t, :]).then_inc(out_stored, 16)
            sp.wait_ge(out_stored, 16 * NT)

        @block.gpsimd
        def _(pool):
            own = Own(pool, pool_own)

            def split_lo(m, slot):
                pool.wait_ge(w_hi_ready, m + 1)
                pool.tensor_tensor(w_lo[:, slot, :], w_raw[:, slot, :], w_hi[:, slot, :].bitcast(f32),
                                   ALU.subtract).then_inc(w_lo_ready, 1)

            def split_range(a, b):
                b = min(b, n_tiles)
                if a >= b:
                    return
                if a % 2:
                    split_lo(a, 1)
                    a += 1
                if b - a >= 2:
                    with pool.Fori(0, (b - a) // 2) as j:
                        for slot in range(2):
                            split_lo(2 * j + (a + slot), slot)
                if (b - a) % 2:
                    split_lo(b - 1, 0)

            def table(tab, shape):
                return tab.unsqueeze(2).broadcast_to(shape)

            def rope_tile(g, t, parts=None):
                pool.wait_ge(part_copied, parts or 8 * g + (t + 5))
                src = y[:, t, ds(384 * g, 256)].rearrange("p (m d) -> p m d", m=4)
                dst = stage[:, t, :].rearrange("p (m d) -> p m d", m=4)
                t1, t2 = (tmp[:, j, 256 * (t % 2):256 * (t % 2) + 256].rearrange("p (m d) -> p m d", m=4) for j in range(2))
                cos, sin = (tab[:, t, :].unsqueeze(1).broadcast_to([128, 4, 64]) for tab in (cos64, sin64))
                own.mark(pool.tensor_tensor(t1, src, cos, ALU.mult))
                own.mark(pool.tensor_tensor(t2[:, :, 0:32], src[:, :, 32:64], sin[:, :, 0:32], ALU.mult))
                own.link(pool.tensor_tensor(t2[:, :, 32:64], src[:, :, 0:32], sin[:, :, 32:64], ALU.mult))
                pool.tensor_tensor(dst, t1, t2, ALU.add).then_inc(rope_ready, 1)

            split_lo(0, 0)
            split_lo(1, 1)
            pool.wait_ge(cst_loaded, 16)
            for t in range(NT):
                if t >= 2:
                    pool.wait_ge(rope_ready, t - 1)
                rope_tile(0, t, 2 * t + 2)
            split_lo(2, 0)
            split_lo(3, 1)
            with pool.Fori(1, 8) as g:
                end = own.loop(g - 1, 7, 12)
                pool.wait_ge(qk_turned, 2 * g)
                for t in range(NT):
                    pool.wait_ge(rope_ready, 4 * g + t - 1)
                    rope_tile(g, t)
                    if t == 1:
                        split_lo(2 * g + 2, 0)
                split_lo(2 * g + 3, 1)
                end()
            split_range(W_OUT0 + 2, W_OUT1 + 2)
            pool.wait_ge(kr_copied, 1)
            pool.wait_ge(c_lo, 5)
            kr4 = kr[:, :, :].unsqueeze(2)
            t1 = c_tmp[:, 0, 0:128].rearrange("p (t d) -> p t d", t=NT).unsqueeze(2)
            t2 = c_tmp[:, 1, 0:128].rearrange("p (t d) -> p t d", t=NT).unsqueeze(2)
            c4, s4 = cos32.unsqueeze(2), sin32.unsqueeze(2)
            own.mark(pool.tensor_tensor(t1, kr4, c4, ALU.mult))
            own.mark(pool.tensor_tensor(t2[:, :, :, 0:16], kr4[:, :, :, 16:], s4[:, :, :, 0:16], ALU.mult))
            own.link(pool.tensor_tensor(t2[:, :, :, 16:], kr4[:, :, :, 0:16], s4[:, :, :, 16:], ALU.mult))
            own.link(pool.tensor_tensor(kr4, t1, t2, ALU.add))
            pool.wait_ge(q_scaled, NT)
            q4 = q_tok.rearrange("p t (h d) -> p t h d", h=4)[:, :, :, 64:96]
            t1 = c_tmp[:, 0, :].rearrange("p (t h d) -> p t h d", t=NT, h=4)
            t2 = c_tmp[:, 1, :].rearrange("p (t h d) -> p t h d", t=NT, h=4)
            c4, s4 = table(cos32, [128, NT, 4, 32]), table(sin32, [128, NT, 4, 32])
            own.mark(pool.tensor_tensor(t1, q4, c4, ALU.mult))
            own.mark(pool.tensor_tensor(t2[:, :, :, 0:16], q4[:, :, :, 16:], s4[:, :, :, 0:16], ALU.mult))
            own.link(pool.tensor_tensor(t2[:, :, :, 16:], q4[:, :, :, 0:16], s4[:, :, :, 16:], ALU.mult))
            pool.tensor_tensor(q4, t1, t2, ALU.add).then_inc(c_roped, 1)
            pool.wait_ge(kv_scaled, NT)
            k4 = k_tok.rearrange("p t (h d) -> p t h d", h=4)
            pool.tensor_copy(k4[:, :, :, 0:64],
                             kv_tok.rearrange("p t (h d) -> p t h d", h=4)[:, :, :, 0:64]).then_inc(c_roped, 1)
            pool.tensor_copy(k4[:, :, :, 64:96],
                             kr.unsqueeze(2).broadcast_to([128, NT, 4, 32])).then_inc(c_roped, 1)
            split_range(W_OUT1 + 2, n_tiles)

        @block.scalar
        def _(sc):
            own = Own(sc, act_own)

            def split_hi(slot, fill):
                sc.wait_ge(w_loaded[slot], 16 * fill)
                sc.activation(w_hi[:, slot, :], w_raw[:, slot, :], ACT.Copy).then_inc(w_hi_ready, 1)

            def split_after(n):
                if n + 2 < n_tiles:
                    sc.wait_ge(mm_done, 4 * (n + 1))
                    split_hi(n % 2, n // 2 + 2)

            def split_after_in_loop(i, n0):
                sc.wait_ge(mm_done, 8 * i + 4 * (n0 + 1))
                split_hi(n0 % 2, i + (n0 // 2 + 2))

            gains_asked = [0]

            def load_gain():
                g = gains_asked[0]
                sc.dma_start(gain[:, :], gains[:, g, :]).then_inc(gain_loaded, 16)
                gains_asked[0] += 1

            roots = [0]

            def root(a, b):
                sc.wait_ge(var_ready, roots[0] + 1)
                roots[0] += 1
                sc.activation(sd[:, a:b], var[:, a:b], ACT.Sqrt).then_inc(sd_ready, 1)

            def square(k, t):
                if k == 0:
                    sc.wait_ge(x_loaded[t], 16)
                else:
                    sc.wait_ge(x_done, norm_base(k) + t + 1)
                if t >= 1:
                    sc.wait_ge(ss_ready, 4 * k + t)
                sc.activation(tmp[:, :, :].rearrange("p a n -> p (a n)"), x[:, t, :], ACT.Square,
                              accum_out=ss[:, t:t + 1]).then_inc(ss_ready, 1)

            turns = [0]

            def turn_tile(t):
                for g in range(2):
                    b = 2 * t + g
                    sc.wait_ge(turned, 8 * turns[0] + b + 1)
                    sc.activation(hT_hi[:, 4 * g:4 * g + 4, t * 128:(t + 1) * 128],
                                  ps[:, b, :].rearrange("p (j n) -> p j n", j=4), ACT.Copy).then_inc(turn_hi, 1)

            def turn():
                for t in range(NT):
                    turn_tile(t)
                turns[0] += 1

            def norm(k, n):
                square(k, 0)
                root(0, 1)
                sc.wait_ge(mm_done, 4 * n + A_FREE)
                split_hi(n % 2, n // 2 + 2)
                square(k, 1)
                root(1, 2)
                turn_tile(0)
                square(k, 2)
                root(2, 3)
                turn_tile(1)
                square(k, 3)
                root(3, 4)
                sc.wait_ge(mm_done, 4 * n + B_FREE)
                split_hi((n + 1) % 2, (n + 1) // 2 + 2)
                turn_tile(2)
                turn_tile(3)
                turns[0] += 1

            def copy_q(g):
                sc.wait_ge(qk_turned, 2 * g + 1)
                sc.activation(qk[:, 0, :], ps[:, 4, :], ACT.Copy, scale=0.125).then_inc(qT_ready, 1)

            def attention(kind, h, g, ahead=False):
                for s in range(2 if kind == "C" else 0):
                    sc.wait_ge(qk_turned, 16 + 4 * (g - 8) + 2 * s + 1)
                    sc.activation(qk[0:96, s, :], ps[0:96, 4 + 2 * s, :], ACT.Copy, scale=96 ** -0.5)\
                      .then_inc(qT_ready, 1)
                for k in range(9):
                    if ahead and k == 3:
                        sc.wait_ge(mm_done, 8 * g + 12)
                        split_hi(0, g + 3)
                    if ahead and k == 8:
                        copy_q(g + 1)
                    if k < 8:
                        i, m, w = unit(k)
                        sc.wait_ge(max_ready, 8 * g + k + 1)
                        if k >= 2:
                            sc.wait_ge(pT_ready, 8 * g + k - 1)
                        if kind == "B":
                            sc.activation(probs[:, m, 0:w], ps[:, m, 0:w], ACT.Exp, bias=neg_max[:, k:k + 1])\
                              .then_inc(exp_ready, 1)
                        else:
                            sc.activation(probs[:, m, 0:w], ps[:, m, 0:w], ACT.Exp, bias=neg_max[:, k:k + 1],
                                          accum_out=den[:, k:k + 1]).then_inc(exp_ready, 1)
                    if k >= 1:
                        i, m, w = unit(k - 1)
                        sc.wait_ge(pT_ready, 8 * g + k)
                        if k >= 3:
                            sc.wait_ge(pv_ready, 8 * g + k - 2)
                        sc.activation(probsT[:, m, 0:w], ps[:, 2 + m, 0:w], ACT.Copy).then_inc(pT_copied, 1)
                if ahead:
                    sc.wait_ge(mm_done, 8 * g + 16)
                    split_hi(1, g + 3)

            def mlp(l, n0):
                n1 = n0 + FT

                def pair(i, before_last_split=None):
                    for s in range(2):
                        sc.wait_ge(mm_done, 8 * i + 4 * n0 + 2 * s + 2)
                        col = V_CONV + l * FT * 4 + 4 * s
                        sc.activation(qk[:, s, :], ps[:, s, :], ACT.Identity,
                                      scale=vec[:, ds(8 * i + (col + 2), 1)],
                                      bias=vec[:, ds(8 * i + (col + 3), 1)]).then_inc(conv_started[l], 1)
                    split_after_in_loop(i, n0)
                    for s in range(2):
                        sc.wait_ge(conv_done[l], 2 * i + s + 1)
                        sc.activation(qk[:, 2 + s, :], qk[:, s, :], ACT.Silu).then_inc(silu_ready[l], 1)
                    if before_last_split:
                        before_last_split()
                    split_after_in_loop(i, n0 + 1)
                    sc.wait_ge(silu_ready[l], 2 * i + 2)

                def first_highs():
                    sc.wait_ge(val_bank_free[l], 2 + 4)
                    for u in (0, 2):
                        sc.activation(first_hi[:, u:u + 2, :], act[:, u:u + 2, :], ACT.Copy).then_inc(act_hi[l], 2)
                    sc.preload_act_table_set("sqrt_and_others")

                with sc.Fori(0, FT // 2 - 1) as i:
                    pair(i)
                pair(FT // 2 - 1, first_highs)

                def halves(u0, kt, slot, count=4):
                    sc.activation(hT_hi[:, 4 * slot + u0:4 * slot + u0 + count, :], act[:, ds(kt, count), :], ACT.Copy)\
                      .then_inc(act_hi[l], count)

                sc.wait_ge(mm_done, 4 * n1)
                halves(0, 4, 1)
                for j in range(4):
                    sc.wait_ge(mm_done, 4 * (n1 + j + 1))
                    split_hi(j % 2, (n1 + j) // 2 + 2)
                    if j == 3:
                        halves(0, 20, 1, 2)
                        halves(2, 0, 1, 2)
                    else:
                        halves(0, 8 + 4 * j, j % 2)
                with sc.Fori(0, 2) as i:
                    for b in range(2):
                        sc.wait_ge(mm_done, 8 * i + 4 * (n1 + b + 5))
                        split_hi(b, i + ((n1 + 4) // 2 + 2))
                        halves(0, 8 * i + (2 + 4 * b), b)
                sc.wait_ge(mm_done, 4 * (n1 + 9))
                split_hi(0, (n1 + 8) // 2 + 2)
                halves(0, 18, 0)

            load_x(sc, 0)
            load_gain()
            sc.preload_act_table_set("sqrt_and_others")
            split_hi(0, 1)
            square(0, 0)
            root(0, 1)
            split_hi(1, 1)
            turn_tile(0)
            square(0, 1)
            root(1, 2)
            square(0, 2)
            turn_tile(1)
            root(2, 3)
            square(0, 3)
            root(3, 4)
            turn_tile(2)
            turn_tile(3)
            turns[0] += 1
            sc.preload_act_table_set("exp_and_others")
            load_gain()
            sc.wait_ge(lam_dots, 1)
            sc.activation(lam_s[:, 2:4], lam_s[:, 0:2], ACT.Exp).then_inc(lam_exps, 1)
            for n in range(2):
                sc.wait_ge(mm_done, 8)
                split_hi(n, 2)
            copy_q(0)
            with sc.Fori(0, 4) as g:
                attention("A", g, g, ahead=True)
            root(0, 16)
            sc.preload_act_table_set("exp_and_others")
            with sc.Fori(4, 7) as g:
                attention("B", g - 4, g, ahead=True)
            attention("B", 3, 7)
            sc.preload_act_table_set("sqrt_and_others")
            turn()
            for n in (W_OUT0, W_OUT0 + 1):
                split_after(n)
            norm(1, W_OUT0 + 2)
            sc.preload_act_table_set("silu_and_others")
            load_gain()
            mlp(0, W_UP0)
            norm(2, W_DQK - 2)
            load_gain()
            for n in range(W_DQK, W_C):
                split_after(n)
            for c in range(5):
                n = W_C + c // 2
                sc.wait_ge(mm_done, 4 * n + 2 * (c % 2) + 2)
                sc.activation(cT[:, c, :], ps[:, c, :], ACT.Copy, scale=vec[:, V_CG + c:V_CG + c + 1])\
                  .then_inc(c_copied, 1)
                sq = qk[:, c, :] if c < 4 else tmp[:, 0, :]
                sc.activation(sq, ps[:, c, :], ACT.Square).then_inc(sq_ready, 1)
                if c % 2:
                    split_after(n)
            split_after(W_C + 2)
            root(0, 8)
            split_after(W_DV)
            split_after(W_DV + 1)
            sc.wait_ge(c_copied, 5)
            for c in range(5):
                sc.activation(hT_hi[:, c, :], cT[:, c, :], ACT.Copy).then_inc(c_hi, 1)
            split_after(W_UQ)
            split_after(W_UKV)
            sc.preload_act_table_set("natural_log_exp_and_others")
            with sc.Fori(0, 2) as p:
                for m in range(2):
                    sc.activation(qk[:, m, :].unsqueeze(1), dT[:, ds(2 * p + m, 1), :], ACT.Copy, scale=128 ** -0.5)\
                      .then_inc(d_q, 1)
                end = own.loop(p, 2, 16)
                for k in range(9):
                    if k < 8:
                        i, m, w = unit(k)
                        bank = (0, 1, 4, 5)[k % 4]
                        sc.wait_ge(d_scores, 8 * p + k + 1)
                        if k >= 2:
                            sc.wait_ge(d_sp, 8 * p + k - 1)
                        own.link(sc.activation(tmp[:, m, 0:w], ps[:, bank, 0:w], ACT.Abs))
                        own.link(sc.activation(tmp[:, m, 0:w], tmp[:, m, 0:w], ACT.Exp, scale=-1.0))
                        sc.activation(tmp[:, m, 0:w], tmp[:, m, 0:w], ACT.Ln, bias=ones[:, 0:1]).then_inc(d_soft, 1)
                    if k >= 1:
                        i, m, w = unit(k - 1)
                        sc.wait_ge(d_arg, 8 * p + k)
                        sc.activation(probs[:, m, 0:w], probs[:, m, 0:w], ACT.Exp).then_inc(d_exp, 1)
                end()
            for g in (8, 9):
                attention("C", g - 8, g)
            sc.preload_act_table_set("sqrt_and_others")
            turn()
            for n in (W_OUT1, W_OUT1 + 1):
                split_after(n)
            norm(3, W_OUT1 + 2)
            sc.preload_act_table_set("silu_and_others")
            load_gain()
            mlp(1, W_UP1)
            for t in range(NT):
                square(4, t)
                root(t, t + 1)

        @block.vector
        def _(ve):
            own = Own(ve, dve_own)
            roots = [0]
            norms = [0]
            turns = [0]

            def variance(a, b, scale, last=True):
                ins = ve.tensor_scalar(var[:, a:b], ss[:, a:b], scale, EPS, ALU.mult, ALU.add)
                if last:
                    ins.then_inc(var_ready, 1)
                    roots[0] += 1
                else:
                    own.link(ins)

            def rsqrt(a, b):
                ve.wait_ge(sd_ready, roots[0])
                cols = slice(a, b)
                own.link(ve.reciprocal(rstd[:, cols], sd[:, cols]))
                own.link(ve.tensor_tensor(rs_a[:, cols], rstd[:, cols], rstd[:, cols], ALU.mult))
                own.link(ve.scalar_tensor_tensor(rs_a[:, cols], rs_a[:, cols], -0.5, var[:, cols], ALU.mult, ALU.mult))
                own.link(ve.scalar_tensor_tensor(rstd[:, cols], rs_a[:, cols], 1.5, rstd[:, cols], ALU.add, ALU.mult))

            def lows(b):
                t, g = b // 2, b % 2
                ve.wait_ge(turn_hi, 8 * turns[0] + b + 1)
                hi = hT_hi[:, 4 * g:4 * g + 4, t * 128:(t + 1) * 128]
                ve.tensor_tensor(hT_lo[:, 4 * g:4 * g + 4, t * 128:(t + 1) * 128],
                                 ps[:, b, :].rearrange("p (j n) -> p j n", j=4), hi.bitcast(f32),
                                 ALU.subtract).then_inc(turn_lo, 1)

            def add_to_x(n, t):
                ve.wait_ge(mm_done, 4 * n + X_STEPS[t])
                part = x[:, t, 512:1024]
                ve.tensor_tensor(part, part, ps[:, 4 + t, :], ALU.add).then_inc(x_done, 1)

            def tile_variance(k, t):
                ve.wait_ge(ss_ready, 4 * k + t + 1)
                variance(t, t + 1, 1.0 / DM)

            def scale_x(k, t, dst):
                if dst is xn and t >= 2:
                    ve.wait_ge(turned, 8 * turns[0] + 2 * (t - 1))
                ve.scalar_tensor_tensor(xn[:, t % 2, :] if dst is xn else dst[:, t, :], x[:, t, :],
                                        rstd[:, t:t + 1], gain[:, :], ALU.mult, ALU.mult).then_inc(src_ready, 1)

            def tile_lows(t):
                lows(2 * t)
                lows(2 * t + 1)

            def norm(k, n):
                for t in range(2):
                    add_to_x(n, t)
                    tile_variance(k, t)
                    rsqrt(t, t + 1)
                    if t == 0:
                        ve.wait_ge(gain_loaded, 16 * (k + 1))
                    scale_x(k, t, xn)
                add_to_x(n, 2)
                tile_lows(0)
                tile_variance(k, 2)
                add_to_x(n, 3)
                rsqrt(2, 3)
                tile_lows(1)
                scale_x(k, 2, xn)
                tile_variance(k, 3)
                rsqrt(3, 4)
                scale_x(k, 3, xn)
                tile_lows(2)
                tile_lows(3)
                turns[0] += 1

            def copy_k(g):
                ve.wait_ge(qk_turned, 2 * g + 2)
                ve.tensor_copy(qk[:, 2, :], ps[:, 5, :]).then_inc(kT_ready, 1)

            def copy_whole(t):
                ve.wait_ge(mm_done, 2 * t + 2)
                ve.tensor_copy(y[:, t, 0:384], ps[:, 2 * t, 0:384]).then_inc(part_copied, 2)

            def copy_part(g, u, bank):
                ve.wait_ge(mm_done, 8 * g + (u + 1))
                dst = y[:, u % 4, ds(384 * g, 384)]
                if u < 4:
                    ve.tensor_copy(dst, ps[:, bank, 0:384]).then_inc(part_copied, 1)
                else:
                    ve.wait_ge(part_copied, 8 * g + (u - 3))
                    ve.tensor_tensor(dst, dst, ps[:, bank, 0:384], ALU.add).then_inc(part_copied, 1)

            def attention(kind, h, g, ahead=False):
                for s in range(2 if kind == "C" else 0):
                    ve.wait_ge(qk_turned, 16 + 4 * (g - 8) + 2 * s + 2)
                    ve.tensor_copy(qk[0:96, 2 + s, :], ps[0:96, 5 + 2 * s, :]).then_inc(kT_ready, 1)
                for k in range(11):
                    if k < 8:
                        i, m, w = unit(k)
                        ve.wait_ge(scores_ready, 8 * g + k + 1)
                        ve.tensor_reduce(neg_max[:, k:k + 1], ps[:, m, 0:w], AX.X, ALU.max, negate=True)\
                          .then_inc(max_ready, 1)
                    if kind == "B" and 1 <= k <= 8:
                        i, m, w = unit(k - 1)
                        ve.wait_ge(exp_ready, 8 * g + k)
                        ve.scalar_tensor_tensor(probs[:, m, 0:w], probs[:, m, 0:w], 1.0, cmul[:, 512 - w:512],
                                                ALU.mult, ALU.mult, accum_out=den[:, k - 1:k])\
                          .then_inc(mult_ready, 1)
                    if k >= 4 and k % 2 == 0:
                        i = (k - 4) // 2
                        bank = ps[:, 6 + i % 2, :]
                        ve.wait_ge(pv_ready, 8 * g + 2 * i + 2)
                        own.link(ve.reciprocal(rden[:, 2 * i:2 * i + 2], den[:, 2 * i:2 * i + 2]))
                        if kind == "A":
                            own.link(ve.tensor_tensor(rden1[:, i:i + 1], rden[:, 2 * i + 1:2 * i + 2], neg_lam[:, :], ALU.mult))
                            own.link(ve.tensor_scalar(o_tmp[:, :], bank[:, 128:256], rden1[:, i:i + 1], None, ALU.mult))
                            o = y[:, i, ds(384 * h, 128)]
                            own.link(ve.scalar_tensor_tensor(o, bank[:, 0:128], rden[:, 2 * i:2 * i + 1],
                                                             o_tmp[:, :], ALU.mult, ALU.add))
                            ve.scalar_tensor_tensor(o_tmp[:, :], o, 1.0, o, ALU.mult, ALU.mult,
                                                    accum_out=ss[:, ds(h + 4 * i, 1)]).then_inc(o_ready, 1)
                            ve.wait_ge(o_ready, 4 * g + (i + 1))
                        elif kind == "B":
                            ve.tensor_tensor(y[:, i, ds(384 * g, 128)].rearrange("p (m d) -> p m d", m=2),
                                             bank[:, 0:128].rearrange("p (m d) -> p m d", m=2),
                                             rden[:, 2 * i:2 * i + 2].unsqueeze(2).broadcast_to([128, 2, 64]),
                                             ALU.mult).then_inc(o_ready, 1)
                        else:
                            ve.tensor_tensor(o_C[:, i, h * 256:(h + 1) * 256].rearrange("p (m d) -> p m d", m=2),
                                             bank[:, 0:256].rearrange("p (m d) -> p m d", m=2),
                                             rden[:, 2 * i:2 * i + 2].unsqueeze(2).broadcast_to([128, 2, 128]),
                                             ALU.mult).then_inc(o_ready, 1)
                    if ahead:
                        for u in FILL.get(k, ()):
                            copy_part(g + 1, u, 4 + u % 2)
                        if k == 9:
                            copy_k(g + 1)

            def residual(n0):
                for t in range(NT):
                    ve.wait_ge(mm_done, 4 * (n0 + 1) + t + 1)
                    part = x[:, t, 0:512]
                    ve.tensor_tensor(part, part, ps[:, t, :], ALU.add)

            def mlp(l, n0):
                ve.sem_inc(val_bank_free[l], 2)
                n1 = n0 + FT

                def pair(i, before_values=None):
                    for s in range(2):
                        col = V_CONV + l * FT * 4 + 4 * s
                        ve.wait_ge(conv_started[l], 2 * i + s + 1)
                        own.link(ve.scalar_tensor_tensor(qk[:, s, 1:SEQ], ps[:, s, 0:SEQ - 1],
                                                         vec[:, ds(8 * i + (col + 1), 1)], qk[:, s, 1:SEQ],
                                                         ALU.mult, ALU.add))
                        ve.scalar_tensor_tensor(qk[:, s, 2:SEQ], ps[:, s, 0:SEQ - 2], vec[:, ds(8 * i + col, 1)],
                                                qk[:, s, 2:SEQ], ALU.mult, ALU.add).then_inc(conv_done[l], 1)
                    if before_values:
                        before_values()
                    for s in range(2):
                        ve.wait_ge(silu_ready[l], 2 * i + s + 1)
                        ve.wait_ge(mm_done, 8 * i + 4 * (n0 + 1) + 2 * s + 2)
                        ve.tensor_tensor(act[:, ds(2 * i + s, 1), :], ps[:, 2 + s:3 + s, :], qk[:, 2 + s:3 + s, :],
                                         ALU.mult).then_inc(val_bank_free[l], 1)

                def first_lows():
                    for u in (0, 2):
                        ve.wait_ge(act_hi[l], u + 2)
                        ve.tensor_tensor(first_lo[:, u:u + 2, :], act[:, u:u + 2, :], first_hi[:, u:u + 2, :].bitcast(f32),
                                         ALU.subtract).then_inc(act_lo[l], 2)

                with ve.Fori(0, FT // 2 - 1) as i:
                    end = own.loop(i, FT // 2 - 1, 2)
                    pair(i)
                    end()
                pair(FT // 2 - 1, first_lows)

                def lows_of(done, u0, kt, slot, count=4):
                    ve.wait_ge(act_hi[l], done)
                    places = slice(4 * slot + u0, 4 * slot + u0 + count)
                    ve.tensor_tensor(hT_lo[:, places, :], act[:, ds(kt, count), :], hT_hi[:, places, :].bitcast(f32),
                                     ALU.subtract).then_inc(act_lo[l], count)

                lows_of(8, 0, 4, 1)
                for j in range(2, 5):
                    lows_of(4 * j + 4, 0, 4 * j, j % 2)
                lows_of(22, 0, 20, 1, 2)
                lows_of(24, 2, 0, 1, 2)
                lows_of(28, 0, 2, 0)
                ve.wait_ge(mm_done, 4 * (n1 + 5) + 2)
                for t in range(NT):
                    part = x[:, t, 0:512]
                    ve.tensor_tensor(part, part, ps[:, t, :], ALU.add)
                lows_of(32, 0, 6, 1)
                for j in range(8, 11):
                    lows_of(4 * j + 4, 0, 4 * j - FT, j % 2)

            ve.memset(ones[:, :], 1.0).then_inc(ones_ready, 1)
            tile_variance(0, 0)
            rsqrt(0, 1)
            ve.wait_ge(gain_loaded, 16)
            scale_x(0, 0, xn)
            tile_lows(0)
            tile_variance(0, 1)
            rsqrt(1, 2)
            scale_x(0, 1, xn)
            tile_variance(0, 2)
            tile_lows(1)
            rsqrt(2, 3)
            scale_x(0, 2, xn)
            tile_variance(0, 3)
            copy_whole(0)
            rsqrt(3, 4)
            scale_x(0, 3, xn)
            tile_lows(2)
            tile_lows(3)
            turns[0] += 1
            copy_whole(1)
            ve.wait_ge(ident_loaded, 16)
            own.mark(ve.tensor_copy(ident_bf[:, :], ident))
            ve.wait_ge(cst_loaded, 16)
            ve.wait_ge(mask_loaded, 16)
            ve.tensor_copy(mask_bf[:, :], masks_f32).then_inc(masks_ready, 1)
            ve.wait_ge(vec_loaded, 16)
            for j in range(2):
                a = V_LAM + 128 * j
                own.link(ve.tensor_tensor(o_tmp[:, 64 * j:64 * j + 64], vec[:, a:a + 64], vec[:, a + 64:a + 128], ALU.mult))
            ve.tensor_reduce(lam_s[:, 0:2], o_tmp[:, :].rearrange("p (a n) -> p a n", a=2), AX.X, ALU.add)\
              .then_inc(lam_dots, 1)
            own.mark(ve.tensor_scalar(sub_gain[:, :], vec[:, V_SUB:V_SUB + 128], 1.0 - LAM_INIT, None, ALU.mult))
            ve.wait_ge(lam_exps, 1)
            own.link(ve.tensor_tensor(neg_lam[:, :], lam_s[:, 3:4], lam_s[:, 2:3], ALU.subtract))
            own.link(ve.tensor_scalar(neg_lam[:, :], neg_lam[:, :], -LAM_INIT, None, ALU.add))
            ve.wait_ge(masks_ready, 1)
            copy_whole(2)
            copy_whole(3)
            copy_k(0)
            with ve.Fori(0, 4) as g:
                end = own.loop(g, 4, 16)
                attention("A", g, g, ahead=True)
                end()
            variance(0, 16, 1.0 / 128)
            rsqrt(0, 16)
            with ve.Fori(4, 7) as g:
                end = own.loop(g - 4, 3, 4)
                attention("B", g - 4, g, ahead=True)
                end()
            attention("B", 3, 7)
            for t in range(NT):
                if t >= 2:
                    ve.wait_ge(turned, 8 * turns[0] + 2 * (t - 1) - 1)
                for h in range(4):
                    ins = ve.scalar_tensor_tensor(xn[:, t % 2, h * 128:(h + 1) * 128], y[:, t, 384 * h:384 * h + 128],
                                                  rstd[:, 4 * t + h:4 * t + h + 1], sub_gain[:, :], ALU.mult, ALU.mult)
                ins.then_inc(src_ready, 1)
                if t >= 1:
                    lows(2 * t - 2)
                    lows(2 * t - 1)
            lows(6)
            lows(7)
            turns[0] += 1
            residual(W_OUT0)
            norm(1, W_OUT0 + 2)
            mlp(0, W_UP0)
            norm(2, W_DQK - 2)
            with ve.Fori(0, 2) as i:
                for c in range(4):
                    ve.wait_ge(mm_done, 8 * i + 4 * (W_DQK + c // 2) + 2 * (c % 2) + 2)
                    ve.tensor_copy(dT[:, ds(4 * i + c, 1), :], ps[:, ds(4 * i + c, 1), :]).then_inc(dT_copied, 1)
            ve.wait_ge(mm_done, 4 * (W_C + 3))
            ve.tensor_copy(kr, ps[:, 5, 0:128].rearrange("p (t d) -> p t d", t=NT)).then_inc(kr_copied, 1)
            ve.wait_ge(c_stats, 1)
            own.link(ve.tensor_copy(ss[:, 0:8], ps[:, 6, 0:8]))
            variance(0, 4, 1.0 / 384, last=False)
            variance(4, 8, 1.0 / 256)
            rsqrt(0, 8)
            for t in range(NT):
                ve.wait_ge(mm_done, 4 * (W_DV + 1) + t + 1)
                ve.tensor_copy(dv[:, t, :], ps[:, t, :]).then_inc(dv_copied, 1)
            for c in range(5):
                ve.wait_ge(c_hi, c + 1)
                ve.tensor_tensor(hT_lo[:, c, :], cT[:, c, :], hT_hi[:, c, :].bitcast(f32), ALU.subtract)\
                  .then_inc(c_lo, 1)
            for t in range(NT):
                ve.wait_ge(mm_done, 4 * W_UQ + t + 1)
                ve.tensor_scalar(q_tok[:, t, :], ps[:, 4 + t, 0:384], rstd[:, t:t + 1], None, ALU.mult)\
                  .then_inc(q_scaled, 1)
            for t in range(NT):
                ve.wait_ge(mm_done, 4 * W_UKV + t + 1)
                for c in range(2):
                    ins = ve.tensor_scalar(kv_tok[:, t, 384 * c:384 * c + 384], ps[:, 4 * c + t, 0:384],
                                           rstd[:, 4 + t:5 + t], None, ALU.mult)
                ins.then_inc(kv_scaled, 1)
            with ve.Fori(0, 2) as p:
                end = own.loop(p, 2, 8)
                for k in range(12):
                    if k < 8:
                        i, m, w = unit(k)
                        bank = (0, 1, 4, 5)[k % 4]
                        ve.wait_ge(d_soft, 8 * p + k + 1)
                        sp_ = d_sums[:, m, 0:w]
                        ve.scalar_tensor_tensor(sp_, ps[:, bank, 0:w], 0.0, tmp[:, m, 0:w], ALU.max, ALU.add)\
                          .then_inc(d_sp, 1)
                        ve.wait_ge(d_sp, 8 * p + k + 1)
                        own.link(ve.tensor_tensor_scan(sp_[:, ::-1], sp_[:, ::-1], sp_[:, ::-1], 0.0, ALU.add, ALU.max))
                        if k >= 2:
                            ve.wait_ge(d_turned, 8 * p + k - 1)
                        ve.tensor_tensor(probs[:, m, 0:w], ps[:, bank, 0:w], sp_, ALU.subtract).then_inc(d_arg, 1)
                    if 2 <= k < 10:
                        i, m, w = unit(k - 2)
                        ve.wait_ge(d_turned, 8 * p + k - 1)
                        if k >= 4:
                            ve.wait_ge(d_pv, 8 * p + k - 3)
                        ve.tensor_copy(probsT[:, m, 0:w], ps[:, 2 + m, 0:w]).then_inc(d_copied, 1)
                    if k >= 5 and k % 2:
                        i = (k - 5) // 2
                        ve.wait_ge(d_pv, 8 * p + 2 * i + 2)
                        ve.tensor_copy(o_D[:, i, ds(256 * p, 256)], ps[:, 6 + i % 2, 0:256]).then_inc(d_out, 1)
                end()
            for g in (8, 9):
                attention("C", g - 8, g)
            for b in range(8):
                lows(b)
            turns[0] += 1
            residual(W_OUT1)
            norm(3, W_OUT1 + 2)
            mlp(1, W_UP1)
            for t in range(NT):
                add_to_x(W_ALL - 2, t)
                tile_variance(4, t)
                rsqrt(t, t + 1)
                if t == 0:
                    ve.wait_ge(gain_loaded, 16 * 5)
                scale_x(4, t, final)

        @block.tensor
        def _(pe):
            PASSES = ((hT_hi, w_hi), (hT_hi, w_lo), (hT_lo, w_hi))
            turns = [0]

            def turn_tile(t, source, ready):
                for j in range(KT):
                    if j % 4 == 0:
                        ready(t, j // 4)
                    ins = pe.transpose(ps[:, 2 * t + j // 4, 128 * (j % 4):128 * (j % 4) + 128], source(t, j), ident)
                    if j % 4 == 3:
                        ins.then_inc(turned, 1)

            def turn(source, ready):
                for t in range(NT):
                    turn_tile(t, source, ready)
                turns[0] += 1

            norms = [0]

            def turn_xn(t):
                turn_tile(t, lambda t, j: xn[:, t % 2, j * 128:(j + 1) * 128],
                          lambda t, g: pe.wait_ge(src_ready, src_base() + t + 1) if g == 0 else None)

            def src_base():
                return 4 * norms[0] + (4 if norms[0] else 0)

            def last_two(n, a_part, b_part, b_ready=None):
                for step in ("A0", "A1", "A2", "B0", "A3", "B1", "x0", "B2", "B3", "x1"):
                    t = int(step[1])
                    if step[0] == "x":
                        if not final_norm():
                            turn_xn(t)
                        continue
                    k0, first = a_part if step[0] == "A" else b_part
                    slot = (n + (step[0] == "B")) % 2
                    if step in ("A0", "B0"):
                        pe.wait_ge(w_lo_ready, n + 1 + (step == "B0"))
                        if step == "B0" and b_ready:
                            b_ready()
                    for k in range(4):
                        for m, (h, w) in enumerate(PASSES):
                            ins = pe.matmul(ps[:, 4 + t, :], h[:, k0 + k, t * 128:(t + 1) * 128],
                                            w[:, slot, k * 512:(k + 1) * 512], start=first and k == 0 and m == 0,
                                            stop=step[0] == "B" and k == 3 and m == 2)
                    ins.then_inc(mm_done, 1)

            def final_norm():
                return norms[0] == 4

            def first_tile(slot):
                for half, s in ((0, 0), (0, 1), (1, 0), (1, 1)):
                    pe.wait_ge(turn_lo, 8 * turns[0] + 4 * half + 4)
                    for k in range(KT):
                        for m, (h, w) in enumerate(PASSES):
                            ins = pe.matmul(ps[:, s, 256 * half:256 * half + 256],
                                            w[:, slot, k * 256 + 128 * s:k * 256 + 128 * s + 128],
                                            h[:, k, 256 * half:256 * half + 256],
                                            start=k == 0 and m == 0, stop=k == KT - 1 and m == 2)
                    if half:
                        ins.then_inc(mm_done, 2)
                    elif s == 0:
                        turn_xn(2)
                        turn_xn(3)
                turns[0] += 1
                norms[0] += 1

            def tokens_tile(slot, first, last, k0, nk, width, banks, before=None, offset=0, inc=1):
                for t in range(NT):
                    if before:
                        before(t)
                    for k in range(nk):
                        for n, (h, w) in enumerate(PASSES):
                            ins = pe.matmul(ps[:, banks[t], 0:width], h[:, k0 + k, t * 128:(t + 1) * 128],
                                            w[:, slot, k * width:(k + 1) * width],
                                            start=first and k == 0 and n == 0,
                                            stop=last and k == nk - 1 and n == 2)
                    ins.then_inc(mm_done, inc)

            def channels(slot, s, bank, pitch=256):
                for k in range(KT):
                    for n, (h, w) in enumerate(PASSES):
                        ins = pe.matmul(bank, w[:, slot, k * pitch + 128 * s:k * pitch + 128 * s + 128], h[:, k:k + 1, :],
                                        start=k == 0 and n == 0, stop=k == KT - 1 and n == 2)
                ins.then_inc(mm_done, 2)

            def tok_ready(t):
                pe.wait_ge(turn_lo, 8 * (turns[0] - 1) + 2 * t + 2)

            def project_out(n0):
                for half in range(2):
                    pe.wait_ge(w_lo_ready, n0 + half + 1)
                    tokens_tile(half, half == 0, half == 1, 4 * half, 4, 512, range(NT), tok_ready if half == 0 else None)
                last_two(n0 + 2, (0, True), (4, False))

            def turn_qk(g):
                pe.wait_ge(part_copied, 8 * g + 8)
                for t in range(NT):
                    pe.wait_ge(rope_ready, 4 * g + (t + 1))
                    for s in range(2):
                        ins = pe.transpose(ps[:, 4 + s, t * 128:(t + 1) * 128], stage[:, t, s * 128:(s + 1) * 128], ident)
                        if t == NT - 1:
                            ins.then_inc(qk_turned, 1)

            def part(g, u, bank):
                half, t = u // 4, u % 4
                if t == 0:
                    pe.wait_ge(w_lo_ready, 2 * g + (half + 1))
                for k in range(4):
                    for n, (h_, w_) in enumerate(PASSES):
                        ins = pe.matmul(ps[:, bank, 0:384], h_[:, 4 * half + k, t * 128:(t + 1) * 128],
                                        w_[:, half, k * 384:(k + 1) * 384], start=k == 0 and n == 0, stop=k == 3 and n == 2)
                ins.then_inc(mm_done, 1)

            def attention(kind, h, g, ahead=False):
                if kind == "C":
                    for s in range(2):
                        if s == 1 and g > 8:
                            pe.wait_ge(o_ready, 4 * g)
                        for src, bank in ((q_tok, 4 + 2 * s), (k_tok, 5 + 2 * s)):
                            for t in range(NT):
                                ins = pe.transpose(ps[0:96, bank, t * 128:(t + 1) * 128],
                                                   src[:, t, (2 * h + s) * 96:(2 * h + s + 1) * 96], ident)
                            ins.then_inc(qk_turned, 1)
                for k in range(10):
                    fill = FILL.get(k, ()) if ahead else ()
                    if k < 8:
                        i, m, w = unit(k)
                        if kind == "C":
                            pe.wait_ge(qT_ready, 8 + 2 * (g - 8) + m + 1)
                            pe.wait_ge(kT_ready, 8 + 2 * (g - 8) + m + 1)
                            q, kk = qk[0:96, m, i * 128:(i + 1) * 128], qk[0:96, 2 + m, 0:w]
                        else:
                            if k == 0:
                                pe.wait_ge(qT_ready, g + 1)
                                pe.wait_ge(kT_ready, g + 1)
                            q, kk = qk[64 * m:64 * m + 64, 0, i * 128:(i + 1) * 128], qk[64 * m:64 * m + 64, 2, 0:w]
                        if k >= 2:
                            pe.wait_ge(exp_ready, 8 * g + k - 1)
                        pe.matmul(ps[:, m, 0:w], q, kk, start=True, stop=False)
                        if kind == "B":
                            ins = pe.matmul(ps[:, m, 0:w], ident_bf[:, :], mask_bf[:, M_END - w:M_END], start=False, stop=True)
                        else:
                            ins = pe.matmul(ps[:, m, w - 128:w], ident_bf[:, :], mask_bf[:, M_CAUSAL:M_CAUSAL + 128],
                                            start=False, stop=True)
                        ins.then_inc(scores_ready, 1)
                    if ahead and k == 8:
                        turn_qk(g + 1)
                    for u in fill[:1]:
                        if u >= 2:
                            pe.wait_ge(part_copied, 8 * g + (7 + u))
                        part(g + 1, u, 4 + u % 2)
                    if 1 <= k <= 8:
                        i, m, w = unit(k - 1)
                        if kind == "B":
                            pe.wait_ge(mult_ready, 8 * (g - 4) + k)
                        else:
                            pe.wait_ge(exp_ready, 8 * g + k)
                        if k >= 3:
                            pe.wait_ge(pT_copied, 8 * g + k - 2)
                        for b in range(i + 1):
                            ins = pe.transpose(ps[:, 2 + m, b * 128:(b + 1) * 128], probs[:, m, b * 128:(b + 1) * 128], ident)
                        ins.then_inc(pT_ready, 1)
                    for u in fill[1:]:
                        if u >= 2:
                            pe.wait_ge(part_copied, 8 * g + (7 + u))
                        part(g + 1, u, 4 + u % 2)
                    if k >= 2:
                        i, m, w = unit(k - 2)
                        pe.wait_ge(pT_copied, 8 * g + k - 1)
                        if i >= 2 and m == 0:
                            pe.wait_ge(o_ready, 4 * g + i - 1)
                        for b in range(i + 1):
                            if kind == "A":
                                v, o = y[:, b, ds(384 * g + 256, 128)], ps[:, 6 + i % 2, 128 * m:128 * m + 128]
                            elif kind == "B":
                                v, o = y[:, b, ds(384 * g + (256 + 64 * m), 64)], ps[:, 6 + i % 2, 64 * m:64 * m + 64]
                            else:
                                c0 = 192 * (2 * h + m) + 64
                                v, o = kv_tok[:, b, c0:c0 + 128], ps[:, 6 + i % 2, 128 * m:128 * m + 128]
                            ins = pe.matmul(o, probsT[:, m, b * 128:(b + 1) * 128], v, start=b == 0, stop=b == i)
                        ins.then_inc(pv_ready, 1)

            def mlp(l, n0):
                def pair(i, first=False):
                    for half in range(2):
                        pe.wait_ge(w_lo_ready, 2 * i + (n0 + half + 1))
                        if first and half == 0:
                            first_tile(n0 % 2)
                            continue
                        for s in range(2):
                            if half:
                                pe.wait_ge(val_bank_free[l], 2 * i + s + 1)
                            channels(half, s, ps[:, 2 * half + s:2 * half + s + 1, :])
                    pe.wait_ge(conv_done[l], 2 * i + 2)

                pair(0, first=True)
                with pe.Fori(1, FT // 2) as i:
                    pair(i)
                n1 = n0 + FT

                def down_tile(slot, parts, last, wait_w, wait_lo, beside=False):
                    pe.wait_ge(w_lo_ready, wait_w)
                    pe.wait_ge(act_lo[l], wait_lo)
                    for c, units, first, stop, incs in parts:
                        for t in range(NT):
                            if beside and t == 2:
                                pe.wait_ge(val_bank_free[l], 2 + FT)
                            for u in units:
                                for n, (h, w) in enumerate(PASSES):
                                    if beside:
                                        a = first_lo[:, u, :] if n == 2 else first_hi[:, u, :]
                                    else:
                                        a = h[:, 4 * slot + u, :]
                                    ins = pe.matmul(ps[:, 4 * c + t, :], a[:, t * 128:(t + 1) * 128],
                                                    w[:, slot, u * 512:(u + 1) * 512],
                                                    start=first and u == units[0] and n == 0,
                                                    stop=stop and u == units[-1] and n == 2)
                            if incs[t]:
                                ins.then_inc(mm_done, incs[t])

                every, four = (1, 1, 1, 1), (0, 1, 2, 3)
                down_tile(0, [(0, four, True, False, every)], False, n1 + 1, 4, beside=True)
                with pe.Fori(0, 2) as i:
                    for b in range(2):
                        down_tile(1 - b, [(0, four, False, False, every)], False,
                                  2 * i + (n1 + b + 2), 8 * i + 4 * (b + 2))
                down_tile(1, [(0, (0, 1), False, True, (0, 0, 0, 2)), (1, (2, 3), True, False, (0, 0, 0, 2))],
                          False, n1 + 6, 24)
                for j in (6, 7, 8):
                    down_tile(j % 2, [(1, four, False, False, every)], False, n1 + j + 1, 4 * (j + 1))
                pe.wait_ge(act_lo[l], 40)
                last_two(n1 + 9, (4, False), (0, False), lambda: pe.wait_ge(act_lo[l], 44))

            pe.wait_ge(ident_loaded, 16)
            turn_xn(0)
            for t in range(NT):
                for half in range(2):
                    if half == 0:
                        pe.wait_ge(turn_lo, 2 * t + 2)
                    elif t < 3:
                        turn_xn(t + 1)
                    if t == 0:
                        pe.wait_ge(w_lo_ready, half + 1)
                    for k in range(4):
                        for n, (h_, w_) in enumerate(PASSES):
                            ins = pe.matmul(ps[:, 2 * t, 0:384], h_[:, 4 * half + k, t * 128:(t + 1) * 128],
                                            w_[:, half, k * 384:(k + 1) * 384],
                                            start=half == 0 and k == 0 and n == 0, stop=half == 1 and k == 3 and n == 2)
                ins.then_inc(mm_done, 2)
            turns[0] += 1
            norms[0] += 1
            turn_qk(0)
            pe.wait_ge(masks_ready, 1)
            with pe.Fori(0, 4) as g:
                attention("A", g, g, ahead=True)
            with pe.Fori(4, 7) as g:
                attention("B", g - 4, g, ahead=True)
            attention("B", 3, 7)

            def mixed_ready(t, g):
                if g == 0:
                    pe.wait_ge(src_ready, 4 + t + 1)
            turn(lambda t, j: xn[:, t % 2, j * 128:(j + 1) * 128] if j < 4 else y[:, t, 384 * j:384 * j + 128],
                 mixed_ready)
            project_out(W_OUT0)
            mlp(0, W_UP0)
            for n in range(4):
                pe.wait_ge(w_lo_ready, W_DQK + n + 1)
                if n == 0:
                    first_tile(W_DQK % 2)
                    continue
                for s in range(2):
                    channels((W_DQK + n) % 2, s, ps[:, 2 * n + s:2 * n + s + 1, :])
            for c in range(5):
                n = W_C + c // 2
                pe.wait_ge(w_lo_ready, n + 1)
                pe.wait_ge(dT_copied, c + 1)
                channels(n % 2, c % 2, ps[:, c:c + 1, :], 160 if c == 4 else 256)
            pe.wait_ge(dT_copied, 6)
            n = W_C + 2
            for t in range(NT):
                for k in range(KT):
                    for m, (h, w) in enumerate(PASSES):
                        ins = pe.matmul(ps[:, 5, 32 * t:32 * t + 32], h[:, k, t * 128:(t + 1) * 128],
                                        w[:, n % 2, k * 160 + 128:k * 160 + 160],
                                        start=k == 0 and m == 0, stop=k == KT - 1 and m == 2)
            ins.then_inc(mm_done, 2)
            pe.wait_ge(sq_ready, 5)
            pe.wait_ge(dT_copied, 7)
            pe.wait_ge(ones_ready, 1)
            for which, cs in ((0, (0, 1, 2)), (1, (3, 4))):
                for t in range(NT):
                    for c in cs:
                        sq = qk[:, c, t * 128:(t + 1) * 128] if c < 4 else tmp[:, 0, t * 128:(t + 1) * 128]
                        ins = pe.matmul(ps[:, 6, 4 * which + t:4 * which + t + 1], sq, ones[:, :],
                                        start=c == cs[0], stop=c == cs[-1])
            ins.then_inc(c_stats, 1)
            for half in range(2):
                n = W_DV + half
                pe.wait_ge(w_lo_ready, n + 1)
                if half == 0:
                    pe.wait_ge(c_copied, 5)
                tokens_tile(n % 2, half == 0, half == 1, 4 * half, 4, 512, range(NT))
            pe.wait_ge(w_lo_ready, W_UQ + 1)
            pe.wait_ge(c_lo, 5)
            tokens_tile(W_UQ % 2, True, True, 0, 3, 384, [4, 5, 6, 7])
            pe.wait_ge(w_lo_ready, W_UKV + 1)
            for t in range(NT):
                pe.wait_ge(q_scaled, t + 1)
                for c in range(2):
                    for k in range(2):
                        for m, (h, w) in enumerate(PASSES):
                            ins = pe.matmul(ps[:, 4 * c + t, 0:384], h[:, 3 + k, t * 128:(t + 1) * 128],
                                            w[:, W_UKV % 2, k * 768 + 384 * c:k * 768 + 384 * c + 384],
                                            start=k == 0 and m == 0, stop=k == 1 and m == 2)
                ins.then_inc(mm_done, 1)
            pe.wait_ge(kv_scaled, NT)
            with pe.Fori(0, 2) as p:
                for k in range(11):
                    if k < 8:
                        i, m, w = unit(k)
                        bank = (0, 1, 4, 5)[k % 4]
                        if k < 2:
                            pe.wait_ge(d_q, 2 * p + m + 1)
                        if k >= 4:
                            pe.wait_ge(d_arg, 8 * p + k - 3)
                        pe.matmul(ps[:, bank:bank + 1, 0:w], qk[:, m, i * 128:(i + 1) * 128],
                                  dT[:, ds(2 * p + (4 + m), 1), 0:w], start=True, stop=False)
                        pe.matmul(ps[:, bank, w - 128:w], ident_bf[:, :], mask_bf[:, M_STRICT:M_STRICT + 128],
                                  start=False, stop=True).then_inc(d_scores, 1)
                    if 2 <= k < 10:
                        i, m, w = unit(k - 2)
                        pe.wait_ge(d_exp, 8 * p + k - 1)
                        if k >= 4:
                            pe.wait_ge(d_copied, 8 * p + k - 3)
                        for b in range(i + 1):
                            ins = pe.transpose(ps[:, 2 + m, b * 128:(b + 1) * 128], probs[:, m, b * 128:(b + 1) * 128], ident)
                        ins.then_inc(d_turned, 1)
                    if k >= 3:
                        i, m, w = unit(k - 3)
                        pe.wait_ge(d_copied, 8 * p + k - 2)
                        if i >= 2 and m == 0:
                            pe.wait_ge(d_out, 4 * p + i - 1)
                        for b in range(i + 1):
                            ins = pe.matmul(ps[:, 6 + i % 2, 128 * m:128 * m + 128], probsT[:, m, b * 128:(b + 1) * 128],
                                            dv[:, b, ds(256 * p + 128 * m, 128)], start=b == 0, stop=b == i)
                        ins.then_inc(d_pv, 1)
            pe.wait_ge(c_roped, 3)
            pe.wait_ge(d_out, 8)
            for g in (8, 9):
                attention("C", g - 8, g)
            pe.wait_ge(o_ready, 40)
            turn(lambda t, j: o_C[:, t, j * 128:(j + 1) * 128] if j < 4 else o_D[:, t, (j - 4) * 128:(j - 3) * 128],
                 lambda t, g: None)
            project_out(W_OUT1)
            mlp(1, W_UP1)


def _constants():
    import numpy as np
    p = np.arange(128)
    consts = np.zeros((128, C_END), np.float32)
    consts[:, C_ID:C_ID + 128] = np.eye(128)
    masks = np.zeros((128, M_END), np.float32)
    q, k = p[:, None], p[None, :]
    masks[:, M_CAUSAL:M_CAUSAL + 128] = np.where(k <= q, 0.0, -1e30)
    masks[:, M_STRICT:M_STRICT + 128] = np.where(k < q, 0.0, -1e30)
    for s in range(4):
        d = q - k + 128 * (3 - s)
        seen = ((d >= 0) & (d <= 128)).astype(np.float32) + ((d >= 0) & (d % 4 == 0)) + ((d >= 0) & (d % 16 == 0))
        consts[:, C_CMUL + 128 * s:C_CMUL + 128 * s + 128] = seen
        masks[:, M_DIL + 128 * s:M_DIL + 128 * s + 128] = np.where(seen > 0, 0.0, -1e30)
    for dim, c0, s0 in ((64, C_COS64, C_SIN64), (32, C_COS32, C_SIN32)):
        inv = (np.float32(10000.0) ** (-np.arange(0, dim, 2, dtype=np.float32) / np.float32(dim))).astype(np.float32)
        ang = np.arange(SEQ, dtype=np.float32)[:, None] * inv[None, :]
        cos, sin = np.cos(ang).astype(np.float32), np.sin(ang).astype(np.float32)
        for base, tab in ((c0, np.concatenate([cos, cos], 1)), (s0, np.concatenate([-sin, sin], 1))):
            consts[:, base:base + NT * dim] = tab.reshape(NT, 128, dim).transpose(1, 0, 2).reshape(128, -1)
    return consts, masks


def _weight_tiles(ab_w_in, ab_w_out, cd_w_in, c_w_uq, c_w_ukv, cd_w_out, ffn_w_up, ffn_w_down):
    import numpy as np

    def tiles(a):
        a = a.transpose(1, 0, 2).reshape(128, -1)
        out = np.zeros((1, 128, UNIT), np.float32)
        out[0, :, :a.shape[1]] = a
        return out

    def tokens(w):
        w = w.reshape(KT, 128, -1)
        return [tiles(w[4 * h:4 * h + 4, :, c:c + 512]) for c in range(0, w.shape[2], 512) for h in range(2)]

    def channels(w, width=256):
        w = w.reshape(KT, 128, -1)
        return [tiles(w[:, :, c:c + width]) for c in range(0, w.shape[2], width)]

    def mlp(l):
        gate, val = channels(ffn_w_up[l][:, :DFF]), channels(ffn_w_up[l][:, DFF:])
        up = [t for pair in zip(gate, val) for t in pair]
        units = [ffn_w_down[l].reshape(FT, 128, DM)[k, :, 512 * c:512 * c + 512] for c in range(2) for k in range(FT)]
        return up + [tiles(np.stack(units[u:u + 4])) for u in range(0, 2 * FT, 4)]

    cd = cd_w_in[0]
    qkv = ab_w_in[0].reshape(KT, 128, 2, 3, 4, 128).transpose(2, 4, 0, 1, 3, 5).reshape(8, 2, 4, 128, 384)
    all_tiles = [tiles(qkv[g, h]) for g in range(8) for h in range(2)] + tokens(ab_w_out[0]) + mlp(0)
    all_tiles += channels(cd[:, 672:1696]) + channels(cd[:, 0:512]) + channels(cd[:, 512:672], 160)
    all_tiles += tokens(cd[:, 1696:2208])
    all_tiles += [tiles(c_w_uq[0].reshape(3, 128, 384)), tiles(c_w_ukv[0].reshape(2, 128, 768))]
    all_tiles += tokens(cd_w_out[0]) + mlp(1)
    out = np.concatenate(all_tiles)
    assert out.shape == (W_ALL, 128, UNIT)
    return out


def kernel(x, mix_norm_g, ffn_norm_g, final_norm_g, ab_w_in, a_lambda_q1, a_lambda_k1, a_lambda_q2, a_lambda_k2,
           a_subln_g, ab_w_out, cd_w_in, c_q_norm_g, c_w_uq, c_kv_norm_g, c_w_ukv, cd_w_out, ffn_w_up, ffn_conv_w,
           ffn_conv_b, ffn_w_down):
    import numpy as np
    import concourse.bacc as bacc
    from concourse.bass_utils import run_bass_kernel_spmd

    consts, masks = _constants()
    a = np.asarray
    conv = np.concatenate([a(ffn_conv_w), a(ffn_conv_b)[:, None, :]], 1)
    conv = conv.reshape(2, 4, FT, 128).transpose(3, 0, 2, 1).reshape(128, -1)
    rows = np.concatenate([a(a_lambda_q1)[0], a(a_lambda_k1)[0], a(a_lambda_q2)[0], a(a_lambda_k2)[0], a(a_subln_g)[0]])
    latent = np.concatenate([a(c_q_norm_g)[0], a(c_kv_norm_g)[0]]).reshape(5, 128).T
    vectors = np.concatenate([np.broadcast_to(rows, (128, 384)), conv, latent], 1)
    gains = np.stack([a(mix_norm_g)[0], a(ffn_norm_g)[0], a(mix_norm_g)[1], a(ffn_norm_g)[1], a(final_norm_g)])
    arrays = {
        "x_in": a(x),
        "weights": _weight_tiles(*(a(w) for w in (ab_w_in, ab_w_out, cd_w_in, c_w_uq, c_w_ukv, cd_w_out,
                                                   ffn_w_up, ffn_w_down))),
        "consts": consts, "masks": masks, "vectors": vectors,
        "gains": np.broadcast_to(gains, (128, 5, DM)),
    }
    arrays = {name: np.ascontiguousarray(v) for name, v in arrays.items()}
    nc = bacc.Bacc("TRN2", target_bir_lowering=False, num_devices=1)
    args = [nc.dram_tensor(name, v.shape, mybir.dt.from_np(v.dtype), kind="ExternalInput").ap()
            for name, v in arrays.items()]
    out = nc.dram_tensor("out", (1, SEQ, DM), mybir.dt.float32, kind="ExternalOutput").ap()
    trunk_program(nc, *args, out)
    r = run_bass_kernel_spmd(nc, [arrays], core_ids=[0])
    return r.results[0]["out"]
```

```python
import math
from contextlib import ExitStack

import concourse.bass as bass
from concourse import mybir

SEQ, DM, DFF = 512, 1024, 2816
NT = SEQ // 128
KT = DM // 128
FT = DFF // 128
UNIT = 2048
EPS = 1e-6
LAM_INIT = 0.8 - 0.6 * math.exp(-0.3 * 0)

W_IN0 = 0
W_OUT0 = W_IN0 + 16
W_UP0 = W_OUT0 + 4
W_DN0 = W_UP0 + FT
W_DQK = W_DN0 + FT // 2
W_DV = W_DQK + 4
W_C = W_DV + 2
W_UQ = W_C + 3
W_UKV = W_UQ + 1
W_OUT1 = W_UKV + 1
W_UP1 = W_OUT1 + 4
W_DN1 = W_UP1 + FT
W_ALL = W_DN1 + FT // 2

C_ID, C_CMUL, C_COS64, C_SIN64, C_COS32, C_SIN32, C_END = 0, 128, 640, 896, 1152, 1280, 1408
M_CAUSAL, M_STRICT, M_DIL, M_END = 0, 128, 256, 768
V_LAM, V_SUB, V_CONV, V_CG, V_END = 0, 256, 384, 384 + 2 * FT * 4, 384 + 2 * FT * 4 + 5


def trunk_program(nc, x_in, weights, consts, masks, vectors, gains, out):
    f32, f32r, bf16 = mybir.dt.float32, mybir.dt.float32r, mybir.dt.bfloat16
    ACT, ALU, AX = mybir.ActivationFunctionType, mybir.AluOpType, mybir.AxisListType
    ds = bass.ds
    n_tiles = W_ALL

    with ExitStack() as ctx:
        def sb(name, shape, dt=f32):
            return ctx.enter_context(nc.sbuf_tensor(name, shape, dt))

        def sem(name):
            return ctx.enter_context(nc.semaphore(name))

        x = sb("x", [128, NT, DM])
        hT_hi = sb("hT_hi", [128, KT, SEQ], f32r)
        hT_lo = sb("hT_lo", [128, KT, SEQ], f32r)
        w_raw = sb("w_raw", [128, 2, UNIT])
        w_hi = sb("w_hi", [128, 2, UNIT], f32r)
        w_lo = sb("w_lo", [128, 2, UNIT], f32r)
        region_at = nc.sbuf_base
        region = sb("region", [128, 17024])
        y = region[:, 0:12288].rearrange("p (t n) -> p t n", t=NT)
        act = region[:, 0:FT * SEQ].rearrange("p (j n) -> p j n", j=FT)
        final = region[:, 0:4096].rearrange("p (t n) -> p t n", t=NT)
        dT = region[:, 0:4096].rearrange("p (c n) -> p c n", c=8)
        c_tok = region[:, 4096:6784].rearrange("p (t n) -> p t n", t=NT)
        kr = c_tok[:, :, 640:672]
        o_C = region[:, 4096:6144].rearrange("p (t n) -> p t n", t=NT)
        dv = region[:, 6784:8832].rearrange("p (t n) -> p t n", t=NT)
        q_tok = region[:, 8832:10368].rearrange("p (t n) -> p t n", t=NT)
        v_tok = region[:, 10368:12416].rearrange("p (t n) -> p t n", t=NT)
        k_tok = region[:, 12416:13952].rearrange("p (t n) -> p t n", t=NT)
        o_D = region[:, 13952:16000].rearrange("p (t n) -> p t n", t=NT)
        c_tmp = region[:, 16000:17024].rearrange("p (a n) -> p a n", a=2)

        xn = sb("xn", [128, 2, DM])
        probs = xn[:, 0, :].rearrange("p (a n) -> p a n", a=2)
        probsT = xn[:, 1, :].rearrange("p (a n) -> p a n", a=2)
        stage_mem = sb("stage", [128, 1024])
        stage = stage_mem[:, :].rearrange("p (t n) -> p t n", t=NT)
        d_sums = stage_mem[:, :].rearrange("p (a n) -> p a n", a=2)
        qk = sb("qk", [128, 4, SEQ])
        tmp = sb("tmp", [128, 2, SEQ])
        gain = sb("gain", [128, DM])
        cst = sb("cst", [128, C_END])
        vec = sb("vec", [128, V_END])
        mask_bf = sb("mask_bf", [128, M_END], bf16)
        ident_bf = sb("ident_bf", [128, 128], bf16)
        ones = sb("ones", [128, 1])
        sub_gain = sb("sub_gain", [128, 128])
        neg_lam = sb("neg_lam", [128, 1])
        lam_s = sb("lam_s", [128, 4])
        ss = sb("ss", [128, 16])
        var = sb("var", [128, 16])
        sd = sb("sd", [128, 16])
        rstd = sb("rstd", [128, 16])
        rs_a = sb("rs_a", [128, 16])
        neg_max = sb("neg_max", [128, 8])
        den = sb("den", [128, 8])
        rden = sb("rden", [128, 8])
        rden1 = sb("rden1", [128, 4])
        o_tmp = sb("o_tmp", [128, 128])

        ident = cst[:, C_ID:C_ID + 128]
        cmul = cst[:, C_CMUL:C_CMUL + 512]
        cos64 = cst[:, C_COS64:C_COS64 + 256].rearrange("p (t d) -> p t d", t=NT)
        sin64 = cst[:, C_SIN64:C_SIN64 + 256].rearrange("p (t d) -> p t d", t=NT)
        cos32 = cst[:, C_COS32:C_COS32 + 128].rearrange("p (t d) -> p t d", t=NT)
        sin32 = cst[:, C_SIN32:C_SIN32 + 128].rearrange("p (t d) -> p t d", t=NT)
        first_hi = nc.alloc_sbuf_tensor_at("first_hi", [128, 4, SEQ], f32r, offset=region_at + 4 * 12288)
        first_lo = nc.alloc_sbuf_tensor_at("first_lo", [128, 4, SEQ], f32r, offset=region_at + 4 * (12288 + 4 * SEQ))
        masks_f32 = region[:, 12288:12288 + M_END]

        ps = ctx.enter_context(nc.psum_tensor("ps", [128, 8, 512], f32))

        x_loaded = [sem(f"x_loaded{t}") for t in range(NT)]
        ident_loaded, cst_loaded, vec_loaded, mask_loaded = sem("ident_loaded"), sem("cst_loaded"), sem("vec_loaded"), sem("mask_loaded")
        gain_loaded, out_stored = sem("gain_loaded"), sem("out_stored")
        w_loaded = [sem("w_loaded0"), sem("w_loaded1")]
        w_hi_ready, w_lo_ready, mm_done = sem("w_hi_ready"), sem("w_lo_ready"), sem("mm_done")
        masks_ready, ones_ready = sem("masks_ready"), sem("ones_ready")
        lam_dots, lam_exps = sem("lam_dots"), sem("lam_exps")
        x_done = sem("x_done")
        ss_ready, var_ready, sd_ready = sem("ss_ready"), sem("var_ready"), sem("sd_ready")
        src_ready = sem("src_ready")
        turned, turn_hi, turn_lo = sem("turned"), sem("turn_hi"), sem("turn_lo")
        part_copied = sem("part_copied")
        rope_ready, qk_turned, qT_ready, kT_ready = sem("rope_ready"), sem("qk_turned"), sem("qT_ready"), sem("kT_ready")
        scores_ready, max_ready, exp_ready, mult_ready = sem("scores_ready"), sem("max_ready"), sem("exp_ready"), sem("mult_ready")
        pT_ready, pT_copied, pv_ready, o_ready = sem("pT_ready"), sem("pT_copied"), sem("pv_ready"), sem("o_ready")
        conv_started, conv_done, silu_ready = [[sem(f"{n}{l}") for l in range(2)] for n in
                                               ("conv_started", "conv_done", "silu_ready")]
        val_bank_free = [sem(f"val_bank_free{l}") for l in range(2)]
        act_hi, act_lo = [[sem(f"{n}{l}") for l in range(2)] for n in ("act_hi", "act_lo")]
        half_turned, half_hi, half_lo, early_added = sem("half_turned"), sem("half_hi"), sem("half_lo"), sem("early_added")
        dT_copied, dv_copied, c_copied, c_squared, c_turned, c_hi, c_lo, q_scaled, kv_scaled, c_roped = (
            sem(n) for n in ("dT_copied", "dv_copied", "c_copied", "c_squared", "c_turned", "c_hi", "c_lo",
                             "q_scaled", "kv_scaled", "c_roped"))
        d_q, d_scores, d_soft, d_sp, d_arg, d_exp, d_turned, d_copied, d_pv, d_out = (
            sem(n) for n in ("d_q", "d_scores", "d_soft", "d_sp", "d_arg", "d_exp", "d_turned", "d_copied", "d_pv", "d_out"))
        act_own, dve_own, pool_own = sem("act_own"), sem("dve_own"), sem("pool_own")

        block = ctx.enter_context(nc.Block())

        class Own:

            def __init__(self, eng, steps):
                self.eng, self.steps, self.n, self.shift = eng, steps, 0, 0

            def mark(self, ins):
                ins.then_inc(self.steps, 1)
                self.n += 1
                return self.n

            def wait(self, value):
                self.eng.wait_ge(self.steps, self.shift + value)

            def link(self, ins):
                self.wait(self.mark(ins))

            def loop(self, i, turns, marks):
                start, self.shift = self.n, i * marks

                def end():
                    assert self.n - start == marks, self.n - start
                    self.n, self.shift = start + turns * marks, 0
                return end

        def load_x(eng, t):
            eng.dma_start(x[:, t, :], x_in[0, t * 128:(t + 1) * 128, :]).then_inc(x_loaded[t], 16)

        def norm_base(k):
            return 4 * (k - 1)

        def unit(k):
            return k // 2, k % 2, 128 * (k // 2 + 1)

        X_STEPS, A_FREE, B_FREE = (4, 5, 7, 8), 6, 8

        BOTH = (0, 1)
        D_FILL = {0: (("q", 0, (0,)), ("q", 1, (0,))), 1: (("q", 0, (1,)), ("q", 1, (1,))), 2: (("q", 2, BOTH),),
                  3: (("q", 3, BOTH),), 4: (("kv", 0, (0,)), ("kv", 1, (0,))), 6: (("kv", 0, (1,)),),
                  7: (("kv", 1, (1,)),), 8: (("kv", 2, BOTH),), 9: (("kv", 3, BOTH),)}
        D_TURN = {10: (0, 1), 11: (2, 3), 12: (4,)}
        D_UQ = {13: (0, 1), 14: (2, 3)}
        D_UKV = {15: 0, 16: 1, 17: 2, 18: 3}

        def latent_done(n):
            return [(kind, t) for kind, t, parts in D_FILL.get(n, ()) if 1 in parts]

        def d_unit(n):
            p, (i, m, w) = n // 8, unit(n % 8)
            return (p, i, m, w) if p == 0 else (p, 3 - i, m, 128 * (4 - i))

        def c_fill(what):
            kind, t = what
            return (t, t, 0, 384) if kind == "q" else (4 + t, t, 384, 672)

        EARLY_TURN = {7: {0: (0, 1), 1: (2, 3)}, 8: {0: (0, 1), 1: (2, 3)}}
        EARLY_FILL = {7: {k: k - 3 for k in range(3, 10)}, 8: {3: 0, 5: 1, 7: 2, 9: 3}, 9: {2: 4, 5: 5, 8: 6}}

        def layer_of(g):
            return (0, W_OUT0, 0) if g < 8 else (1, W_OUT1, 4)

        FILL = {0: (0,), 1: (1,), 2: (2,), 3: (3,), 4: (4,), 5: (5,), 6: (6,), 7: (7,)}

        @block.sync
        def _(sp):
            def load(m, slot):
                sp.dma_start(w_raw[:, slot, :], weights[m, :, :]).then_inc(w_loaded[slot], 16)

            load(0, 0)
            sp.dma_start(cst[:, 0:C_CMUL], consts[:, 0:C_CMUL]).then_inc(ident_loaded, 16)
            load(1, 1)
            for t in range(1, NT):
                load_x(sp, t)
            sp.dma_start(cst[:, C_CMUL:], consts[:, C_CMUL:]).then_inc(cst_loaded, 16)
            sp.dma_start(vec[:, :], vectors).then_inc(vec_loaded, 16)
            sp.dma_start(masks_f32, masks).then_inc(mask_loaded, 16)
            with sp.Fori(1, n_tiles // 2) as j:
                for slot in range(2):
                    sp.wait_ge(w_lo_ready, 2 * j + slot - 1)
                    sp.dma_start(w_raw[:, slot, :].unsqueeze(1),
                                 weights[ds(2 * j + slot, 1), :, :].rearrange("m p n -> p m n"))\
                      .then_inc(w_loaded[slot], 16)
            if n_tiles % 2:
                sp.wait_ge(w_lo_ready, n_tiles - 2)
                load(n_tiles - 1, (n_tiles - 1) % 2)
            for t in range(NT):
                sp.wait_ge(src_ready, 5 * NT + t + 1)
                sp.dma_start(out[0, t * 128:(t + 1) * 128, :], final[:, t, :]).then_inc(out_stored, 16)
            sp.wait_ge(out_stored, 16 * NT)

        @block.gpsimd
        def _(pool):
            own = Own(pool, pool_own)

            def split_lo(m, slot):
                pool.wait_ge(w_hi_ready, m + 1)
                pool.tensor_tensor(w_lo[:, slot, :], w_raw[:, slot, :], w_hi[:, slot, :].bitcast(f32),
                                   ALU.subtract).then_inc(w_lo_ready, 1)

            def split_range(a, b):
                b = min(b, n_tiles)
                if a >= b:
                    return
                if a % 2:
                    split_lo(a, 1)
                    a += 1
                if b - a >= 2:
                    with pool.Fori(0, (b - a) // 2) as j:
                        for slot in range(2):
                            split_lo(2 * j + (a + slot), slot)
                if (b - a) % 2:
                    split_lo(b - 1, 0)

            def table(tab, shape):
                return tab.unsqueeze(2).broadcast_to(shape)

            def rope_tile(g, t, parts=None):
                pool.wait_ge(part_copied, parts or 8 * g + (t + 5))
                src = y[:, t, ds(384 * g, 256)].rearrange("p (m d) -> p m d", m=4)
                dst = stage[:, t, :].rearrange("p (m d) -> p m d", m=4)
                t1, t2 = (tmp[:, j, 256 * (t % 2):256 * (t % 2) + 256].rearrange("p (m d) -> p m d", m=4) for j in range(2))
                cos, sin = (tab[:, t, :].unsqueeze(1).broadcast_to([128, 4, 64]) for tab in (cos64, sin64))
                own.mark(pool.tensor_tensor(t1, src, cos, ALU.mult))
                own.mark(pool.tensor_tensor(t2[:, :, 0:32], src[:, :, 32:64], sin[:, :, 0:32], ALU.mult))
                own.link(pool.tensor_tensor(t2[:, :, 32:64], src[:, :, 0:32], sin[:, :, 32:64], ALU.mult))
                pool.tensor_tensor(dst, t1, t2, ALU.add).then_inc(rope_ready, 1)

            split_lo(0, 0)
            split_lo(1, 1)
            pool.wait_ge(cst_loaded, 16)
            for t in range(2):
                rope_tile(0, t, 2 * t + 2)
            split_lo(2, 0)
            split_lo(3, 1)
            with pool.Fori(1, 8) as g:
                end = own.loop(g - 1, 7, 12)
                pool.wait_ge(qk_turned, 2 * g)
                split_lo(2 * g + 2, 0)
                for t in range(NT):
                    pool.wait_ge(rope_ready, 4 * g + t - 1)
                    rope_tile(g, t)
                split_lo(2 * g + 3, 1)
                end()
            split_range(W_OUT0 + 2, W_UKV + 1)
            pool.wait_ge(c_copied, 8)
            kr4 = kr.unsqueeze(2)
            t1 = c_tmp[:, 0, 0:128].rearrange("p (t d) -> p t d", t=NT).unsqueeze(2)
            t2 = c_tmp[:, 1, 0:128].rearrange("p (t d) -> p t d", t=NT).unsqueeze(2)
            c4, s4 = cos32.unsqueeze(2), sin32.unsqueeze(2)
            own.mark(pool.tensor_tensor(t1, kr4, c4, ALU.mult))
            own.mark(pool.tensor_tensor(t2[:, :, :, 0:16], kr4[:, :, :, 16:], s4[:, :, :, 0:16], ALU.mult))
            own.link(pool.tensor_tensor(t2[:, :, :, 16:], kr4[:, :, :, 0:16], s4[:, :, :, 16:], ALU.mult))
            own.link(pool.tensor_tensor(kr4, t1, t2, ALU.add))
            k4 = k_tok.rearrange("p t (h d) -> p t h d", h=4)
            pool.tensor_copy(k4[:, :, :, 64:96], kr4.broadcast_to([128, NT, 4, 32])).then_inc(c_roped, 1)
            pool.wait_ge(q_scaled, NT)
            q4 = q_tok.rearrange("p t (h d) -> p t h d", h=4)[:, :, :, 64:96]
            t1 = c_tmp[:, 0, :].rearrange("p (t h d) -> p t h d", t=NT, h=4)
            t2 = c_tmp[:, 1, :].rearrange("p (t h d) -> p t h d", t=NT, h=4)
            c4, s4 = table(cos32, [128, NT, 4, 32]), table(sin32, [128, NT, 4, 32])
            own.mark(pool.tensor_tensor(t1, q4, c4, ALU.mult))
            own.mark(pool.tensor_tensor(t2[:, :, :, 0:16], q4[:, :, :, 16:], s4[:, :, :, 0:16], ALU.mult))
            own.link(pool.tensor_tensor(t2[:, :, :, 16:], q4[:, :, :, 0:16], s4[:, :, :, 16:], ALU.mult))
            pool.tensor_tensor(q4, t1, t2, ALU.add).then_inc(c_roped, 1)
            split_range(W_OUT1, n_tiles)

        @block.scalar
        def _(sc):
            own = Own(sc, act_own)

            def split_hi(slot, fill):
                sc.wait_ge(w_loaded[slot], 16 * fill)
                sc.activation(w_hi[:, slot, :], w_raw[:, slot, :], ACT.Copy).then_inc(w_hi_ready, 1)

            def split_after(n):
                if n + 2 < n_tiles:
                    sc.wait_ge(mm_done, 4 * (n + 1))
                    split_hi(n % 2, n // 2 + 2)

            def split_after_in_loop(i, n0):
                sc.wait_ge(mm_done, 8 * i + 4 * (n0 + 1))
                split_hi(n0 % 2, i + (n0 // 2 + 2))

            gains_asked = [0]

            def load_gain():
                g = gains_asked[0]
                sc.dma_start(gain[:, :], gains[:, g, :]).then_inc(gain_loaded, 16)
                gains_asked[0] += 1

            roots = [0]

            def root(a, b):
                sc.wait_ge(var_ready, roots[0] + 1)
                roots[0] += 1
                sc.activation(sd[:, a:b], var[:, a:b], ACT.Sqrt).then_inc(sd_ready, 1)

            def inverse_root(width):
                sc.wait_ge(var_ready, roots[0] + 1)
                roots[0] += 1
                own.link(sc.activation(sd[:, 0:width], var[:, 0:width], ACT.Ln))
                sc.activation(sd[:, 0:width], sd[:, 0:width], ACT.Exp, scale=-0.5).then_inc(sd_ready, 1)

            def square(k, t):
                if k == 0:
                    sc.wait_ge(x_loaded[t], 16)
                else:
                    sc.wait_ge(x_done, norm_base(k) + t + 1)
                if t >= 1:
                    sc.wait_ge(ss_ready, 4 * k + t)
                sc.activation(tmp[:, :, :].rearrange("p a n -> p (a n)"), x[:, t, :], ACT.Square,
                              accum_out=ss[:, t:t + 1]).then_inc(ss_ready, 1)

            turns = [0]

            def turn_tile(t):
                for g in range(2):
                    b = 2 * t + g
                    sc.wait_ge(turned, 8 * turns[0] + b + 1)
                    sc.activation(hT_hi[:, 4 * g:4 * g + 4, t * 128:(t + 1) * 128],
                                  ps[:, b, :].rearrange("p (j n) -> p j n", j=4), ACT.Copy).then_inc(turn_hi, 1)

            def turn():
                for t in range(NT):
                    turn_tile(t)
                turns[0] += 1

            def norm(k, n):
                square(k, 0)
                root(0, 1)
                square(k, 1)
                root(1, 2)
                sc.wait_ge(mm_done, 4 * n + A_FREE)
                split_hi(n % 2, n // 2 + 2)
                turn_tile(0)
                square(k, 2)
                turn_tile(1)
                root(2, 3)
                square(k, 3)
                root(3, 4)
                sc.wait_ge(mm_done, 4 * n + B_FREE)
                split_hi((n + 1) % 2, (n + 1) // 2 + 2)
                turn_tile(2)
                turn_tile(3)
                turns[0] += 1

            def half_high(count, bank, place, t):
                sc.wait_ge(half_turned, count)
                sc.activation(hT_hi[:, place:place + 4, t * 128:(t + 1) * 128],
                              ps[:, bank, :].rearrange("p (j n) -> p j n", j=4), ACT.Copy).then_inc(half_hi, 1)

            def late_half(l):
                n0, place = (W_OUT1, 0) if l else (W_OUT0, 4)
                for t in range(NT):
                    if t == 3:
                        sc.wait_ge(mm_done, 4 * (n0 + 2))
                        split_hi((n0 + 1) % 2, (n0 + 1) // 2 + 2)
                    half_high(8 * l + 5 + t, t, place, t)

            def copy_q(g):
                sc.wait_ge(qk_turned, 2 * g + 1)
                sc.activation(qk[:, 0, :], ps[:, 4, :], ACT.Copy, scale=0.125).then_inc(qT_ready, 1)

            def attention(kind, h, g, ahead=False):
                g_static = None if ahead else g
                l, n0, early = (None, None, None) if ahead else layer_of(g)
                for s in range(2 if kind == "C" else 0):
                    sc.wait_ge(qk_turned, 16 + 4 * (g - 8) + 2 * s + 1)
                    sc.activation(qk[0:96, s, :], ps[0:96, 4 + 2 * s, :], ACT.Copy, scale=96 ** -0.5)\
                      .then_inc(qT_ready, 1)
                for k in range(9):
                    if ahead and k == 3:
                        sc.wait_ge(mm_done, 8 * g + 12)
                        split_hi(0, g + 3)
                    if k < 8:
                        i, m, w = unit(k)
                        sc.wait_ge(max_ready, 8 * g + k + 1)
                        if k >= 2:
                            sc.wait_ge(pT_ready, 8 * g + k - 1)
                        if kind == "B":
                            sc.activation(probs[:, m, 0:w], ps[:, m, 0:w], ACT.Exp, bias=neg_max[:, k:k + 1])\
                              .then_inc(exp_ready, 1)
                        else:
                            sc.activation(probs[:, m, 0:w], ps[:, m, 0:w], ACT.Exp, bias=neg_max[:, k:k + 1],
                                          accum_out=den[:, k:k + 1]).then_inc(exp_ready, 1)
                    for t in EARLY_TURN.get(g_static, {}).get(k, ()):
                        half_high(8 * l + t + 1, 4 + t % 2, early, t)
                    if EARLY_FILL.get(g_static, {}).get(k - 1) == 3:
                        split_after(n0)
                    if k >= 1:
                        i, m, w = unit(k - 1)
                        sc.wait_ge(pT_ready, 8 * g + k)
                        if k >= 3:
                            sc.wait_ge(pv_ready, 8 * g + k - 2)
                        sc.activation(probsT[:, m, 0:w], ps[:, 2 + m, 0:w], ACT.Copy).then_inc(pT_copied, 1)
                if ahead:
                    copy_q(g + 1)
                    sc.wait_ge(mm_done, 8 * g + 16)
                    split_hi(1, g + 3)

            def mlp(l, n0):
                n1 = n0 + FT

                def pair(i, before_last_split=None):
                    for s in range(2):
                        sc.wait_ge(mm_done, 8 * i + 4 * n0 + 2 * s + 2)
                        col = V_CONV + l * FT * 4 + 4 * s
                        sc.activation(qk[:, s, :], ps[:, s, :], ACT.Identity,
                                      scale=vec[:, ds(8 * i + (col + 2), 1)],
                                      bias=vec[:, ds(8 * i + (col + 3), 1)]).then_inc(conv_started[l], 1)
                    split_after_in_loop(i, n0)
                    for s in range(2):
                        sc.wait_ge(conv_done[l], 2 * i + s + 1)
                        sc.activation(qk[:, 2 + s, :], qk[:, s, :], ACT.Silu).then_inc(silu_ready[l], 1)
                    if before_last_split:
                        before_last_split()
                    split_after_in_loop(i, n0 + 1)
                    sc.wait_ge(silu_ready[l], 2 * i + 2)

                def first_highs():
                    sc.wait_ge(val_bank_free[l], 2 + 4)
                    for u in (0, 2):
                        sc.activation(first_hi[:, u:u + 2, :], act[:, u:u + 2, :], ACT.Copy).then_inc(act_hi[l], 2)
                    sc.preload_act_table_set("sqrt_and_others")

                with sc.Fori(0, FT // 2 - 1) as i:
                    pair(i)
                pair(FT // 2 - 1, first_highs)

                def halves(u0, kt, slot, count=4):
                    sc.activation(hT_hi[:, 4 * slot + u0:4 * slot + u0 + count, :], act[:, ds(kt, count), :], ACT.Copy)\
                      .then_inc(act_hi[l], count)

                sc.wait_ge(mm_done, 4 * n1)
                halves(0, 4, 1)
                for j in range(4):
                    sc.wait_ge(mm_done, 4 * (n1 + j + 1))
                    split_hi(j % 2, (n1 + j) // 2 + 2)
                    if j == 3:
                        halves(0, 20, 1, 2)
                        halves(2, 0, 1, 2)
                    else:
                        halves(0, 8 + 4 * j, j % 2)
                with sc.Fori(0, 2) as i:
                    for b in range(2):
                        sc.wait_ge(mm_done, 8 * i + 4 * (n1 + b + 5))
                        split_hi(b, i + ((n1 + 4) // 2 + 2))
                        halves(0, 8 * i + (2 + 4 * b), b)
                sc.wait_ge(mm_done, 4 * (n1 + 9))
                split_hi(0, (n1 + 8) // 2 + 2)
                halves(0, 18, 0)

            load_x(sc, 0)
            load_gain()
            sc.preload_act_table_set("sqrt_and_others")
            split_hi(0, 1)
            square(0, 0)
            root(0, 1)
            split_hi(1, 1)
            turn_tile(0)
            square(0, 1)
            root(1, 2)
            square(0, 2)
            turn_tile(1)
            root(2, 3)
            square(0, 3)
            root(3, 4)
            turn_tile(2)
            turn_tile(3)
            turns[0] += 1
            sc.preload_act_table_set("natural_log_exp_and_others")
            load_gain()
            for n in range(2):
                sc.wait_ge(mm_done, (5, 8)[n])
                split_hi(n, 2)
            copy_q(0)
            sc.wait_ge(lam_dots, 1)
            sc.activation(lam_s[:, 2:4], lam_s[:, 0:2], ACT.Exp).then_inc(lam_exps, 1)
            with sc.Fori(0, 4) as g:
                attention("A", g, g, ahead=True)
            inverse_root(16)
            with sc.Fori(4, 7) as g:
                attention("B", g - 4, g, ahead=True)
            attention("B", 3, 7)
            sc.preload_act_table_set("sqrt_and_others")
            late_half(0)
            norm(1, W_OUT0 + 2)
            sc.preload_act_table_set("silu_and_others")
            load_gain()
            mlp(0, W_UP0)
            norm(2, W_DQK - 2)
            load_gain()
            sc.preload_act_table_set("natural_log_exp_and_others")
            for n in range(W_DQK, W_DV + 1):
                split_after(n)

            def square_latent(j):
                t = j % 4
                sc.wait_ge(c_copied, j + 1)
                if j < 4:
                    sc.activation(q_tok[:, t, :], c_tok[:, t, 0:384], ACT.Square, accum_out=ss[:, j:j + 1])\
                      .then_inc(c_squared, 1)
                else:
                    sc.activation(v_tok[:, t, 0:256], c_tok[:, t, 384:640], ACT.Square, accum_out=ss[:, j:j + 1])\
                      .then_inc(c_squared, 1)

            def d_q_half(p):
                for m in range(2):
                    sc.activation(qk[:, 2 * p + m, :], dT[:, 2 * p + m, :], ACT.Copy, scale=128 ** -0.5).then_inc(d_q, 1)

            sc.wait_ge(dT_copied, 4)
            d_q_half(0)
            split_after(W_DV + 1)
            for n in range(17):
                if n < 16:
                    p, i, m, w = d_unit(n)
                    sc.wait_ge(d_scores, n + 1)
                    if n >= 2:
                        sc.wait_ge(d_sp, n - 1)
                    own.link(sc.activation(tmp[:, m, 0:w], ps[:, m, 0:w], ACT.Abs))
                    own.link(sc.activation(tmp[:, m, 0:w], tmp[:, m, 0:w], ACT.Exp, scale=-1.0))
                    sc.activation(tmp[:, m, 0:w], tmp[:, m, 0:w], ACT.Ln, bias=ones[:, 0:1]).then_inc(d_soft, 1)
                if n >= 1:
                    p, i, m, w = d_unit(n - 1)
                    sc.wait_ge(d_arg, n)
                    sc.activation(probs[:, m, 0:w], probs[:, m, 0:w], ACT.Exp).then_inc(d_exp, 1)
                for what in latent_done(n - 1):
                    square_latent(c_fill(what)[0])
                if n == 3:
                    split_after(W_C)
                    d_q_half(1)
                for c in D_TURN.get(n, ()):
                    sc.wait_ge(c_turned, c + 1)
                    sc.activation(hT_hi[:, c, :], ps[:, 4 + c % 2, :], ACT.Copy, scale=vec[:, V_CG + c:V_CG + c + 1])\
                      .then_inc(c_hi, 1)
                if n == 10:
                    inverse_root(8)
                if n in (10, 11):
                    m = W_C + n - 9
                    sc.wait_ge(mm_done, 4 * W_UQ)
                    split_hi(m % 2, m // 2 + 2)
                if n == 16:
                    split_after(W_UQ)
            split_after(W_UKV)
            attention("C", 0, 8)
            split_after(W_OUT1)
            attention("C", 1, 9)
            sc.preload_act_table_set("sqrt_and_others")
            late_half(1)
            norm(3, W_OUT1 + 2)
            sc.preload_act_table_set("silu_and_others")
            load_gain()
            mlp(1, W_UP1)
            for t in range(NT):
                square(4, t)
                root(t, t + 1)

        @block.vector
        def _(ve):
            own = Own(ve, dve_own)
            roots = [0]
            norms = [0]
            turns = [0]

            def variance(a, b, scale, last=True):
                ins = ve.tensor_scalar(var[:, a:b], ss[:, a:b], scale, EPS, ALU.mult, ALU.add)
                if last:
                    ins.then_inc(var_ready, 1)
                    roots[0] += 1
                else:
                    own.link(ins)

            def rsqrt(a, b):
                ve.wait_ge(sd_ready, roots[0])
                cols = slice(a, b)
                own.link(ve.reciprocal(rstd[:, cols], sd[:, cols]))
                own.link(ve.tensor_tensor(rs_a[:, cols], rstd[:, cols], rstd[:, cols], ALU.mult))
                own.link(ve.scalar_tensor_tensor(rs_a[:, cols], rs_a[:, cols], -0.5, var[:, cols], ALU.mult, ALU.mult))
                own.link(ve.scalar_tensor_tensor(rstd[:, cols], rs_a[:, cols], 1.5, rstd[:, cols], ALU.add, ALU.mult))

            def refine(a, b):
                ve.wait_ge(sd_ready, roots[0])
                cols = slice(a, b)
                own.link(ve.tensor_tensor(rs_a[:, cols], sd[:, cols], sd[:, cols], ALU.mult))
                own.link(ve.scalar_tensor_tensor(rs_a[:, cols], rs_a[:, cols], -0.5, var[:, cols], ALU.mult, ALU.mult))
                own.link(ve.scalar_tensor_tensor(rstd[:, cols], rs_a[:, cols], 1.5, sd[:, cols], ALU.add, ALU.mult))

            def lows(b):
                t, g = b // 2, b % 2
                ve.wait_ge(turn_hi, 8 * turns[0] + b + 1)
                hi = hT_hi[:, 4 * g:4 * g + 4, t * 128:(t + 1) * 128]
                ve.tensor_tensor(hT_lo[:, 4 * g:4 * g + 4, t * 128:(t + 1) * 128],
                                 ps[:, b, :].rearrange("p (j n) -> p j n", j=4), hi.bitcast(f32),
                                 ALU.subtract).then_inc(turn_lo, 1)

            def add_to_x(n, t):
                ve.wait_ge(mm_done, 4 * n + X_STEPS[t])
                part = x[:, t, 512:1024]
                ve.tensor_tensor(part, part, ps[:, 4 + t, :], ALU.add).then_inc(x_done, 1)

            def tile_variance(k, t):
                ve.wait_ge(ss_ready, 4 * k + t + 1)
                variance(t, t + 1, 1.0 / DM)

            def scale_x(k, t, dst):
                if dst is xn and t >= 2:
                    ve.wait_ge(turned, 8 * turns[0] + 2 * (t - 1))
                ve.scalar_tensor_tensor(xn[:, t % 2, :] if dst is xn else dst[:, t, :], x[:, t, :],
                                        rstd[:, t:t + 1], gain[:, :], ALU.mult, ALU.mult).then_inc(src_ready, 1)

            def tile_lows(t):
                lows(2 * t)
                lows(2 * t + 1)

            def norm(k, n):
                after_output = k in (1, 3)
                if after_output:
                    for t in range(3):
                        late_first(n, t)
                for t in range(2):
                    add_to_x(n, t)
                    if after_output and t == 1:
                        late_first(n, 3)
                    tile_variance(k, t)
                    rsqrt(t, t + 1)
                    if t == 0:
                        ve.wait_ge(gain_loaded, 16 * (k + 1))
                    scale_x(k, t, xn)
                add_to_x(n, 2)
                tile_lows(0)
                tile_lows(1)
                tile_variance(k, 2)
                add_to_x(n, 3)
                rsqrt(2, 3)
                scale_x(k, 2, xn)
                tile_variance(k, 3)
                rsqrt(3, 4)
                scale_x(k, 3, xn)
                tile_lows(2)
                tile_lows(3)
                turns[0] += 1

            def copy_k(g):
                ve.wait_ge(qk_turned, 2 * g + 2)
                ve.tensor_copy(qk[:, 2, :], ps[:, 5, :]).then_inc(kT_ready, 1)

            def copy_whole(t):
                ve.wait_ge(mm_done, 2 * t + 2)
                ve.tensor_copy(y[:, t, 0:384], ps[:, 2 * t, 0:384]).then_inc(part_copied, 2)

            def copy_part(g, u, bank):
                ve.wait_ge(mm_done, 8 * g + (u + 1))
                dst = y[:, u % 4, ds(384 * g, 384)]
                if u < 4:
                    ve.tensor_copy(dst, ps[:, bank, 0:384]).then_inc(part_copied, 1)
                else:
                    ve.wait_ge(part_copied, 8 * g + (u - 3))
                    ve.tensor_tensor(dst, dst, ps[:, bank, 0:384], ALU.add).then_inc(part_copied, 1)

            def half_low(count, bank, place, t):
                ve.wait_ge(half_hi, count)
                hi = hT_hi[:, place:place + 4, t * 128:(t + 1) * 128]
                ve.tensor_tensor(hT_lo[:, place:place + 4, t * 128:(t + 1) * 128],
                                 ps[:, bank, :].rearrange("p (j n) -> p j n", j=4), hi.bitcast(f32),
                                 ALU.subtract).then_inc(half_lo, 1)

            def add_early(n0, f):
                c, t = f // 4, f % 4
                ve.wait_ge(mm_done, 4 * n0 + f + 1)
                xs = x[:, t, 512 * c:512 * c + 512]
                ve.tensor_tensor(xs, xs, ps[:, 4 + f % 2, :], ALU.add).then_inc(early_added, 1)

            def late_half(l):
                for t in range(NT):
                    if t == 3:
                        add_early(W_OUT1 if l else W_OUT0, 7)
                    half_low(8 * l + 5 + t, t, 0 if l else 4, t)

            def attention(kind, h, g, ahead=False, between=None):
                g_static = None if ahead else g
                l, n0, early = (None, None, None) if ahead else layer_of(g)
                for s in range(2 if kind == "C" else 0):
                    ve.wait_ge(qk_turned, 16 + 4 * (g - 8) + 2 * s + 2)
                    ve.tensor_copy(qk[0:96, 2 + s, :], ps[0:96, 5 + 2 * s, :]).then_inc(kT_ready, 1)
                for k in range(11):
                    if k < 8:
                        i, m, w = unit(k)
                        ve.wait_ge(scores_ready, 8 * g + k + 1)
                        ve.tensor_reduce(neg_max[:, k:k + 1], ps[:, m, 0:w], AX.X, ALU.max, negate=True)\
                          .then_inc(max_ready, 1)
                    if kind == "B" and 1 <= k <= 8:
                        i, m, w = unit(k - 1)
                        ve.wait_ge(exp_ready, 8 * g + k)
                        ve.scalar_tensor_tensor(probs[:, m, 0:w], probs[:, m, 0:w], 1.0, cmul[:, 512 - w:512],
                                                ALU.mult, ALU.mult, accum_out=den[:, k - 1:k])\
                          .then_inc(mult_ready, 1)
                    if k >= 4 and k % 2 == 0:
                        i = (k - 4) // 2
                        bank = ps[:, 6 + i % 2, :]
                        ve.wait_ge(pv_ready, 8 * g + 2 * i + 2)
                        own.link(ve.reciprocal(rden[:, 2 * i:2 * i + 2], den[:, 2 * i:2 * i + 2]))
                        if kind == "A":
                            own.link(ve.tensor_tensor(rden1[:, i:i + 1], rden[:, 2 * i + 1:2 * i + 2], neg_lam[:, :], ALU.mult))
                            own.link(ve.tensor_scalar(o_tmp[:, :], bank[:, 128:256], rden1[:, i:i + 1], None, ALU.mult))
                            o = y[:, i, ds(384 * h, 128)]
                            own.link(ve.scalar_tensor_tensor(o, bank[:, 0:128], rden[:, 2 * i:2 * i + 1],
                                                             o_tmp[:, :], ALU.mult, ALU.add))
                            ve.scalar_tensor_tensor(o_tmp[:, :], o, 1.0, o, ALU.mult, ALU.mult,
                                                    accum_out=ss[:, ds(h + 4 * i, 1)]).then_inc(o_ready, 1)
                            ve.wait_ge(o_ready, 4 * g + (i + 1))
                        elif kind == "B":
                            ve.tensor_tensor(y[:, i, ds(384 * g, 128)].rearrange("p (m d) -> p m d", m=2),
                                             bank[:, 0:128].rearrange("p (m d) -> p m d", m=2),
                                             rden[:, 2 * i:2 * i + 2].unsqueeze(2).broadcast_to([128, 2, 64]),
                                             ALU.mult).then_inc(o_ready, 1)
                        else:
                            ve.tensor_tensor(o_C[:, i, h * 256:(h + 1) * 256].rearrange("p (m d) -> p m d", m=2),
                                             bank[:, 0:256].rearrange("p (m d) -> p m d", m=2),
                                             rden[:, 2 * i:2 * i + 2].unsqueeze(2).broadcast_to([128, 2, 128]),
                                             ALU.mult).then_inc(o_ready, 1)
                    if k == 5 and between:
                        between()
                    for t in EARLY_TURN.get(g_static, {}).get(k, ()):
                        half_low(8 * l + t + 1, 4 + t % 2, early, t)
                    f = EARLY_FILL.get(g_static, {}).get(k)
                    if f is not None:
                        add_early(n0, f)
                    if ahead:
                        for u in FILL.get(k, ()):
                            copy_part(g + 1, u, 4 + u % 2)
                        if k == 9:
                            copy_k(g + 1)

            def late_first(n, t):
                ve.wait_ge(mm_done, 4 * n + (1, 2, 3, 6)[t])
                part = x[:, t, 0:512]
                ve.tensor_tensor(part, part, ps[:, t, :], ALU.add)

            def mlp(l, n0):
                ve.sem_inc(val_bank_free[l], 2)
                n1 = n0 + FT

                def pair(i, before_values=None):
                    for s in range(2):
                        col = V_CONV + l * FT * 4 + 4 * s
                        ve.wait_ge(conv_started[l], 2 * i + s + 1)
                        own.link(ve.scalar_tensor_tensor(qk[:, s, 1:SEQ], ps[:, s, 0:SEQ - 1],
                                                         vec[:, ds(8 * i + (col + 1), 1)], qk[:, s, 1:SEQ],
                                                         ALU.mult, ALU.add))
                        ve.scalar_tensor_tensor(qk[:, s, 2:SEQ], ps[:, s, 0:SEQ - 2], vec[:, ds(8 * i + col, 1)],
                                                qk[:, s, 2:SEQ], ALU.mult, ALU.add).then_inc(conv_done[l], 1)
                    if before_values:
                        before_values()
                    for s in range(2):
                        ve.wait_ge(silu_ready[l], 2 * i + s + 1)
                        ve.wait_ge(mm_done, 8 * i + 4 * (n0 + 1) + 2 * s + 2)
                        ve.tensor_tensor(act[:, ds(2 * i + s, 1), :], ps[:, 2 + s:3 + s, :], qk[:, 2 + s:3 + s, :],
                                         ALU.mult).then_inc(val_bank_free[l], 1)

                def first_lows():
                    for u in (0, 2):
                        ve.wait_ge(act_hi[l], u + 2)
                        ve.tensor_tensor(first_lo[:, u:u + 2, :], act[:, u:u + 2, :], first_hi[:, u:u + 2, :].bitcast(f32),
                                         ALU.subtract).then_inc(act_lo[l], 2)

                with ve.Fori(0, FT // 2 - 1) as i:
                    end = own.loop(i, FT // 2 - 1, 2)
                    pair(i)
                    end()
                pair(FT // 2 - 1, first_lows)

                def lows_of(done, u0, kt, slot, count=4):
                    ve.wait_ge(act_hi[l], done)
                    places = slice(4 * slot + u0, 4 * slot + u0 + count)
                    ve.tensor_tensor(hT_lo[:, places, :], act[:, ds(kt, count), :], hT_hi[:, places, :].bitcast(f32),
                                     ALU.subtract).then_inc(act_lo[l], count)

                lows_of(8, 0, 4, 1)
                for j in range(2, 5):
                    lows_of(4 * j + 4, 0, 4 * j, j % 2)
                lows_of(22, 0, 20, 1, 2)
                lows_of(24, 2, 0, 1, 2)
                lows_of(28, 0, 2, 0)
                ve.wait_ge(mm_done, 4 * (n1 + 5) + 2)
                for t in range(NT):
                    part = x[:, t, 0:512]
                    ve.tensor_tensor(part, part, ps[:, t, :], ALU.add)
                lows_of(32, 0, 6, 1)
                for j in range(8, 11):
                    lows_of(4 * j + 4, 0, 4 * j - FT, j % 2)

            ve.memset(ones[:, :], 1.0).then_inc(ones_ready, 1)
            tile_variance(0, 0)
            rsqrt(0, 1)
            ve.wait_ge(gain_loaded, 16)
            scale_x(0, 0, xn)
            tile_lows(0)
            tile_variance(0, 1)
            rsqrt(1, 2)
            scale_x(0, 1, xn)
            tile_variance(0, 2)
            tile_lows(1)
            rsqrt(2, 3)
            scale_x(0, 2, xn)
            tile_variance(0, 3)
            copy_whole(0)
            rsqrt(3, 4)
            scale_x(0, 3, xn)
            tile_lows(2)
            tile_lows(3)
            turns[0] += 1
            copy_whole(1)
            ve.wait_ge(ident_loaded, 16)
            own.mark(ve.tensor_copy(ident_bf[:, :], ident))
            ve.wait_ge(cst_loaded, 16)
            ve.wait_ge(mask_loaded, 16)
            ve.tensor_copy(mask_bf[:, :], masks_f32).then_inc(masks_ready, 1)
            def rope(t):
                copy_whole(t)
                ve.wait_ge(turned, 8)
                ve.wait_ge(part_copied, 2 * t + 2)
                src = y[:, t, 0:256].rearrange("p (m d) -> p m d", m=4)
                t1, t2 = (xn[:, t - 2, 256 * j:256 * j + 256].rearrange("p (m d) -> p m d", m=4) for j in range(2))
                cos, sin = (tab[:, t, :].unsqueeze(1).broadcast_to([128, 4, 64]) for tab in (cos64, sin64))
                own.mark(ve.tensor_tensor(t1, src, cos, ALU.mult))
                own.mark(ve.tensor_tensor(t2[:, :, 0:32], src[:, :, 32:64], sin[:, :, 0:32], ALU.mult))
                own.link(ve.tensor_tensor(t2[:, :, 32:64], src[:, :, 0:32], sin[:, :, 32:64], ALU.mult))
                ve.tensor_tensor(stage[:, t, :].rearrange("p (m d) -> p m d", m=4), t1, t2, ALU.add).then_inc(rope_ready, 1)

            rope(2)
            rope(3)
            ve.wait_ge(vec_loaded, 16)
            for j in range(2):
                a = V_LAM + 128 * j
                own.link(ve.tensor_tensor(o_tmp[:, 64 * j:64 * j + 64], vec[:, a:a + 64], vec[:, a + 64:a + 128], ALU.mult))
            ve.tensor_reduce(lam_s[:, 0:2], o_tmp[:, :].rearrange("p (a n) -> p a n", a=2), AX.X, ALU.add)\
              .then_inc(lam_dots, 1)
            own.mark(ve.tensor_scalar(sub_gain[:, :], vec[:, V_SUB:V_SUB + 128], 1.0 - LAM_INIT, None, ALU.mult))
            copy_k(0)
            ve.wait_ge(lam_exps, 1)
            own.link(ve.tensor_tensor(neg_lam[:, :], lam_s[:, 3:4], lam_s[:, 2:3], ALU.subtract))
            own.link(ve.tensor_scalar(neg_lam[:, :], neg_lam[:, :], -LAM_INIT, None, ALU.add))
            ve.wait_ge(masks_ready, 1)
            with ve.Fori(0, 4) as g:
                end = own.loop(g, 4, 16)
                attention("A", g, g, ahead=True)
                end()
            variance(0, 16, 1.0 / 128)
            refine(0, 16)

            def sub_norm(t):
                for h in range(4):
                    o = y[:, ds(t, 1), 384 * h:384 * h + 128]
                    ins = ve.scalar_tensor_tensor(o, o, rstd[:, ds(4 * t + h, 1)], sub_gain[:, :].unsqueeze(1),
                                                  ALU.mult, ALU.mult)
                ins.then_inc(src_ready, 1)

            sub_norm(0)
            with ve.Fori(4, 7) as g:
                end = own.loop(g - 4, 3, 4)
                attention("B", g - 4, g, ahead=True, between=lambda: sub_norm(g - 3))
                end()
            attention("B", 3, 7)
            late_half(0)
            norm(1, W_OUT0 + 2)
            mlp(0, W_UP0)
            norm(2, W_DQK - 2)
            with ve.Fori(0, 2) as i:
                for c in range(4):
                    ve.wait_ge(mm_done, 8 * i + 4 * (W_DQK + c // 2) + 2 * (c % 2) + 2)
                    ve.tensor_copy(dT[:, ds(4 * i + c, 1), :], ps[:, ds(4 * i + c, 1), :]).then_inc(dT_copied, 1)
            for t in range(NT):
                ve.wait_ge(mm_done, 4 * (W_DV + 1) + t + 1)
                ve.tensor_copy(dv[:, t, :], ps[:, t, :]).then_inc(dv_copied, 1)
            def copy_latent(what):
                j, t, a, b = c_fill(what)
                ve.wait_ge(mm_done, 4 * W_C + (j + 1 if j < 4 else 2 * j - 2))
                ve.tensor_copy(c_tok[:, t, a:b], ps[:, 4 + j % 2, 0:b - a]).then_inc(c_copied, 1)

            for n in range(20):
                if n < 16:
                    p, i, m, w = d_unit(n)
                    ve.wait_ge(d_soft, n + 1)
                    sp_ = d_sums[:, m, 0:w]
                    ve.scalar_tensor_tensor(sp_, ps[:, m, 0:w], 0.0, tmp[:, m, 0:w], ALU.max, ALU.add).then_inc(d_sp, 1)
                    ve.wait_ge(d_sp, n + 1)
                    own.link(ve.tensor_tensor_scan(sp_[:, ::-1], sp_[:, ::-1], sp_[:, ::-1], 0.0, ALU.add, ALU.max))
                    if n >= 2:
                        ve.wait_ge(d_turned, n - 1)
                    ve.tensor_tensor(probs[:, m, 0:w], ps[:, m, 0:w], sp_, ALU.subtract).then_inc(d_arg, 1)
                for what in latent_done(n):
                    copy_latent(what)
                if n == 10:
                    ve.wait_ge(c_squared, 8)
                    variance(0, 4, 1.0 / 384, last=False)
                    variance(4, 8, 1.0 / 256)
                if n == 11:
                    refine(0, 8)
                for t in D_UQ.get(n, ()):
                    ve.wait_ge(mm_done, 4 * W_UQ + t + 1)
                    ve.tensor_scalar(q_tok[:, t, :], ps[:, 4 + t % 2, 0:384], rstd[:, t:t + 1], None, ALU.mult)\
                      .then_inc(q_scaled, 1)
                if n in D_UKV:
                    t = D_UKV[n]
                    ve.wait_ge(mm_done, 4 * W_UKV + t + 1)
                    kv = ps[:, 4:6, 0:384].rearrange("p c (h d) -> p c h d", h=2)
                    ve.tensor_scalar(k_tok[:, t, :].rearrange("p (c h d) -> p c h d", c=2, h=2)[:, :, :, 0:64],
                                     kv[:, :, :, 0:64], rstd[:, 4 + t:5 + t], None, ALU.mult)
                    ve.tensor_scalar(v_tok[:, t, :].rearrange("p (c h d) -> p c h d", c=2, h=2),
                                     kv[:, :, :, 64:192], rstd[:, 4 + t:5 + t], None, ALU.mult).then_inc(kv_scaled, 1)
                if 2 <= n < 18:
                    p, i, m, w = d_unit(n - 2)
                    ve.wait_ge(d_turned, n - 1)
                    if n >= 4:
                        ve.wait_ge(d_pv, n - 3)
                    ve.tensor_copy(probsT[:, m, 0:w], ps[:, 2 + m, 0:w]).then_inc(d_copied, 1)
                if n >= 5 and n % 2:
                    p, i, m, w = d_unit(n - 5)
                    ve.wait_ge(d_pv, n - 3)
                    ve.tensor_copy(o_D[:, i, 256 * p:256 * p + 256], ps[:, 6 + (n - 5) // 2 % 2, 0:256]).then_inc(d_out, 1)
                for c in D_TURN.get(n, ()):
                    ve.wait_ge(c_hi, c + 1)
                    ve.scalar_tensor_tensor(hT_lo[:, c, :], ps[:, 4 + c % 2, :], vec[:, V_CG + c:V_CG + c + 1],
                                            hT_hi[:, c, :].bitcast(f32), ALU.mult, ALU.subtract).then_inc(c_lo, 1)
            for g in (8, 9):
                attention("C", g - 8, g)
            late_half(1)
            norm(3, W_OUT1 + 2)
            mlp(1, W_UP1)
            for t in range(NT):
                add_to_x(W_ALL - 2, t)
                tile_variance(4, t)
                rsqrt(t, t + 1)
                if t == 0:
                    ve.wait_ge(gain_loaded, 16 * 5)
                scale_x(4, t, final)

        @block.tensor
        def _(pe):
            PASSES = ((hT_hi, w_hi), (hT_hi, w_lo), (hT_lo, w_hi))
            turns = [0]

            def turn_tile(t, source, ready):
                for j in range(KT):
                    if j % 4 == 0:
                        ready(t, j // 4)
                    ins = pe.transpose(ps[:, 2 * t + j // 4, 128 * (j % 4):128 * (j % 4) + 128], source(t, j), ident)
                    if j % 4 == 3:
                        ins.then_inc(turned, 1)

            def turn(source, ready):
                for t in range(NT):
                    turn_tile(t, source, ready)
                turns[0] += 1

            norms = [0]

            def turn_xn(t):
                turn_tile(t, lambda t, j: xn[:, t % 2, j * 128:(j + 1) * 128],
                          lambda t, g: pe.wait_ge(src_ready, src_base() + t + 1) if g == 0 else None)

            def src_base():
                return 4 * norms[0] + (4 if norms[0] else 0)

            def last_two(n, a_part, b_part, b_ready=None, a_bank=4, a_ready=None):
                for step in ("A0", "A1", "A2", "B0", "B1", "A3", "x0", "B2", "x1", "B3"):
                    t = int(step[1])
                    if step[0] == "x":
                        if not final_norm():
                            turn_xn(t)
                        continue
                    k0, first = a_part if step[0] == "A" else b_part
                    if a_ready and step[0] == "A":
                        a_ready(t)
                    slot = (n + (step[0] == "B")) % 2
                    if step in ("A0", "B0"):
                        pe.wait_ge(w_lo_ready, n + 1 + (step == "B0"))
                        if step == "B0" and b_ready:
                            b_ready()
                    for k in range(4):
                        for m, (h, w) in enumerate(PASSES):
                            bank = t + (4 if step[0] == "B" else a_bank)
                            ins = pe.matmul(ps[:, bank, :], h[:, k0 + k, t * 128:(t + 1) * 128],
                                            w[:, slot, k * 512:(k + 1) * 512], start=first and k == 0 and m == 0,
                                            stop=(step[0] == "B" or a_bank == 0) and k == 3 and m == 2)
                    ins.then_inc(mm_done, 1)

            def final_norm():
                return norms[0] == 4

            def first_tile(slot):
                for half, s in ((0, 0), (0, 1), (1, 0), (1, 1)):
                    pe.wait_ge(turn_lo, 8 * turns[0] + 4 * half + 4)
                    for k in range(KT):
                        for m, (h, w) in enumerate(PASSES):
                            ins = pe.matmul(ps[:, s, 256 * half:256 * half + 256],
                                            w[:, slot, k * 256 + 128 * s:k * 256 + 128 * s + 128],
                                            h[:, k, 256 * half:256 * half + 256],
                                            start=k == 0 and m == 0, stop=k == KT - 1 and m == 2)
                    if half:
                        ins.then_inc(mm_done, 2)
                    elif s == 0:
                        turn_xn(2)
                        turn_xn(3)
                turns[0] += 1
                norms[0] += 1

            def tokens_tile(slot, first, last, k0, nk, width, banks, before=None, offset=0, inc=1):
                for t in range(NT):
                    if before:
                        before(t)
                    for k in range(nk):
                        for n, (h, w) in enumerate(PASSES):
                            ins = pe.matmul(ps[:, banks[t], 0:width], h[:, k0 + k, t * 128:(t + 1) * 128],
                                            w[:, slot, k * width:(k + 1) * width],
                                            start=first and k == 0 and n == 0,
                                            stop=last and k == nk - 1 and n == 2)
                    ins.then_inc(mm_done, inc)

            def channels(slot, s, bank, pitch=256):
                for k in range(KT):
                    for n, (h, w) in enumerate(PASSES):
                        ins = pe.matmul(bank, w[:, slot, k * pitch + 128 * s:k * pitch + 128 * s + 128], h[:, k:k + 1, :],
                                        start=k == 0 and n == 0, stop=k == KT - 1 and n == 2)
                ins.then_inc(mm_done, 2)

            def tok_ready(t):
                pe.wait_ge(turn_lo, 8 * (turns[0] - 1) + 2 * t + 2)

            def half_source(l, early):
                if l == 0:
                    j0 = 0 if early else 4
                    return lambda t, j: y[:, t, 384 * (j0 + j):384 * (j0 + j) + 128]
                o = o_D if early else o_C
                return lambda t, j: o[:, t, j * 128:(j + 1) * 128]

            def turn_half(source, t, bank):
                for j in range(4):
                    ins = pe.transpose(ps[:, bank, 128 * j:128 * j + 128], source(t, j), ident)
                ins.then_inc(half_turned, 1)

            def early_turn(l, t):
                if l == 0:
                    pe.wait_ge(src_ready, 4 + t + 1)
                if t >= 2:
                    pe.wait_ge(half_lo, 8 * l + t - 1)
                turn_half(half_source(l, True), t, 4 + t % 2)

            def early_product(l, n0, place, f):
                c, t = f // 4, f % 4
                if t == 0:
                    pe.wait_ge(w_lo_ready, n0 + c + 1)
                    pe.wait_ge(half_lo, 8 * l + 4)
                if f >= 2:
                    pe.wait_ge(early_added, 8 * l + f - 1)
                for k in range(4):
                    for m, (h_, w_) in enumerate(PASSES):
                        ins = pe.matmul(ps[:, 4 + f % 2, :], h_[:, place + k, t * 128:(t + 1) * 128],
                                        w_[:, (n0 + c) % 2, k * 512:(k + 1) * 512], start=k == 0 and m == 0,
                                        stop=k == 3 and m == 2)
                ins.then_inc(mm_done, 1)

            def project_late(l):
                n0, place, last_group = (W_OUT1, 0, 9) if l else (W_OUT0, 4, 7)
                for t in range(NT):
                    if t == 3:
                        early_product(l, n0, 0 if l == 0 else 4, 7)
                    pe.wait_ge(o_ready, 4 * last_group + t + 1)
                    turn_half(half_source(l, False), t, t)
                pe.wait_ge(early_added, 8 * l + 8)
                last_two(n0 + 2, (place, True), (place, True), a_bank=0,
                         a_ready=lambda t: pe.wait_ge(half_lo, 8 * l + 5 + t))

            def turn_qk(g, at_once=False):
                pe.wait_ge(part_copied, 8 * g + 8)
                for t in range(NT):
                    pe.wait_ge(rope_ready, 4 * g + (4 if at_once else t + 1))
                    for s in range(2):
                        ins = pe.transpose(ps[:, 4 + s, t * 128:(t + 1) * 128], stage[:, t, s * 128:(s + 1) * 128], ident)
                        if t == NT - 1:
                            ins.then_inc(qk_turned, 1)

            def part(g, u, bank):
                half, t = u // 4, u % 4
                if t == 0:
                    pe.wait_ge(w_lo_ready, 2 * g + (half + 1))
                for k in range(4):
                    for n, (h_, w_) in enumerate(PASSES):
                        ins = pe.matmul(ps[:, bank, 0:384], h_[:, 4 * half + k, t * 128:(t + 1) * 128],
                                        w_[:, half, k * 384:(k + 1) * 384], start=k == 0 and n == 0, stop=k == 3 and n == 2)
                ins.then_inc(mm_done, 1)

            def attention(kind, h, g, ahead=False):
                g_static = None if ahead else g
                l, n0, early = (None, None, None) if ahead else layer_of(g)
                if kind == "C":
                    if g == 9:
                        pe.wait_ge(early_added, 8 + 4)
                    for s in range(2):
                        if s == 1 and g > 8:
                            pe.wait_ge(o_ready, 4 * g)
                        for src, bank in ((q_tok, 4 + 2 * s), (k_tok, 5 + 2 * s)):
                            for t in range(NT):
                                ins = pe.transpose(ps[0:96, bank, t * 128:(t + 1) * 128],
                                                   src[:, t, (2 * h + s) * 96:(2 * h + s + 1) * 96], ident)
                            ins.then_inc(qk_turned, 1)
                for k in range(10):
                    fill = FILL.get(k, ()) if ahead else ()
                    if k < 8:
                        i, m, w = unit(k)
                        if kind == "C":
                            pe.wait_ge(qT_ready, 8 + 2 * (g - 8) + m + 1)
                            pe.wait_ge(kT_ready, 8 + 2 * (g - 8) + m + 1)
                            q, kk = qk[0:96, m, i * 128:(i + 1) * 128], qk[0:96, 2 + m, 0:w]
                        else:
                            if k == 0:
                                pe.wait_ge(qT_ready, g + 1)
                                pe.wait_ge(kT_ready, g + 1)
                            q, kk = qk[64 * m:64 * m + 64, 0, i * 128:(i + 1) * 128], qk[64 * m:64 * m + 64, 2, 0:w]
                        if k >= 2:
                            pe.wait_ge(exp_ready, 8 * g + k - 1)
                        pe.matmul(ps[:, m, 0:w], q, kk, start=True, stop=False)
                        if kind == "B":
                            ins = pe.matmul(ps[:, m, 0:w], ident_bf[:, :], mask_bf[:, M_END - w:M_END], start=False, stop=True)
                        else:
                            ins = pe.matmul(ps[:, m, w - 128:w], ident_bf[:, :], mask_bf[:, M_CAUSAL:M_CAUSAL + 128],
                                            start=False, stop=True)
                        ins.then_inc(scores_ready, 1)
                    for t in EARLY_TURN.get(g_static, {}).get(k, ()):
                        early_turn(l, t)
                    f = EARLY_FILL.get(g_static, {}).get(k)
                    if f is not None:
                        early_product(l, n0, early, f)
                    if ahead and k == 9:
                        turn_qk(g + 1)
                    for u in fill[:1]:
                        if u >= 2:
                            pe.wait_ge(part_copied, 8 * g + (7 + u))
                        part(g + 1, u, 4 + u % 2)
                    if 1 <= k <= 8:
                        i, m, w = unit(k - 1)
                        if kind == "B":
                            pe.wait_ge(mult_ready, 8 * (g - 4) + k)
                        else:
                            pe.wait_ge(exp_ready, 8 * g + k)
                        if k >= 3:
                            pe.wait_ge(pT_copied, 8 * g + k - 2)
                        for b in range(i + 1):
                            ins = pe.transpose(ps[:, 2 + m, b * 128:(b + 1) * 128], probs[:, m, b * 128:(b + 1) * 128], ident)
                        ins.then_inc(pT_ready, 1)
                    for u in fill[1:]:
                        if u >= 2:
                            pe.wait_ge(part_copied, 8 * g + (7 + u))
                        part(g + 1, u, 4 + u % 2)
                    if k >= 2:
                        i, m, w = unit(k - 2)
                        pe.wait_ge(pT_copied, 8 * g + k - 1)
                        if i >= 2 and m == 0:
                            pe.wait_ge(o_ready, 4 * g + i - 1)
                        for b in range(i + 1):
                            if kind == "A":
                                v, o = y[:, b, ds(384 * g + 256, 128)], ps[:, 6 + i % 2, 128 * m:128 * m + 128]
                            elif kind == "B":
                                v, o = y[:, b, ds(384 * g + (256 + 64 * m), 64)], ps[:, 6 + i % 2, 64 * m:64 * m + 64]
                            else:
                                v, o = v_tok[:, b, (2 * h + m) * 128:(2 * h + m) * 128 + 128], ps[:, 6 + i % 2, 128 * m:128 * m + 128]
                            ins = pe.matmul(o, probsT[:, m, b * 128:(b + 1) * 128], v, start=b == 0, stop=b == i)
                        ins.then_inc(pv_ready, 1)

            def mlp(l, n0):
                def pair(i, first=False):
                    for half in range(2):
                        pe.wait_ge(w_lo_ready, 2 * i + (n0 + half + 1))
                        if first and half == 0:
                            first_tile(n0 % 2)
                            continue
                        for s in range(2):
                            if half:
                                pe.wait_ge(val_bank_free[l], 2 * i + s + 1)
                            channels(half, s, ps[:, 2 * half + s:2 * half + s + 1, :])
                    pe.wait_ge(conv_done[l], 2 * i + 2)

                pair(0, first=True)
                with pe.Fori(1, FT // 2) as i:
                    pair(i)
                n1 = n0 + FT

                def down_tile(slot, parts, last, wait_w, wait_lo, beside=False):
                    pe.wait_ge(w_lo_ready, wait_w)
                    pe.wait_ge(act_lo[l], wait_lo)
                    for c, units, first, stop, incs in parts:
                        for t in range(NT):
                            if beside and t == 2:
                                pe.wait_ge(val_bank_free[l], 2 + FT)
                            for u in units:
                                for n, (h, w) in enumerate(PASSES):
                                    if beside:
                                        a = first_lo[:, u, :] if n == 2 else first_hi[:, u, :]
                                    else:
                                        a = h[:, 4 * slot + u, :]
                                    ins = pe.matmul(ps[:, 4 * c + t, :], a[:, t * 128:(t + 1) * 128],
                                                    w[:, slot, u * 512:(u + 1) * 512],
                                                    start=first and u == units[0] and n == 0,
                                                    stop=stop and u == units[-1] and n == 2)
                            if incs[t]:
                                ins.then_inc(mm_done, incs[t])

                every, four = (1, 1, 1, 1), (0, 1, 2, 3)
                down_tile(0, [(0, four, True, False, every)], False, n1 + 1, 4, beside=True)
                with pe.Fori(0, 2) as i:
                    for b in range(2):
                        down_tile(1 - b, [(0, four, False, False, every)], False,
                                  2 * i + (n1 + b + 2), 8 * i + 4 * (b + 2))
                down_tile(1, [(0, (0, 1), False, True, (0, 0, 0, 2)), (1, (2, 3), True, False, (0, 0, 0, 2))],
                          False, n1 + 6, 24)
                for j in (6, 7, 8):
                    down_tile(j % 2, [(1, four, False, False, every)], False, n1 + j + 1, 4 * (j + 1))
                pe.wait_ge(act_lo[l], 40)
                last_two(n1 + 9, (4, False), (0, False), lambda: pe.wait_ge(act_lo[l], 44))

            pe.wait_ge(ident_loaded, 16)
            def group_0(t, half, inc):
                if half == 0:
                    pe.wait_ge(turn_lo, 2 * t + 2)
                if t == 0:
                    pe.wait_ge(w_lo_ready, half + 1)
                for k in range(4):
                    for n, (h_, w_) in enumerate(PASSES):
                        ins = pe.matmul(ps[:, 2 * t, 0:384], h_[:, 4 * half + k, t * 128:(t + 1) * 128],
                                        w_[:, half, k * 384:(k + 1) * 384],
                                        start=half == 0 and k == 0 and n == 0, stop=half == 1 and k == 3 and n == 2)
                if inc:
                    ins.then_inc(mm_done, inc)

            turn_xn(0)
            group_0(0, 0, 0)
            turn_xn(1)
            group_0(0, 1, 2)
            group_0(1, 0, 0)
            turn_xn(2)
            group_0(1, 1, 2)
            turn_xn(3)
            group_0(2, 0, 0)
            group_0(3, 0, 1)
            group_0(2, 1, 1)
            group_0(3, 1, 2)
            turns[0] += 1
            norms[0] += 1
            turn_qk(0, at_once=True)
            pe.wait_ge(masks_ready, 1)
            with pe.Fori(0, 4) as g:
                attention("A", g, g, ahead=True)
            with pe.Fori(4, 7) as g:
                attention("B", g - 4, g, ahead=True)
            attention("B", 3, 7)

            project_late(0)
            mlp(0, W_UP0)
            for n in range(4):
                pe.wait_ge(w_lo_ready, W_DQK + n + 1)
                if n == 0:
                    first_tile(W_DQK % 2)
                    continue
                for s in range(2):
                    channels((W_DQK + n) % 2, s, ps[:, 2 * n + s:2 * n + s + 1, :])
            for half in range(2):
                pe.wait_ge(w_lo_ready, W_DV + half + 1)
                pe.wait_ge(dT_copied, 4)
                tokens_tile((W_DV + half) % 2, half == 0, half == 1, 4 * half, 4, 512, range(NT))

            def latent(what, parts):
                j, t, a, b = c_fill(what)
                width, n = b - a, W_C + (j >= 4)
                cut = 5 if j < 4 else 3
                for part in parts:
                    if t == 0:
                        pe.wait_ge(w_lo_ready, n + part + 1)
                    if part == 0 and j >= 2:
                        pe.wait_ge(c_copied, j - 1)
                    if part == 0 and j < 2:
                        pe.wait_ge(dT_copied, 5 + j)
                    for k in ((range(cut), range(cut, KT))[part]):
                        col = width * (k - cut * part) + (3 * 384 if j >= 4 and part == 0 else 0)
                        for m, (h, w) in enumerate(PASSES):
                            ins = pe.matmul(ps[:, 4 + j % 2, 0:width], h[:, k, t * 128:(t + 1) * 128],
                                            w[:, (n + part) % 2, col:col + width],
                                            start=k == 0 and m == 0, stop=k == KT - 1 and m == 2)
                if 1 in parts:
                    ins.then_inc(mm_done, 1 if j < 4 else 2)

            def turn_latent(c):
                pe.wait_ge(c_copied, 8)
                if c >= 2:
                    pe.wait_ge(c_lo, c - 1)
                for t in range(NT):
                    ins = pe.transpose(ps[:, 4 + c % 2, t * 128:(t + 1) * 128], c_tok[:, t, c * 128:(c + 1) * 128], ident)
                ins.then_inc(c_turned, 1)

            def up_q(t):
                if t == 0:
                    pe.wait_ge(w_lo_ready, W_UQ + 1)
                    pe.wait_ge(c_lo, 5)
                if t >= 2:
                    pe.wait_ge(q_scaled, t - 1)
                for k in range(3):
                    for m, (h, w) in enumerate(PASSES):
                        ins = pe.matmul(ps[:, 4 + t % 2, 0:384], h[:, k, t * 128:(t + 1) * 128],
                                        w[:, W_UQ % 2, k * 384:k * 384 + 384],
                                        start=k == 0 and m == 0, stop=k == 2 and m == 2)
                ins.then_inc(mm_done, 1)

            def up_kv(t):
                if t == 0:
                    pe.wait_ge(w_lo_ready, W_UKV + 1)
                    pe.wait_ge(q_scaled, NT)
                else:
                    pe.wait_ge(kv_scaled, t)
                for c in range(2):
                    for k in range(2):
                        for m, (h, w) in enumerate(PASSES):
                            ins = pe.matmul(ps[:, 4 + c, 0:384], h[:, 3 + k, t * 128:(t + 1) * 128],
                                            w[:, W_UKV % 2, k * 768 + 384 * c:k * 768 + 384 * c + 384],
                                            start=k == 0 and m == 0, stop=k == 1 and m == 2)
                ins.then_inc(mm_done, 1)

            for n in range(19):
                if n < 4:
                    pe.wait_ge(dv_copied, n + 1)
                if n < 16:
                    p, i, m, w = d_unit(n)
                    if n % 8 < 2:
                        pe.wait_ge(d_q, 2 * p + m + 1)
                    if n >= 2:
                        pe.wait_ge(d_arg, n - 1)
                    pe.matmul(ps[:, m, 0:w], qk[:, 2 * p + m, i * 128:(i + 1) * 128], dT[:, 2 * p + (4 + m), 0:w],
                              start=True, stop=False)
                    pe.matmul(ps[:, m, w - 128:w], ident_bf[:, :], mask_bf[:, M_STRICT:M_STRICT + 128],
                              start=False, stop=True).then_inc(d_scores, 1)
                for kind, t, parts in D_FILL.get(n, ()):
                    latent((kind, t), parts)
                for t in D_UQ.get(n, ()):
                    up_q(t)
                if n in D_UKV:
                    up_kv(D_UKV[n])
                if 2 <= n < 18:
                    p, i, m, w = d_unit(n - 2)
                    pe.wait_ge(d_exp, n - 1)
                    if n >= 4:
                        pe.wait_ge(d_copied, n - 3)
                    for b in range(i + 1):
                        ins = pe.transpose(ps[:, 2 + m, b * 128:(b + 1) * 128], probs[:, m, b * 128:(b + 1) * 128], ident)
                    ins.then_inc(d_turned, 1)
                if n >= 3:
                    p, i, m, w = d_unit(n - 3)
                    pe.wait_ge(d_copied, n - 2)
                    if m == 0 and n >= 7:
                        pe.wait_ge(d_out, (n - 5) // 2)
                    for b in range(i + 1):
                        ins = pe.matmul(ps[:, 6 + (n - 3) // 2 % 2, 128 * m:128 * m + 128], probsT[:, m, b * 128:(b + 1) * 128],
                                        dv[:, b, 256 * p + 128 * m:256 * p + 128 * m + 128], start=b == 0, stop=b == i)
                    ins.then_inc(d_pv, 1)
                for c in D_TURN.get(n, ()):
                    turn_latent(c)
            pe.wait_ge(c_roped, 2)
            pe.wait_ge(kv_scaled, NT)
            pe.wait_ge(d_out, 8)
            for g in (8, 9):
                attention("C", g - 8, g)
            project_late(1)
            mlp(1, W_UP1)


def _constants():
    import numpy as np
    p = np.arange(128)
    consts = np.zeros((128, C_END), np.float32)
    consts[:, C_ID:C_ID + 128] = np.eye(128)
    masks = np.zeros((128, M_END), np.float32)
    q, k = p[:, None], p[None, :]
    masks[:, M_CAUSAL:M_CAUSAL + 128] = np.where(k <= q, 0.0, -1e30)
    masks[:, M_STRICT:M_STRICT + 128] = np.where(k < q, 0.0, -1e30)
    for s in range(4):
        d = q - k + 128 * (3 - s)
        seen = ((d >= 0) & (d <= 128)).astype(np.float32) + ((d >= 0) & (d % 4 == 0)) + ((d >= 0) & (d % 16 == 0))
        consts[:, C_CMUL + 128 * s:C_CMUL + 128 * s + 128] = seen
        masks[:, M_DIL + 128 * s:M_DIL + 128 * s + 128] = np.where(seen > 0, 0.0, -1e30)
    for dim, c0, s0 in ((64, C_COS64, C_SIN64), (32, C_COS32, C_SIN32)):
        inv = (np.float32(10000.0) ** (-np.arange(0, dim, 2, dtype=np.float32) / np.float32(dim))).astype(np.float32)
        ang = np.arange(SEQ, dtype=np.float32)[:, None] * inv[None, :]
        cos, sin = np.cos(ang).astype(np.float32), np.sin(ang).astype(np.float32)
        for base, tab in ((c0, np.concatenate([cos, cos], 1)), (s0, np.concatenate([-sin, sin], 1))):
            consts[:, base:base + NT * dim] = tab.reshape(NT, 128, dim).transpose(1, 0, 2).reshape(128, -1)
    return consts, masks


def _weight_tiles(ab_w_in, ab_w_out, cd_w_in, c_w_uq, c_w_ukv, cd_w_out, ffn_w_up, ffn_w_down):
    import numpy as np

    def tiles(a):
        a = a.transpose(1, 0, 2).reshape(128, -1)
        out = np.zeros((1, 128, UNIT), np.float32)
        out[0, :, :a.shape[1]] = a
        return out

    def join(a, b):
        out = tiles(a)
        na, nb = a.shape[0] * a.shape[2], b.shape[0] * b.shape[2]
        out[0, :, na:na + nb] = tiles(b)[0, :, :nb]
        return out

    def tokens(w):
        w = w.reshape(KT, 128, -1)
        return [tiles(w[4 * h:4 * h + 4, :, c:c + 512]) for c in range(0, w.shape[2], 512) for h in range(2)]

    def output(w, early):
        w = w.reshape(2, 4, 128, 2, 512)
        return [tiles(w[h, :, :, c, :]) for h in (early, 1 - early) for c in range(2)]

    def channels(w, width=256):
        w = w.reshape(KT, 128, -1)
        return [tiles(w[:, :, c:c + width]) for c in range(0, w.shape[2], width)]

    def mlp(l):
        gate, val = channels(ffn_w_up[l][:, :DFF]), channels(ffn_w_up[l][:, DFF:])
        up = [t for pair in zip(gate, val) for t in pair]
        units = [ffn_w_down[l].reshape(FT, 128, DM)[k, :, 512 * c:512 * c + 512] for c in range(2) for k in range(FT)]
        return up + [tiles(np.stack(units[u:u + 4])) for u in range(0, 2 * FT, 4)]

    cd = cd_w_in[0]
    qkv = ab_w_in[0].reshape(KT, 128, 2, 3, 4, 128).transpose(2, 4, 0, 1, 3, 5).reshape(8, 2, 4, 128, 384)
    all_tiles = [tiles(qkv[g, h]) for g in range(8) for h in range(2)] + output(ab_w_out[0], 0) + mlp(0)
    all_tiles += channels(cd[:, 672:1696]) + tokens(cd[:, 1696:2208])
    latent_q, latent_kv = (cd[:, a:b].reshape(KT, 128, b - a) for a, b in ((0, 384), (384, 672)))
    all_tiles += [tiles(latent_q[0:5]), join(latent_q[5:], latent_kv[0:3]), tiles(latent_kv[3:])]
    all_tiles += [tiles(c_w_uq[0].reshape(3, 128, 384)), tiles(c_w_ukv[0].reshape(2, 128, 768))]
    all_tiles += output(cd_w_out[0], 1) + mlp(1)
    out = np.concatenate(all_tiles)
    assert out.shape == (W_ALL, 128, UNIT)
    return out


def kernel(x, mix_norm_g, ffn_norm_g, final_norm_g, ab_w_in, a_lambda_q1, a_lambda_k1, a_lambda_q2, a_lambda_k2,
           a_subln_g, ab_w_out, cd_w_in, c_q_norm_g, c_w_uq, c_kv_norm_g, c_w_ukv, cd_w_out, ffn_w_up, ffn_conv_w,
           ffn_conv_b, ffn_w_down):
    import numpy as np
    import concourse.bacc as bacc
    from concourse.bass_utils import run_bass_kernel_spmd

    consts, masks = _constants()
    a = np.asarray
    conv = np.concatenate([a(ffn_conv_w), a(ffn_conv_b)[:, None, :]], 1)
    conv = conv.reshape(2, 4, FT, 128).transpose(3, 0, 2, 1).reshape(128, -1)
    rows = np.concatenate([a(a_lambda_q1)[0], a(a_lambda_k1)[0], a(a_lambda_q2)[0], a(a_lambda_k2)[0], a(a_subln_g)[0]])
    latent = np.concatenate([a(c_q_norm_g)[0], a(c_kv_norm_g)[0]]).reshape(5, 128).T
    vectors = np.concatenate([np.broadcast_to(rows, (128, 384)), conv, latent], 1)
    gains = np.stack([a(mix_norm_g)[0], a(ffn_norm_g)[0], a(mix_norm_g)[1], a(ffn_norm_g)[1], a(final_norm_g)])
    arrays = {
        "x_in": a(x),
        "weights": _weight_tiles(*(a(w) for w in (ab_w_in, ab_w_out, cd_w_in, c_w_uq, c_w_ukv, cd_w_out,
                                                   ffn_w_up, ffn_w_down))),
        "consts": consts, "masks": masks, "vectors": vectors,
        "gains": np.broadcast_to(gains, (128, 5, DM)),
    }
    arrays = {name: np.ascontiguousarray(v) for name, v in arrays.items()}
    nc = bacc.Bacc("TRN2", target_bir_lowering=False, num_devices=1)
    args = [nc.dram_tensor(name, v.shape, mybir.dt.from_np(v.dtype), kind="ExternalInput").ap()
            for name, v in arrays.items()]
    out = nc.dram_tensor("out", (1, SEQ, DM), mybir.dt.float32, kind="ExternalOutput").ap()
    trunk_program(nc, *args, out)
    r = run_bass_kernel_spmd(nc, [arrays], core_ids=[0])
    return r.results[0]["out"]
```
